# Optimizing a Trainium2 kernel written in Bass

```python
import math
import jax, jax.numpy as jnp
from jax import lax
import numpy as np

D_MODEL = 2048
BATCH = 1
SEQ = 256
DEPTH = 2

N_A_LAYERS = DEPTH // 2
N_B_LAYERS = DEPTH - N_A_LAYERS

RWKV_HEAD = 64
RWKV_HEADS = D_MODEL // RWKV_HEAD
D_DECAY_LORA = max(32, int(round(1.8 * D_MODEL ** 0.5 / 32)) * 32)
D_AAA_LORA = max(32, int(round(1.8 * D_MODEL ** 0.5 / 32)) * 32)
D_GATE_LORA = max(32, int(round(0.6 * D_MODEL ** 0.8 / 32)) * 32)
GN_EPS = 64e-5

MOBA_HEAD_DIM = 128
MOBA_HEADS = D_MODEL // MOBA_HEAD_DIM
MOBA_BLOCK = 256
MOBA_TOPK = 3
MOBA_Q_CHUNK = 32
NEG = -1e30

D_FF = ((8 * D_MODEL // 3 + 255) // 256) * 256

ALPHA = (2 * DEPTH) ** 0.25
BETA = (8 * DEPTH) ** -0.25
LN_EPS = 1e-5

kernel_name = "yoco_rwkv7_moba_deepnorm"

def _layernorm(x, w, b):
    xf = x.astype(jnp.float32)
    mu = jnp.mean(xf, axis=-1, keepdims=True)
    var = jnp.mean(jnp.square(xf - mu), axis=-1, keepdims=True)
    y = (xf - mu) * lax.rsqrt(var + LN_EPS)
    return (y * w + b).astype(x.dtype)

def _swiglu(x, w_gate, w_up, w_down):
    return (jax.nn.silu(x @ w_gate) * (x @ w_up)) @ w_down

def _rwkv7_step(state, inp):
    r_t, w_t, k_t, v_t, a_t, b_t = inp
    sa = jnp.einsum('bhij,bhj->bhi', state, a_t)
    state = (state * w_t[:, :, None, :]
             + sa[..., None] * b_t[:, :, None, :]
             + v_t[..., None] * k_t[:, :, None, :])
    y = jnp.einsum('bhij,bhj->bhi', state, r_t)
    return state, y

def _rwkv7_scan(r, w, k, v, a, b):
    B, S, H, N = r.shape
    seq = tuple(jnp.moveaxis(t.astype(jnp.float32), 1, 0) for t in (r, w, k, v, a, b))
    state0 = jnp.zeros((B, H, N, N), jnp.float32)
    _, y = lax.scan(_rwkv7_step, state0, seq)
    return jnp.moveaxis(y, 0, 1)

def _rwkv7_time_mix(x, mix, w_r, w_k, w_v, w_o, w0, w1, w2, a0, a1, a2,
                    g1, g2, k_k, k_a, r_k, lnx_w, lnx_b):
    B, S, C = x.shape
    H, N = RWKV_HEADS, RWKV_HEAD
    x_prev = jnp.pad(x, ((0, 0), (1, 0), (0, 0)))[:, :-1]
    xx = x_prev - x
    xr = x + xx * mix[0]
    xw = x + xx * mix[1]
    xk = x + xx * mix[2]
    xv = x + xx * mix[3]
    xa = x + xx * mix[4]
    xg = x + xx * mix[5]
    r = xr @ w_r
    k = xk @ w_k
    v = xv @ w_v
    w_log = -jax.nn.softplus(-(w0 + jnp.tanh(xw @ w1) @ w2)) - 0.5
    decay = jnp.exp(-jnp.exp(w_log.astype(jnp.float32)))
    a = jax.nn.sigmoid(a0 + (xa @ a1) @ a2)
    g = jax.nn.sigmoid(xg @ g1) @ g2
    kk = (k * k_k).astype(jnp.float32).reshape(B, S, H, N)
    kk = kk / jnp.maximum(jnp.sqrt(jnp.sum(kk * kk, axis=-1, keepdims=True)), 1e-12)
    k = k * (1.0 + (a - 1.0) * k_a)
    rh = r.reshape(B, S, H, N).astype(jnp.float32)
    kh = k.reshape(B, S, H, N).astype(jnp.float32)
    vh = v.reshape(B, S, H, N).astype(jnp.float32)
    ah = a.reshape(B, S, H, N).astype(jnp.float32)
    y = _rwkv7_scan(rh, decay.reshape(B, S, H, N), kh, vh, -kk, kk * ah)
    mu = jnp.mean(y, axis=-1, keepdims=True)
    var = jnp.mean(jnp.square(y - mu), axis=-1, keepdims=True)
    yn = ((y - mu) * lax.rsqrt(var + GN_EPS)).reshape(B, S, C) * lnx_w + lnx_b
    bonus = (jnp.sum(rh * kh * r_k, axis=-1, keepdims=True) * vh).reshape(B, S, C)
    return ((yn + bonus).astype(x.dtype) * g) @ w_o

def _shared_kv(h, kv_w_k, kv_w_v):
    B, S, C = h.shape
    H, Dh, BLK = MOBA_HEADS, MOBA_HEAD_DIM, MOBA_BLOCK
    n_blocks = -(-S // BLK)
    pad = n_blocks * BLK - S
    k = (h @ kv_w_k).reshape(B, S, H, Dh).transpose(0, 2, 1, 3)
    v = (h @ kv_w_v).reshape(B, S, H, Dh).transpose(0, 2, 1, 3)
    k_pad = jnp.pad(k, ((0, 0), (0, 0), (0, pad), (0, 0)))
    v_pad = jnp.pad(v, ((0, 0), (0, 0), (0, pad), (0, 0)))
    k_mean = jnp.mean(k_pad.reshape(B, H, n_blocks, BLK, Dh).astype(jnp.float32),
                      axis=3).astype(h.dtype)
    return k_pad, v_pad, k_mean

def _moba_attention(x, w_q, w_o, k_pad, v_pad, k_mean):
    B, S, C = x.shape
    H, Dh, BLK, QC = MOBA_HEADS, MOBA_HEAD_DIM, MOBA_BLOCK, MOBA_Q_CHUNK
    n_blocks = k_pad.shape[2] // BLK
    top_k = max(1, min(MOBA_TOPK, n_blocks - 1))
    scale = Dh ** -0.5
    q = (x @ w_q).reshape(B, S, H, Dh).transpose(0, 2, 1, 3)
    k_blocks = k_pad.reshape(B, H, n_blocks, BLK, Dh)
    v_blocks = v_pad.reshape(B, H, n_blocks, BLK, Dh)
    b_ix = jnp.arange(B)[:, None, None, None]
    h_ix = jnp.arange(H)[None, :, None, None]

    def chunk(c):
        t0 = c * QC
        blk = t0 // BLK
        q_c = lax.dynamic_slice_in_dim(q, t0, QC, axis=2)
        gate = jnp.einsum('bhqd,bhnd->bhqn', q_c, k_mean).astype(jnp.float32)
        gate = jnp.where(jnp.arange(n_blocks) < blk, gate, NEG)
        _, sel = lax.top_k(gate, top_k)
        sel_valid = sel < blk
        k_sel = k_blocks[b_ix, h_ix, sel]
        v_sel = v_blocks[b_ix, h_ix, sel]
        s_sel = jnp.einsum('bhqd,bhqnkd->bhqnk', q_c, k_sel).astype(jnp.float32) * scale
        s_sel = jnp.where(sel_valid[..., None], s_sel, NEG).reshape(B, H, QC, top_k * BLK)
        k_own = lax.dynamic_slice_in_dim(k_pad, blk * BLK, BLK, axis=2)
        v_own = lax.dynamic_slice_in_dim(v_pad, blk * BLK, BLK, axis=2)
        s_own = jnp.einsum('bhqd,bhkd->bhqk', q_c, k_own).astype(jnp.float32) * scale
        q_pos = t0 + jnp.arange(QC)
        k_pos = blk * BLK + jnp.arange(BLK)
        s_own = jnp.where(k_pos[None, :] <= q_pos[:, None], s_own, NEG)
        p = jax.nn.softmax(jnp.concatenate([s_sel, s_own], axis=-1), axis=-1).astype(x.dtype)
        p_sel = p[..., :top_k * BLK].reshape(B, H, QC, top_k, BLK)
        p_own = p[..., top_k * BLK:]
        return (jnp.einsum('bhqnk,bhqnkd->bhqd', p_sel, v_sel)
                + jnp.einsum('bhqk,bhkd->bhqd', p_own, v_own))

    out = lax.map(chunk, jnp.arange(S // QC))
    out = out.transpose(1, 0, 3, 2, 4).reshape(B, S, H * Dh)
    return out @ w_o

def setup_inputs(seed: int = 0) -> dict:
    key = jax.random.key(seed)
    ks = iter(jax.random.split(key, 40))
    f32 = jnp.float32
    D, F, H, N = D_MODEL, D_FF, RWKV_HEADS, RWKV_HEAD
    A, Bn = N_A_LAYERS, N_B_LAYERS
    HD = MOBA_HEADS * MOBA_HEAD_DIM

    def dense(shape, fan_in, scale=1.0):
        return jax.random.normal(next(ks), shape, f32) * (scale * fan_in ** -0.5)

    def noise(shape, s):
        return jax.random.normal(next(ks), shape, f32) * s

    ratio = jnp.arange(D, dtype=f32) / (D - 1)
    w0_base = -6.0 + 5.0 * ratio ** 0.85 + 0.5
    return {
        "x": jax.random.normal(next(ks), (BATCH, SEQ, D), f32),
        "a_mix": jax.random.uniform(next(ks), (A, 6, D), f32, 0.1, 0.9),
        "a_w_r": dense((A, D, D), D),
        "a_w_k": dense((A, D, D), D),
        "a_w_v": dense((A, D, D), D),
        "a_w_o": dense((A, D, D), D, BETA),
        "a_w0": w0_base[None, :] + noise((A, D), 0.1),
        "a_w1": dense((A, D, D_DECAY_LORA), D, 0.1),
        "a_w2": dense((A, D_DECAY_LORA, D), D_DECAY_LORA, 0.1),
        "a_a0": noise((A, D), 0.1),
        "a_a1": dense((A, D, D_AAA_LORA), D, 0.1),
        "a_a2": dense((A, D_AAA_LORA, D), D_AAA_LORA, 0.1),
        "a_g1": dense((A, D, D_GATE_LORA), D),
        "a_g2": dense((A, D_GATE_LORA, D), D_GATE_LORA),
        "a_k_k": 0.85 + noise((A, D), 0.02),
        "a_k_a": 1.0 + noise((A, D), 0.02),
        "a_r_k": -0.04 + noise((A, H, N), 0.02),
        "a_lnx_w": 1.0 + noise((A, D), 0.02),
        "a_lnx_b": noise((A, D), 0.02),
        "kv_w_k": dense((D, HD), D),
        "kv_w_v": dense((D, HD), D),
        "b_w_q": dense((Bn, D, HD), D),
        "b_w_o": dense((Bn, HD, D), HD, BETA),
        "ffn_w_gate": dense((DEPTH, D, F), D),
        "ffn_w_up": dense((DEPTH, D, F), D),
        "ffn_w_down": dense((DEPTH, F, D), F, BETA),
        "ln1_w": 1.0 + noise((DEPTH, D), 0.02),
        "ln1_b": noise((DEPTH, D), 0.02),
        "ln2_w": 1.0 + noise((DEPTH, D), 0.02),
        "ln2_b": noise((DEPTH, D), 0.02),
    }

def reference(x, a_mix, a_w_r, a_w_k, a_w_v, a_w_o, a_w0, a_w1, a_w2, a_a0, a_a1, a_a2,
              a_g1, a_g2, a_k_k, a_k_a, a_r_k, a_lnx_w, a_lnx_b, kv_w_k, kv_w_v,
              b_w_q, b_w_o, ffn_w_gate, ffn_w_up, ffn_w_down, ln1_w, ln1_b, ln2_w, ln2_b):
    h = x
    k_pad = v_pad = k_mean = None
    for layer in range(DEPTH):
        if layer < N_A_LAYERS:
            i = layer
            mixed = _rwkv7_time_mix(h, a_mix[i], a_w_r[i], a_w_k[i], a_w_v[i], a_w_o[i],
                                    a_w0[i], a_w1[i], a_w2[i], a_a0[i], a_a1[i], a_a2[i],
                                    a_g1[i], a_g2[i], a_k_k[i], a_k_a[i], a_r_k[i],
                                    a_lnx_w[i], a_lnx_b[i])
        else:
            j = layer - N_A_LAYERS
            mixed = _moba_attention(h, b_w_q[j], b_w_o[j], k_pad, v_pad, k_mean)
        h = _layernorm(ALPHA * h + mixed, ln1_w[layer], ln1_b[layer])
        h = _layernorm(ALPHA * h + _swiglu(h, ffn_w_gate[layer], ffn_w_up[layer], ffn_w_down[layer]),
                       ln2_w[layer], ln2_b[layer])
        if layer == N_A_LAYERS - 1:
            k_pad, v_pad, k_mean = _shared_kv(h, kv_w_k, kv_w_v)
    return h


_drawn_inputs = setup_inputs


def setup_inputs(seed=0):
    import zlib

    import numpy as np

    out = dict(_drawn_inputs(seed))
    spreads = {}
    factors = {'a_w1': 8.0,
     'a_w2': 8.0,
     'a_a0': 5.771,
     'a_a1': 8.0,
     'a_a2': 8.0,
     'a_k_k': 8.0,
     'a_k_a': 8.0,
     'a_r_k': 7.811,
     'a_lnx_w': 8.0,
     'a_lnx_b': 8.0}
    for name, (base, spread) in spreads.items():
        noise = np.random.default_rng([zlib.crc32(name.encode()), seed]).standard_normal(out[name].shape)
        drawn = base * np.exp(spread * noise) if base else spread * noise
        out[name] = __import__('jax').numpy.asarray(drawn.astype(out[name].dtype))
    for name, factor in factors.items():
        out[name] = (out[name] * factor).astype(out[name].dtype)
    return out
```

```python
from contextlib import ExitStack

import numpy as np

import concourse.bass as bass
from concourse import mybir

F32 = mybir.dt.float32
F32R = mybir.dt.float32r
ALU = mybir.AluOpType
ACT = mybir.ActivationFunctionType
AX = mybir.AxisListType

P = 128
D = 2048
T = 256
TT = T // P
KT = D // P
NB = 512
NJ = D // NB
FF = 5632
FT = FF // P
FB = FF // NB
KC = 2
RING = 4
CJ = KT // KC
CF = FT // KC
LR = 96
LG = 256
HD = 64
CHUNK = 64
PAIRS = D // P
LEVELS = 6
HEADS = 16
DEPTH = 2
ALPHA = float((2 * DEPTH) ** 0.25)
LN_EPS = 1e-5
GN_EPS = 64e-5
NEG = -1e30
SCALE = float(P) ** -0.5
DECAY = float(np.exp(-0.5))

C_ID, C_TI, C_TE, C_IND, C_AR, C_LM, C_BD, C_CAP = np.cumsum([0, P, P, P, 2, 2 * P, LEVELS * P, P]).tolist()
C_END = C_CAP + 3 * P


def constants():
    i = np.arange(P)
    s, t = i[:, None], i[None, :]
    same = s // CHUNK == t // CHUNK
    c = np.zeros((P, C_END), np.float32)
    c[:, C_ID:C_ID + P] = s == t
    c[:, C_TI:C_TI + P] = np.where(same & (s <= t), -DECAY, 0)
    c[:, C_TE:C_TE + P] = np.where(same & (s < t), -DECAY, 0)
    c[:, C_IND:C_IND + 2] = np.where(s // CHUNK == np.arange(2)[None, :], -DECAY, 0)
    c[:, C_AR:C_AR + P] = same & (s < t)
    c[:, C_AR + P:C_AR + 2 * P] = same & (s <= t)
    for l in range(LEVELS):
        m = 2 ** l
        c[:, C_LM + l * P:C_LM + (l + 1) * P] = (s // (2 * m) == t // (2 * m)) & (t // m % 2 == 1) & (s // m % 2 == 0)
    c[:, C_BD:C_BD + P] = s // HD == t // HD
    cap = np.where(t <= s, 3e38, NEG / SCALE)
    c[:, C_CAP:C_CAP + P] = cap
    c[:, C_CAP + P:C_CAP + 2 * P] = 3e38
    c[:, C_CAP + 2 * P:C_CAP + 3 * P] = cap
    return c


PH = {}
_c = _j = 0
for _name, _jobs, _per in (("proj", 12, CJ), ("wo", NJ, CJ), ("up0", 2 * FB, CJ), ("down0", NJ, CF), ("kvq", 12, CJ),
                           ("ao", NJ, CJ), ("up1", 2 * FB, CJ), ("down1", NJ, CF)):
    assert _c % RING == 0 and _j % 2 == 0
    PH[_name] = (_c, _j)
    _c += _jobs * _per
    _j += _jobs
CHUNKS = _c


class Count:

    def __init__(self, sem):
        self.sem, self.base, self.n = sem, 0, 0

    def up(self, ins):
        ins.then_inc(self.sem, 1)
        self.n += 1

    def now(self, back=0):
        return self.base + (self.n - back)

    def enter(self, i, per):
        self.start, self.per = self.n, per
        self.base = i * per + self.start
        self.n = 0

    def leave(self, trips):
        assert self.n == self.per, (self.n, self.per)
        self.base, self.n = 0, self.start + trips * self.per


def trunk(nc, x, rows, rwkv_rows, lora, w, consts, ln_rows, y):
    with ExitStack() as ctx:
        def sem(name):
            return ctx.enter_context(nc.semaphore(name))

        def sb(name, shape, dt=F32, stack=ctx):
            return stack.enter_context(nc.sbuf_tensor(name, shape, dt))

        raw = sb("raw", [P, RING, KC, NB])
        whi = sb("whi", [P, RING, KC, NB], F32R)
        wlo = sb("wlo", [P, RING, KC, NB], F32R)
        ident = sb("ident", [P, P])
        mixT = sb("mixT", [P, 6 * KT])
        lnT = sb("lnT", [P, 2 * 2 * 2 * KT])
        stats = sb("stats", [P, TT, NJ, 6])
        mv = sb("mv", [P, TT, 2])
        var = sb("var", [P, TT])
        rstd = sb("rstd", [P, TT])
        small = sb("small", [P, 32])
        with ExitStack() as early:
            a2t = sb("a2t", [P, 8192], stack=early)
        ahi = sb("ahi", [P, KT, T], F32R)
        alo = sb("alo", [P, KT, T], F32R)
        with ExitStack() as early:
            big = sb("big", [P, 124 * 256], stack=early)
        common = sb("common", [P, 36 * 256])
        hThi = sb("hThi", [P, FT, T], F32R)
        hTlo = sb("hTlo", [P, FT, T], F32R)
        ps = ctx.enter_context(nc.psum_tensor("ps", [P, 8, NB], F32))

        def carve(base, at, *shape):
            n = int(np.prod(shape))
            v = base[:, at:at + n]
            if len(shape) == 1:
                return v
            names = "abcd"[:len(shape)]
            return v.rearrange(f"p ({' '.join(names)}) -> p {' '.join(names)}", **{q: n for q, n in zip(names[:-1], shape[:-1])})

        KB = 256
        K_ = carve(big, 0, TT, D)
        L_ = carve(big, 16 * KB, TT, D)
        hw = carve(big, 32 * KB, T)
        ha = carve(big, 33 * KB, T)
        hg = carve(big, 34 * KB, 2, T)
        mtmp = carve(big, 36 * KB, 2, KC, T)
        R_ = carve(big, 40 * KB, TT, D)
        V_ = carve(big, 56 * KB, TT, D)
        A_ = carve(big, 72 * KB, TT, D)
        xT = carve(big, 88 * KB, KT, T + 1)
        xxT = carve(big, 88 * KB + KT * (T + 1), KT, T)
        rowsn = carve(big, 121 * KB, P)
        rowsl = carve(big, 122 * KB, P)
        xn = K_
        w1 = carve(big, 56 * KB, KT, LR)
        a1 = carve(big, 62 * KB, KT, LR)
        g1 = carve(big, 40 * KB, KT, LG)
        w2 = carve(big, 0, D)
        a2 = carve(big, 8 * KB, D)
        g2 = carve(big, 56 * KB, 2, D)
        tri_i = carve(a2t, 0, P)
        tri_e = carve(a2t, P, P)
        ind = carve(a2t, 2 * P, 2)
        mask_ar = carve(a2t, 2 * P + 2, 2 * P)
        mask_lv = carve(a2t, 4 * P + 2, LEVELS, P)
        mask_bd = carve(a2t, (4 + LEVELS) * P + 2, P)
        at_ = [C_BD + P - C_TI + 30]

        def tmp(*shape):
            n = int(np.prod(shape))
            v = carve(a2t, at_[0], *shape)
            at_[0] += n
            assert at_[0] <= 8192
            return v

        par = tmp(2, 5, P)
        GB = tmp(4, 2 * P)
        GK = tmp(4, 2 * P)
        X = tmp(4, P)
        XT = tmp(4, P)
        Z = tmp(4, P)
        AmT = tmp(2, 4, P)
        at_b = [88 * KB]

        def tmpb(*shape):
            n = int(np.prod(shape))
            v = carve(big, at_b[0], *shape)
            at_b[0] += n
            assert at_b[0] <= 124 * KB
            return v

        Ls, Vs, Pi, Pn, Pe, kk, sq, bb, kp = (tmpb(TT, P) for _ in range(9))
        bh, kh, rt, at, bon, yy, yq = (tmpb(TT, P) for _ in range(7))
        arT = tmpb(TT, 2, P)
        bkT = tmpb(2, TT, P)
        AV = tmpb(4, HD)
        U = tmpb(TT, P)
        WT = tmpb(TT, P)
        S = tmpb(4, P)
        PC = tmpb(4)
        s4 = tmpb(8, 4)
        H = carve(common, 0, TT, D)
        Zn = carve(common, 16 * KB, TT, D)
        ltmp = carve(common, 32 * KB, 2, KC, T)
        gtmp = carve(common, 32 * KB, TT, NB)
        wb = carve(big, 40 * KB, 2, D)
        Kn = carve(big, 40 * KB, TT, D)
        Vn = carve(big, 56 * KB, TT, D)
        Qn = carve(big, 72 * KB, TT, D)
        Qs = carve(big, 88 * KB, TT, P)
        Ks = carve(big, 89 * KB, TT, P)
        Va = carve(big, 90 * KB, TT, P)
        QKT = carve(big, 91 * KB, 4, P)
        Sm = carve(big, 93 * KB, 3, P)
        Pr = carve(big, 95 * KB, 3, P)
        PT = carve(big, 97 * KB, 3, P)
        cap = carve(big, 99 * KB, 3, P)

        raw_landed = [sem(f"raw_landed{s}") for s in range(RING)]
        hi_done, split_done, chunk_used = sem("hi_done"), sem("split_done"), sem("chunk_used")
        bank_free = [sem("bank_free0"), sem("bank_free1")]
        x_in, rows_in, g1_in, wa1_in, wa2_in, id_in = (sem(n) for n in ("x_in", "rows_in", "g1_in", "wa1_in", "wa2_in", "id_in"))
        xt_made, xt_copied, xx_done, rows_made = (
            sem(n) for n in ("xt_made", "xt_copied", "xx_done", "rows_made"))
        lmix_done, lora1_made, lora1_copied, ones_set, lora2_made, lora2_copied = (
            sem(n) for n in ("lmix_done", "lora1_made", "lora1_copied", "ones_set", "lora2_made", "lora2_copied"))
        mix_done, mixhi_done, act_ready = sem("mix_done"), sem("mixhi_done"), sem("act_ready")
        dve_step, act_step = sem("dve_step"), sem("act_step")
        par_in, masks_in, g2_in, h0_in, wb_in, cap_in = (sem(n) for n in ("par_in", "masks_in", "g2_in", "h0_in", "wb_in", "cap_in"))
        names = ("ls_set vs_set cum_made decay_done rt_done tr_made arT_set bkT_set gb_made gk_made gb_set gk_set am_set z_made z_set "
                 "x_made x_set xt2_made xt2_set av_made av_set uh_made u_set wt_made wt_set pu_made ps_made s_set y_made y_set zz_done")
        q = {n: sem("r_" + n) for n in names.split()}
        gate_made, gated = sem("gate_made"), sem("gated")
        z_tr, z_tr_done = sem("z_tr"), sem("z_tr_done")
        xhat_done, ln_tr, ln_aff, ln_hi, h_done = (sem(n) for n in ("xhat_done", "ln_tr", "ln_aff", "ln_hi", "h_done"))
        h_tr, hhi_done, hlo_done = (sem(n) for n in ("h_tr", "hhi_done", "hlo_done"))
        anames = "qk_staged v_staged qk_tr qkt_set s_made s_capped nm_set p_set p_normed pt_made pt_set o_made ohi_set olo_set"
        t_ = {n: sem("t_" + n) for n in anames.split()}
        y_out = sem("y_out")

        block = ctx.enter_context(nc.Block())

        @block.sync
        def _(sp):
            def chunk(c, s, src):
                if not isinstance(c, int) or c >= RING:
                    sp.wait_ge(split_done, c - (RING - 1))
                sp.dma_start(raw[:, s], src.rearrange("(k p) n -> p k n", p=P)).then_inc(raw_landed[s], 16)

            def stream(c0, mats, kt, col):
                for n, m in enumerate(mats):
                    for j in range(kt // KC):
                        c = n * (kt // KC) + j
                        chunk(c0 + c, c % RING, m[j * KC * P:(j + 1) * KC * P, col])

            def blocks(c0, mats, kt, n):
                per = len(mats) * kt // KC
                if per % RING:
                    with sp.Fori(0, n // 2) as i:
                        for b in range(2):
                            for j in range(kt // KC):
                                c = b * (kt // KC) + j
                                chunk(i * (2 * per) + (c0 + c), c % RING,
                                      mats[0][j * KC * P:(j + 1) * KC * P, bass.ds(i * (2 * NB) + b * NB, NB)])
                else:
                    with sp.Fori(0, n) as i:
                        stream(i * per + c0, mats, kt, bass.ds(i * NB, NB))

            stream(0, [w["k"]], KT, slice(0, NB))
            for b in range(1, NJ):
                stream(b * CJ, [w["k"]], KT, slice(b * NB, (b + 1) * NB))
            blocks(PH["proj"][0] + NJ * CJ, [w["v"]], KT, NJ)
            blocks(PH["proj"][0] + 2 * NJ * CJ, [w["r"]], KT, NJ)
            blocks(PH["wo"][0], [w["o"]], KT, NJ)
            blocks(PH["up0"][0], [w["gate"][0], w["up"][0]], KT, FB)
            blocks(PH["down0"][0], [w["down"][0]], FT, NJ)
            for n, m in enumerate(("kv_k", "kv_v", "q")):
                blocks(PH["kvq"][0] + n * NJ * CJ, [w[m]], KT, NJ)
            blocks(PH["ao"][0], [w["ao"]], KT, NJ)
            blocks(PH["up1"][0], [w["gate"][1], w["up"][1]], KT, FB)
            blocks(PH["down1"][0], [w["down"][1]], FT, NJ)
            yv = y[0].rearrange("(t p) d -> p t d", p=P)
            for t in range(TT):
                sp.wait_ge(h_done, 3 * TT + t + 1)
                sp.dma_start(yv[:, t], H[:, t]).then_inc(y_out, 16)
            sp.wait_ge(y_out, 16 * TT)

        @block.gpsimd
        def _(pool):
            xv = x[0].rearrange("(t p) d -> p t d", p=P)
            nc.gpsimd.dma_start(ident[:], consts[:, C_ID:C_ID + P]).then_inc(id_in, 16)
            nc.gpsimd.dma_start(xn, xv).then_inc(x_in, 16)
            nc.gpsimd.dma_start(rowsn[0:6 * KT], rows).then_inc(rows_in, 16)
            nc.gpsimd.dma_start(rowsl, ln_rows.rearrange("a b n (k p) -> (a b n k) p", p=P)).then_inc(rows_in, 16)
            nc.gpsimd.dma_start(w1, lora["w1"].rearrange("(k p) n -> p k n", p=P)).then_inc(wa1_in, 16)
            nc.gpsimd.dma_start(a1, lora["a1"].rearrange("(k p) n -> p k n", p=P)).then_inc(wa1_in, 16)
            nc.gpsimd.dma_start(g1, lora["g1"].rearrange("(k p) n -> p k n", p=P)).then_inc(g1_in, 16)
            pool.wait_ge(xt_made, KT // KC)
            for dst, m, bias in ((w2, "w2", "w0"), (a2, "a2", "a0")):
                nc.gpsimd.dma_start(dst[0:LR], lora[m]).then_inc(wa2_in, 16)
                nc.gpsimd.dma_start(dst[LR:LR + 1], lora[bias]).then_inc(wa2_in, 16)
            pool.wait_ge(chunk_used, 12 * CJ)
            nc.gpsimd.dma_start(a2t[:, 0:C_BD + P - C_TI], consts[:, C_TI:C_BD + P]).then_inc(masks_in, 16)

            def load_par(p, s):
                src = rwkv_rows[:, bass.ds(p * P, P) if not isinstance(p, int) else slice(p * P, (p + 1) * P)]
                nc.gpsimd.dma_start(par[:, s], src.partition_broadcast(P)).then_inc(par_in, 16)

            load_par(0, 0)
            pool.wait_ge(masks_in, 16)

            def levels(p):
                pool.wait_ge(q["gb_set"], p + 1)
                for l in range(LEVELS):
                    if l >= 2:
                        pool.wait_ge(q["z_made"], p * LEVELS + (l - 1))
                    if l == 2:
                        pool.wait_ge(q["xt2_set"], p * LEVELS + 1)
                    nc.gpsimd.tensor_tensor(AmT[:, l % 2], GB[:, :, 0:P], mask_lv[:, l].unsqueeze(1).broadcast_to([P, 4, P]),
                                            ALU.mult).then_inc(q["am_set"], 1)

            def pair(p, s):
                pool.wait_ge(par_in, (p + 1) * 16)
                if not isinstance(p, int):
                    pool.wait_ge(q["zz_done"], p)
                if not isinstance(p, int) or p == 0:
                    load_par(p + 1, 1 - s)
                levels(p)

            pair(0, 0)
            with pool.Fori(0, PAIRS // 2 - 1) as i:
                for s in range(2):
                    pair(i * 2 + (1 + s), 1 - s)
            pair(PAIRS - 1, 1)
            pool.wait_ge(q["zz_done"], PAIRS)
            nc.gpsimd.dma_start(g2, lora["g2"].rearrange("(k p) n -> p k n", p=P)).then_inc(g2_in, 16)
            nc.gpsimd.dma_start(H, xv).then_inc(h0_in, 16)
            lnw = lambda n: ln_rows[n // 2, n % 2].partition_broadcast(P)

            def load_wb(n, ready, value):
                pool.wait_ge(ready, value)
                nc.gpsimd.dma_start(wb, lnw(n)).then_inc(wb_in, 16)
            load_wb(0, z_tr, KT // KC)
            load_wb(1, chunk_used, PH["kvq"][0])
            nc.gpsimd.dma_start(cap, consts[:, C_CAP:C_END].rearrange("p (a b) -> p a b", a=3)).then_inc(cap_in, 16)
            load_wb(2, t_["qk_staged"], HEADS)
            load_wb(3, chunk_used, CHUNKS)

        @block.tensor
        def _(pe):
            mm, tr = nc.tensor.matmul, nc.tensor.transpose

            def job(c, u, parity, kt, hi, lo):
                pe.wait_ge(bank_free[parity], u + 1)
                for ch in range(kt // KC):
                    s = (ch + (CF * parity if kt == FT else 0)) % RING
                    pe.wait_ge(split_done, c + (ch + 1))
                    for k2 in range(KC):
                        k = ch * KC + k2
                        for t in range(TT):
                            o, tok = ps[:, 2 * parity + t, :], slice(t * P, (t + 1) * P)
                            mm(o, hi[:, k, tok], whi[:, s, k2, :], start=(k == 0), stop=False)
                            mm(o, hi[:, k, tok], wlo[:, s, k2, :], start=False, stop=False)
                            last = mm(o, lo[:, k, tok], whi[:, s, k2, :], start=False, stop=(k == kt - 1))
                    last.then_inc(chunk_used, 1)

            def jobs(c0, j0, n, kt, hi, lo):
                per = kt // KC
                with pe.Fori(0, n // 2) as i:
                    for b in range(2):
                        job(i * (2 * per) + (c0 + b * per), i + j0 // 2, b, kt, hi, lo)

            pe.wait_ge(id_in, 16)
            pe.wait_ge(x_in, 16)
            for g in range(KT // KC):
                if g >= 4:
                    pe.wait_ge(xt_copied, g - 3)
                for k2 in range(KC):
                    for t in range(TT):
                        k = g * KC + k2
                        last = tr(ps[:, 4 + g % 4, k2 * T + t * P:k2 * T + (t + 1) * P], xn[:, t, k * P:(k + 1) * P], ident[:])
                last.then_inc(xt_made, 1)
            pe.wait_ge(rows_in, 32)
            tr(ps[:, 0, 0:6 * KT], rowsn[0:6 * KT], ident[0:6 * KT, 0:6 * KT]).then_inc(rows_made, 1)
            tr(ps[:, 2, 0:P], rowsl, ident[:]).then_inc(rows_made, 1)
            pe.wait_ge(xt_copied, KT // KC)
            pe.wait_ge(wa1_in, 32)
            for n, (m, buf) in enumerate(((w1, L_), (a1, A_))):
                mx = buf.rearrange("p t (k n) -> p (t k) n", n=T)
                for k in range(KT):
                    pe.wait_ge(lmix_done, n * KT + k + 1)
                    last = mm(ps[0:LR, 4 + n, 0:T], m[:, k, :], mx[:, k, :], start=(k == 0), stop=(k == KT - 1))
                last.then_inc(lora1_made, 1)
            pe.wait_ge(g1_in, 16)
            mx = L_.rearrange("p t (k n) -> p (t k) n", n=T)
            for k in range(KT):
                pe.wait_ge(lmix_done, 2 * KT + k + 1)
                for m in range(2):
                    last = mm(ps[:, 6 + m, 0:T], g1[:, k, m * P:(m + 1) * P], mx[:, k, :], start=(k == 0), stop=(k == KT - 1))
            last.then_inc(lora1_made, 1)
            pe.wait_ge(wa2_in, 64)
            pe.wait_ge(ones_set, 2)
            pe.wait_ge(lora1_copied, 4)
            for n in range(2 * NJ):
                if n >= 2:
                    pe.wait_ge(lora2_copied, n - 1)
                h, m = ((hw, w2), (ha, a2))[n // NJ]
                for t in range(TT):
                    last = mm(ps[:, 4 + 2 * (n % 2) + t, :], h[0:LR + 1, t * P:(t + 1) * P],
                              m[0:LR + 1, (n % NJ) * NB:(n % NJ + 1) * NB], start=True, stop=True)
                last.then_inc(lora2_made, 1)
            for n in range(3):
                pe.wait_ge(act_ready, (n + 1) * KT // KC)
                jobs(n * NJ * CJ, n * NJ, NJ, KT, ahi, alo)
            for b in range(2):
                pe.wait_ge(bank_free[b], 7)

            def recur(p):
                one = p + 1
                pe.wait_ge(q["ls_set"], one)
                for m, tri in enumerate((tri_i, tri_e)):
                    for t in range(TT):
                        mm(ps[:, 0, m * T + t * P:m * T + (t + 1) * P], tri, Ls[:, t, :], start=True, stop=True)
                for t in range(TT):
                    last = mm(ps[:, 1, 2 * t:2 * t + 2], Ls[:, t, :], ind, start=True, stop=True)
                last.then_inc(q["cum_made"], 1)
                pe.wait_ge(q["rt_done"], one)
                for t in range(TT):
                    for n, src in enumerate((at, rt)):
                        tr(ps[:, 2, (t * 2 + n) * P:(t * 2 + n + 1) * P], src[:, t, :], ident[:])
                for n, src in enumerate((bh, kh)):
                    for t in range(TT):
                        last = tr(ps[:, 3, (n * TT + t) * P:(n * TT + t + 1) * P], src[:, t, :], ident[:])
                last.then_inc(q["tr_made"], 1)
                pe.wait_ge(q["arT_set"], one)
                pe.wait_ge(q["bkT_set"], one)
                for n, name in enumerate(("gb_made", "gk_made")):
                    for t in range(TT):
                        for h in range(2):
                            hh = slice(h * HD, (h + 1) * HD)
                            last = mm(ps[:, 4 + 2 * n + h, t * T:(t + 1) * T], bkT[hh, n, t, :],
                                      arT[hh, t].rearrange("p a b -> p (a b)"), start=True, stop=True)
                    last.then_inc(q[name], 1)
                for l in range(LEVELS):
                    pe.wait_ge(q["am_set"], p * LEVELS + (l + 1))
                    if l:
                        pe.wait_ge(q["x_set"], p * (LEVELS - 1) + l)
                    for i in range(4):
                        last = mm(ps[:, 0, i * P:(i + 1) * P], AmT[:, l % 2, i, :], X[:, i, :] if l else ident[:], start=True, stop=True)
                    last.then_inc(q["z_made"], 1)
                    if l == 0:
                        continue
                    pe.wait_ge(q["z_set"], p * (LEVELS - 1) + l)
                    pe.wait_ge(q["xt2_set"], p * LEVELS + l)
                    if l < LEVELS - 1:
                        for i in range(4):
                            last = mm(ps[:, 1, i * P:(i + 1) * P], XT[:, i, :], Z[:, i, :], start=True, stop=True)
                        last.then_inc(q["x_made"], 1)
                    for i in range(4):
                        last = mm(ps[:, 2, i * P:(i + 1) * P], Z[:, i, :], XT[:, i, :], start=True, stop=True)
                    last.then_inc(q["xt2_made"], 1)
                pe.wait_ge(q["gk_set"], one)
                pe.wait_ge(q["vs_set"], one)
                for i in range(4):
                    last = mm(ps[:, 3, i * HD:(i + 1) * HD], GK[:, i, 0:P], Vs[:, i % 2, (i // 2) * HD:(i // 2 + 1) * HD], start=True, stop=True)
                last.then_inc(q["av_made"], 1)
                pe.wait_ge(q["xt2_set"], (p + 1) * LEVELS)
                for t in range(TT):
                    for h in range(2):
                        last = mm(ps[h * HD:(h + 1) * HD, 5, t * P:(t + 1) * P], at[:, t, h * HD:(h + 1) * HD], XT[:, 2 * h + t, :],
                                  start=True, stop=True)
                last.then_inc(q["wt_made"], 1)
                pe.wait_ge(q["av_set"], one)
                for i in range(4):
                    last = mm(ps[:, 4, (i % 2) * P + (i // 2) * HD:(i % 2) * P + (i // 2 + 1) * HD], XT[:, i, :], AV[:, i, :], start=True, stop=True)
                last.then_inc(q["uh_made"], 1)
                pe.wait_ge(q["wt_set"], one)
                for c in range(4):
                    t, rows_ = c // 2, slice((c % 2) * CHUNK, (c % 2 + 1) * CHUNK)
                    if c:
                        pe.wait_ge(q["s_set"], p * 3 + c)
                        mm(ps[rows_, 6, 0:P], WT[:, t, rows_], S[:, c, :], start=True, stop=True).then_inc(q["pu_made"], 1)
                    if c < 3:
                        mm(ps[:, 7, 0:P], kh[rows_, t, :], Vs[rows_, t, :], start=True, stop=False)
                        pe.wait_ge(q["u_set"], p * 4 + (c + 1))
                        mm(ps[:, 7, 0:P], bh[rows_, t, :], U[rows_, t, :], start=False, stop=True).then_inc(q["ps_made"], 1)
                pe.wait_ge(q["u_set"], p * 4 + 4)
                for i in range(4):
                    t, hh = i % 2, slice((i // 2) * HD, (i // 2 + 1) * HD)
                    o = ps[:, 1, t * P + hh.start:t * P + hh.stop]
                    mm(o, GB[:, i, P:2 * P], U[:, t, hh], start=(i == 0), stop=False, skip_group_check=True)
                    mm(o, GK[:, i, P:2 * P], Vs[:, t, hh], start=False, stop=False, skip_group_check=True)
                for c in range(1, 4):
                    t, rows_ = c // 2, slice((c % 2) * CHUNK, (c % 2 + 1) * CHUNK)
                    last = mm(ps[rows_, 1, t * P:(t + 1) * P], arT[:, t, 1, rows_], S[:, c, :], start=False, stop=(c == 3), skip_group_check=True)
                last.then_inc(q["y_made"], 1)

            pe.wait_ge(masks_in, 16)
            with pe.Fori(0, PAIRS) as p:
                recur(p)

            pe.wait_ge(g2_in, 16)
            pe.wait_ge(q["y_set"], PAIRS)
            for n in range(NJ):
                if n >= 2:
                    pe.wait_ge(gated, n - 1)
                for t in range(TT):
                    for k in range(2):
                        last = mm(ps[:, 4 + 2 * (n % 2) + t, :], hg[:, k, t * P:(t + 1) * P], g2[:, k, n * NB:(n + 1) * NB], start=(k == 0), stop=(k == 1))
                last.then_inc(gate_made, 1)

            def transpose_act(src, made, made0, done, done0, first_wait):
                first_wait()
                for g in range(KT // KC):
                    if g >= 4:
                        pe.wait_ge(done, done0 + g - 3)
                    for k2 in range(KC):
                        for t in range(TT):
                            k = g * KC + k2
                            last = tr(ps[:, 4 + g % 4, k2 * T + t * P:k2 * T + (t + 1) * P], src[:, t, k * P:(k + 1) * P], ident[:])
                    last.then_inc(made, 1)

            transpose_act(R_, z_tr, 0, z_tr_done, 0, lambda: pe.wait_ge(gated, NJ))
            pe.wait_ge(z_tr_done, KT // KC)
            jobs(*PH["wo"], NJ, KT, ahi, alo)

            def norm_transposes(n):
                transpose_act(Zn, ln_tr, 0, ln_hi, n * KT // KC, lambda: pe.wait_ge(xhat_done, (n + 1) * TT))
                pe.wait_ge(ln_hi, (n + 1) * KT // KC)

            def ffn(layer):
                c0, j0 = PH[f"up{layer}"]
                u0 = layer * FB

                def h_transposes(i):
                    pe.wait_ge(bank_free[1], i + (j0 // 2 + 2 - u0))
                    for f in range(4):
                        for t in range(TT):
                            last = tr(ps[:, 4 + f // 2, (f % 2) * T + t * P:(f % 2) * T + (t + 1) * P], gtmp[:, t, f * P:(f + 1) * P], ident[:])
                    last.then_inc(h_tr, 1)

                job(c0, j0 // 2, 0, KT, ahi, alo)
                job(c0 + CJ, j0 // 2, 1, KT, ahi, alo)
                with pe.Fori(0, FB - 1) as i:
                    job(i * (2 * CJ) + (c0 + 2 * CJ), i + (j0 // 2 + 1), 0, KT, ahi, alo)
                    h_transposes(i + u0)
                    job(i * (2 * CJ) + (c0 + 3 * CJ), i + (j0 // 2 + 1), 1, KT, ahi, alo)
                    pe.wait_ge(hlo_done, i + (u0 + 1))
                h_transposes(u0 + FB - 1)
                pe.wait_ge(hlo_done, u0 + FB)
                jobs(*PH[f"down{layer}"], NJ, FT, hThi, hTlo)

            norm_transposes(0)
            ffn(0)
            norm_transposes(1)
            jobs(*PH["kvq"], 12, KT, ahi, alo)
            for b in range(2):
                pe.wait_ge(bank_free[b], PH["ao"][1] // 2 + 1)
            pe.wait_ge(cap_in, 16)
            with pe.Fori(0, HEADS) as h:
                one = h + 1
                pe.wait_ge(t_["qk_staged"], one)
                for i in range(4):
                    src = (Qs, Ks)[i // 2]
                    last = tr(ps[:, 4, i * P:(i + 1) * P], src[:, i % 2, :], ident[:])
                last.then_inc(t_["qk_tr"], 1)
                pe.wait_ge(t_["qkt_set"], one)
                mm(ps[:, 5, 0:P], QKT[:, 0, :], QKT[:, 2, :], start=True, stop=True)
                mm(ps[:, 5, P:3 * P], QKT[:, 1, :], QKT[:, 2:4, :].rearrange("p a b -> p (a b)"), start=True, stop=True).then_inc(t_["s_made"], 1)
                pe.wait_ge(t_["p_normed"], one)
                for i in range(3):
                    last = tr(ps[:, 6, i * P:(i + 1) * P], Pr[:, i, :], ident[:])
                last.then_inc(t_["pt_made"], 1)
                pe.wait_ge(t_["pt_set"], one)
                pe.wait_ge(t_["v_staged"], one)
                mm(ps[:, 7, 0:T], Va[:, 0, :], PT[:, 0:2, :].rearrange("p a b -> p (a b)"), start=True, stop=False, skip_group_check=True)
                mm(ps[:, 7, P:T], Va[:, 1, :], PT[:, 2, :], start=False, stop=True, skip_group_check=True).then_inc(t_["o_made"], 1)
            pe.wait_ge(t_["olo_set"], HEADS)
            jobs(*PH["ao"], NJ, KT, ahi, alo)
            norm_transposes(2)
            ffn(1)

        @block.scalar
        def _(act):
            A = nc.scalar.activation

            def split_hi(c, u, n):
                for ch in range(n):
                    s = ch % RING
                    act.wait_ge(raw_landed[s], (u + ch // RING + 1) * 16)
                    if not isinstance(c, int) or c + ch >= RING:
                        act.wait_ge(chunk_used, c + (ch - RING + 1))
                    nc.scalar.copy(whi[:, s], raw[:, s]).then_inc(hi_done, 1)

            for g in range(KT // KC):
                act.wait_ge(xt_made, g + 1)
                nc.scalar.copy(xT[:, g * KC:(g + 1) * KC, 1:T + 1], ps[:, 4 + g % 4, :].rearrange("p (k t) -> p k t", k=KC)).then_inc(xt_copied, 1)
            act.wait_ge(rows_made, 2)
            nc.scalar.copy(mixT[:], ps[:, 0, 0:6 * KT]).then_inc(bank_free[0], 1)
            nc.scalar.copy(lnT[:], ps[:, 2, 0:P]).then_inc(bank_free[1], 1)
            split_hi(0, 0, RING)
            act.wait_ge(lora1_made, 1)
            A(hw[0:LR], ps[0:LR, 4, 0:T], ACT.Tanh).then_inc(lora1_copied, 1)
            act.wait_ge(lora1_made, 2)
            nc.scalar.copy(ha[0:LR], ps[0:LR, 5, 0:T]).then_inc(lora1_copied, 1)
            act.wait_ge(lora1_made, 3)
            for m in range(2):
                A(hg[:, m], ps[:, 6 + m, 0:T], ACT.Sigmoid).then_inc(lora1_copied, 1)
            for n in range(2 * NJ):
                act.wait_ge(lora2_made, n + 1)
                dst = (L_, A_)[n // NJ][:, :, (n % NJ) * NB:(n % NJ + 1) * NB]
                A(dst, ps[:, 4 + 2 * (n % 2):6 + 2 * (n % 2), :], ACT.Sigmoid).then_inc(lora2_copied, 1)

            def project(c0, n, dst):
                with act.Fori(0, n // 2) as i:
                    for b in range(2):
                        split_hi(i * (2 * CJ) + (c0 + b * CJ + RING), i * (2 * CJ // RING) + (c0 + b * CJ + RING) // RING, CJ)
                        act.wait_ge(chunk_used, i * (2 * CJ) + (c0 + (b + 1) * CJ))
                        nc.scalar.copy(dst[:, :, bass.ds(i * (2 * NB) + b * NB, NB)], ps[:, 2 * b:2 * b + 2, :]).then_inc(bank_free[b], 1)

            for n, dst in enumerate((K_, V_, R_)):
                for g in range(KT // KC):
                    act.wait_ge(mix_done, n * (KT // KC) + g + 1)
                    nc.scalar.copy(ahi[:, g * KC:(g + 1) * KC], mtmp[:, g % 2]).then_inc(mixhi_done, 1)
                project(n * NJ * CJ, NJ, dst)
            act.wait_ge(bank_free[0], 7)
            act.wait_ge(bank_free[1], 7)

            def recur(p):
                one = p + 1
                nc.scalar.copy(Ls, L_[:, :, bass.ds(p * P, P)]).then_inc(q["ls_set"], 1)
                nc.scalar.copy(Vs, V_[:, :, bass.ds(p * P, P)]).then_inc(q["vs_set"], 1)
                act.wait_ge(q["cum_made"], one)
                ci = ps[:, 0, 0:T].rearrange("p (t c) -> p t c", t=TT)
                ce = ps[:, 0, T:2 * T].rearrange("p (t c) -> p t c", t=TT)
                A(Pi, ci, ACT.Exp)
                A(Pn, ci, ACT.Exp, scale=-1.0)
                A(Pe, ce, ACT.Exp)
                A(PC, ps[:, 1, 0:4], ACT.Exp).then_inc(q["decay_done"], 1)
                act.wait_ge(q["tr_made"], one)
                nc.scalar.copy(arT, ps[:, 2, :].rearrange("p (t a b) -> p t a b", t=TT, a=2)).then_inc(q["arT_set"], 1)
                for l in range(1, LEVELS):
                    act.wait_ge(q["z_made"], p * LEVELS + (l + 1))
                    nc.scalar.copy(Z, ps[:, 0, :].rearrange("p (a b) -> p a b", a=4)).then_inc(q["z_set"], 1)
                act.wait_ge(q["av_made"], one)
                nc.scalar.copy(AV, ps[:, 3, 0:T].rearrange("p (a b) -> p a b", a=4)).then_inc(q["av_set"], 1)
                act.wait_ge(q["wt_made"], one)
                nc.scalar.copy(WT, ps[:, 5, 0:T].rearrange("p (t b) -> p t b", t=TT)).then_inc(q["wt_set"], 1)
                act.wait_ge(q["y_made"], one)
                nc.scalar.copy(yy, ps[:, 1, 0:T].rearrange("p (t b) -> p t b", t=TT)).then_inc(q["y_set"], 1)
                act.wait_ge(q["zz_done"], one)

            with act.Fori(0, PAIRS) as p:
                recur(p)

            for g in range(KT // KC):
                act.wait_ge(z_tr, g + 1)
                nc.scalar.copy(ahi[:, g * KC:(g + 1) * KC], ps[:, 4 + g % 4, :].rearrange("p (k t) -> p k t", k=KC)).then_inc(mixhi_done, 1)

            def quiet_jobs(c0, n, kt, last=False):
                per = kt // KC
                rounds = n // 2 - (1 if last else 0)
                if rounds:
                    with act.Fori(0, rounds) as i:
                        split_hi(i * (2 * per) + (c0 + RING), i * (2 * per // RING) + (c0 + RING) // RING, 2 * per)
                if last:
                    c = c0 + rounds * 2 * per + RING
                    split_hi(c, c // RING, 2 * per - RING)

            def norm_affine(n):
                for g in range(KT // KC):
                    act.wait_ge(ln_tr, n * (KT // KC) + g + 1)
                    if g >= 2 or n:
                        act.wait_ge(ln_hi, n * (KT // KC) + g - 1)
                    for k2 in range(KC):
                        k = g * KC + k2
                        ins = A(ltmp[:, g % 2, k2], ps[:, 4 + g % 4, k2 * T:(k2 + 1) * T], ACT.Identity,
                                scale=lnT[:, (n * 2) * KT + k:(n * 2) * KT + k + 1],
                                bias=lnT[:, (n * 2 + 1) * KT + k:(n * 2 + 1) * KT + k + 1])
                    ins.then_inc(ln_aff, 1)

            def ffn(layer):
                c0, _ = PH[f"up{layer}"]
                u0 = layer * FB

                def hidden_hi(i, f0):
                    act.wait_ge(h_tr, i + 1)
                    A(hThi[:, f0, :], ps[:, 4:6, :].rearrange("p a (k t) -> p (a k) t", k=2), ACT.Copy).then_inc(hhi_done, 1)

                split_hi(c0 + RING, c0 // RING + 1, CJ)
                act.wait_ge(chunk_used, c0 + CJ)
                A(gtmp, ps[:, 0:2, :], ACT.Silu).then_inc(bank_free[0], 1)
                split_hi(c0 + RING + CJ, c0 // RING + 1 + CJ // RING, CJ)
                act.wait_ge(h_done, (1 if layer == 0 else 3) * TT)
                with act.Fori(0, FB - 1) as i:
                    c = i * (2 * CJ) + (c0 + 2 * CJ)
                    u = i * (2 * CJ // RING) + (c0 + 2 * CJ) // RING
                    split_hi(c + RING, u + 1, CJ)
                    act.wait_ge(h_tr, i + (u0 + 1))
                    act.wait_ge(chunk_used, c + CJ)
                    A(gtmp, ps[:, 0:2, :], ACT.Silu).then_inc(bank_free[0], 1)
                    hidden_hi(i + u0, bass.ds(i * 4, 4))
                    split_hi(c + (RING + CJ), u + (1 + CJ // RING), CJ)
                hidden_hi(u0 + FB - 1, slice((FB - 1) * 4, FB * 4))
                quiet_jobs(PH[f"down{layer}"][0], NJ, FT, last=(layer == 1))

            quiet_jobs(PH["wo"][0], NJ, KT)
            norm_affine(0)
            ffn(0)
            norm_affine(1)
            act.wait_ge(h_done, 2 * TT)
            for n, dst in enumerate((Kn, Vn, Qn)):
                project(PH["kvq"][0] + n * NJ * CJ, NJ, dst)
            act.wait_ge(bank_free[0], PH["ao"][1] // 2 + 1)
            act.wait_ge(bank_free[1], PH["ao"][1] // 2 + 1)
            with act.Fori(0, HEADS) as h:
                one = h + 1
                nc.scalar.copy(Qs, Qn[:, :, bass.ds(h * P, P)])
                nc.scalar.copy(Ks, Kn[:, :, bass.ds(h * P, P)]).then_inc(t_["qk_staged"], 1)
                act.wait_ge(t_["qk_tr"], one)
                nc.scalar.copy(QKT, ps[:, 4, :].rearrange("p (a b) -> p a b", a=4)).then_inc(t_["qkt_set"], 1)
                act.wait_ge(t_["nm_set"], one)
                A(Pr[:, 0, :], Sm[:, 0, :], ACT.Exp, bias=small[:, 2:3], scale=SCALE, accum_out=small[:, 4:5])
                A(Pr[:, 1:3, :], Sm[:, 1:3, :], ACT.Exp, bias=small[:, 3:4], scale=SCALE, accum_out=small[:, 5:6]).then_inc(t_["p_set"], 1)
                act.wait_ge(t_["pt_made"], one)
                nc.scalar.copy(PT, ps[:, 6, 0:3 * P].rearrange("p (a b) -> p a b", a=3)).then_inc(t_["pt_set"], 1)
                act.wait_ge(t_["o_made"], one)
                A(ahi[:, bass.ds(h, 1), :], ps[:, 7, 0:T].unsqueeze(1), ACT.Copy).then_inc(t_["ohi_set"], 1)
            quiet_jobs(PH["ao"][0], NJ, KT)
            norm_affine(2)
            ffn(1)

        @block.vector
        def _(dve):
            V = nc.vector
            step = Count(dve_step)

            def then(ins):
                step.up(ins)
                dve.wait_ge(dve_step, step.now())

            def rsqrt(dst, src, t):
                I32 = mybir.dt.int32
                then(V.tensor_scalar(t.bitcast(I32), src.bitcast(I32), 1, None, ALU.logical_shift_right))
                then(V.tensor_scalar(dst.bitcast(I32), t.bitcast(I32), -1.0, float(0x5F3759DF), ALU.mult, ALU.add))
                for _ in range(3):
                    then(V.tensor_tensor(t, dst, dst, ALU.mult))
                    then(V.scalar_tensor_tensor(out=t, in0=t, scalar=-0.5, in1=src, op0=ALU.mult, op1=ALU.mult))
                    then(V.scalar_tensor_tensor(out=dst, in0=t, scalar=1.5, in1=dst, op0=ALU.add, op1=ALU.mult))

            def split_lo(c, n):
                for ch in range(n):
                    s = ch % RING
                    dve.wait_ge(hi_done, c + (ch + 1))
                    V.tensor_tensor(wlo[:, s], raw[:, s], whi[:, s].bitcast(F32), ALU.subtract).then_inc(split_done, 1)

            then(V.memset(xT[:, :, 0:1], 0.0))
            V.memset(hw[LR:LR + 1], 1.0).then_inc(ones_set, 1)
            V.memset(ha[LR:LR + 1], 1.0).then_inc(ones_set, 1)
            for g in range(KT // KC):
                dve.wait_ge(xt_copied, g + 1)
                k = slice(g * KC, (g + 1) * KC)
                V.tensor_tensor(xxT[:, k], xT[:, k, 0:T], xT[:, k, 1:T + 1], ALU.subtract).then_inc(xx_done, 1)
            dve.wait_ge(xx_done, KT // KC)
            dve.wait_ge(bank_free[0], 1)

            def mixed(out, m, k):
                return V.scalar_tensor_tensor(out=out, in0=xxT[:, k], scalar=mixT[:, m * KT + k:m * KT + k + 1], in1=xT[:, k, 1:T + 1],
                                              op0=ALU.mult, op1=ALU.add)

            for n, (m, buf) in enumerate(((1, L_), (4, A_), (5, L_))):
                mx = buf.rearrange("p t (k n) -> p (t k) n", n=T)
                if n == 2:
                    dve.wait_ge(lora1_made, 1)
                for k in range(KT):
                    mixed(mx[:, k], m, k).then_inc(lmix_done, 1)
            split_lo(0, RING)

            def mix_split(n, m):
                for g in range(KT // KC):
                    if g >= 2 or n:
                        dve.wait_ge(act_ready, n * (KT // KC) + g - 1)
                    if g == 0 and n:
                        dve.wait_ge(chunk_used, n * NJ * CJ)
                    for k2 in range(KC):
                        ins = mixed(mtmp[:, g % 2, k2], m, g * KC + k2)
                    ins.then_inc(mix_done, 1)
                    if g:
                        tail(n, g - 1)
                tail(n, KT // KC - 1)

            def tail(n, g):
                dve.wait_ge(mixhi_done, n * (KT // KC) + g + 1)
                V.tensor_tensor(alo[:, g * KC:(g + 1) * KC], mtmp[:, g % 2], ahi[:, g * KC:(g + 1) * KC].bitcast(F32),
                                ALU.subtract).then_inc(act_ready, 1)

            def quiet(c0, n, kt=KT, last=False):
                per = kt // KC
                with dve.Fori(0, n // 2) as i:
                    split_lo(i * (2 * per) + (c0 + RING), 2 * per)

            for n, m in enumerate((2, 3, 0)):
                mix_split(n, m)
                quiet(n * NJ * CJ, NJ)

            def bcast_row(v):
                return v.unsqueeze(1).broadcast_to([P, TT, P])

            def heads(v):
                return v.rearrange("p t (h i) -> p (t h) i", h=2)

            def bcast_head(v):
                return v.unsqueeze(2).broadcast_to([P, 4, HD])

            dve.wait_ge(masks_in, 16)
            N_STEP = 22 + 2 * 11

            def recur(p):
                one = p + 1
                cs = bass.ds(p * P, P)
                dve.wait_ge(par_in, one * 16)
                k_k, k_a, r_k, lnw, lnb = (bcast_row(par_cur[0][:, j, :]) for j in range(5))
                then(V.tensor_tensor(kk, K_[:, :, cs], k_k, ALU.mult))
                then(V.tensor_tensor(sq, kk, kk, ALU.mult))
                then(V.tensor_reduce(s4[:, 0, :], heads(sq), AX.X, ALU.add))
                then(V.tensor_scalar(s4[:, 6, :], s4[:, 0, :], 1e-24, None, ALU.max))
                rsqrt(s4[:, 1, :], s4[:, 6, :], s4[:, 7, :])
                then(V.tensor_tensor(heads(kk), heads(kk), bcast_head(s4[:, 1, :]), ALU.mult))
                V.tensor_tensor(bb, kk, A_[:, :, cs], ALU.mult)
                then(V.scalar_tensor_tensor(out=sq, in0=A_[:, :, cs], scalar=1.0, in1=k_a, op0=ALU.subtract, op1=ALU.mult))
                then(V.scalar_tensor_tensor(out=kp, in0=sq, scalar=1.0, in1=K_[:, :, cs], op0=ALU.add, op1=ALU.mult))
                then(V.tensor_tensor(sq, kp, r_k, ALU.mult))
                then(V.tensor_tensor(sq, sq, R_[:, :, cs], ALU.mult))
                then(V.tensor_reduce(s4[:, 2, :], heads(sq), AX.X, ALU.add))
                dve.wait_ge(q["decay_done"], one)
                V.scalar_tensor_tensor(out=at, in0=kk, scalar=-1.0, in1=Pe, op0=ALU.mult, op1=ALU.mult)
                V.tensor_tensor(bh, bb, Pn, ALU.mult)
                V.tensor_tensor(kh, kp, Pn, ALU.mult)
                V.tensor_tensor(rt, R_[:, :, cs], Pi, ALU.mult).then_inc(q["rt_done"], 1)
                dve.wait_ge(q["tr_made"], one)
                V.tensor_copy(bkT, ps[:, 3, :].rearrange("p (a t b) -> p a t b", a=2, t=TT)).then_inc(q["bkT_set"], 1)
                for g, bank, made, done in ((GB, 4, "gb_made", "gb_set"), (GK, 6, "gk_made", "gk_set")):
                    dve.wait_ge(q[made], one)
                    V.tensor_tensor(g, ps[:, bank:bank + 2, :].rearrange("p a (b c) -> p (a b) c", b=2),
                                    mask_ar.unsqueeze(1).broadcast_to([P, 4, 2 * P]), ALU.mult).then_inc(q[done], 1)
                idb = ident[:].unsqueeze(1).broadcast_to([P, 4, P])

                def bank4(b):
                    return ps[:, b, :].rearrange("p (a b) -> p a b", a=4)

                dve.wait_ge(q["z_made"], p * LEVELS + 1)
                V.tensor_tensor(X, bank4(0), idb, ALU.add).then_inc(q["x_set"], 1)
                V.tensor_tensor(XT, AmT[:, 0], idb, ALU.add).then_inc(q["xt2_set"], 1)
                for l in range(1, LEVELS):
                    if l < LEVELS - 1:
                        dve.wait_ge(q["x_made"], p * (LEVELS - 2) + l)
                        V.tensor_tensor(X, bank4(1), X, ALU.add).then_inc(q["x_set"], 1)
                    dve.wait_ge(q["xt2_made"], p * (LEVELS - 1) + l)
                    V.tensor_tensor(XT, bank4(2), XT, ALU.add).then_inc(q["xt2_set"], 1)
                dve.wait_ge(q["uh_made"], one)
                V.tensor_copy(U, ps[:, 4, 0:T].rearrange("p (t b) -> p t b", t=TT)).then_inc(q["u_set"], 1)
                dve.wait_ge(q["u_set"], p * 4 + 1)
                for c in range(4):
                    t, rows_ = c // 2, slice((c % 2) * CHUNK, (c % 2 + 1) * CHUNK)
                    if c:
                        dve.wait_ge(q["pu_made"], p * 3 + c)
                        V.tensor_tensor(U[rows_, t], ps[rows_, 6, 0:P], U[rows_, t], ALU.add).then_inc(q["u_set"], 1)
                    if c < 3:
                        dve.wait_ge(q["ps_made"], p * 3 + (c + 1))
                        src = ps[:, 7, 0:P]
                        if c:
                            then(V.tensor_tensor(yq[:, 0], src, S[:, c], ALU.add))
                            src = yq[:, 0]
                        V.scalar_tensor_tensor(out=S[:, c + 1], in0=src, scalar=PC[:, c:c + 1], in1=mask_bd, op0=ALU.mult,
                                               op1=ALU.mult).then_inc(q["s_set"], 1)
                        dve.wait_ge(q["s_set"], p * 3 + (c + 1))
                dve.wait_ge(q["y_set"], one)
                then(V.tensor_reduce(s4[:, 3, :], heads(yy), AX.X, ALU.add))
                then(V.tensor_scalar(s4[:, 4, :], s4[:, 3, :], 1.0 / HD, None, ALU.mult))
                then(V.tensor_tensor(heads(yy), heads(yy), bcast_head(s4[:, 4, :]), ALU.subtract))
                then(V.tensor_tensor(yq, yy, yy, ALU.mult))
                then(V.tensor_reduce(s4[:, 5, :], heads(yq), AX.X, ALU.add))
                then(V.tensor_scalar(s4[:, 6, :], s4[:, 5, :], 1.0 / HD, GN_EPS, ALU.mult, ALU.add))
                rsqrt(s4[:, 7, :], s4[:, 6, :], s4[:, 3, :])
                then(V.tensor_tensor(heads(yy), heads(yy), bcast_head(s4[:, 7, :]), ALU.mult))
                then(V.tensor_tensor(yy, yy, lnw, ALU.mult))
                then(V.tensor_tensor(yy, yy, lnb, ALU.add))
                then(V.tensor_tensor(heads(bon), heads(Vs), bcast_head(s4[:, 2, :]), ALU.mult))
                V.tensor_tensor(R_[:, :, cs], yy, bon, ALU.add).then_inc(q["zz_done"], 1)

            par_cur = [None]
            dve.wait_ge(bank_free[0], 7)
            dve.wait_ge(bank_free[1], 7)
            with dve.Fori(0, PAIRS // 2) as i:
                step.enter(i, 2 * N_STEP)
                for s in range(2):
                    par_cur[0] = par[:, s]
                    recur(i * 2 + s)
                step.leave(PAIRS // 2)

            dve.wait_ge(q["zz_done"], PAIRS)
            for n in range(NJ):
                dve.wait_ge(gate_made, n + 1)
                c = slice(n * NB, (n + 1) * NB)
                V.tensor_tensor(R_[:, :, c], R_[:, :, c], ps[:, 4 + 2 * (n % 2):6 + 2 * (n % 2), :], ALU.mult).then_inc(gated, 1)
            for g in range(KT // KC):
                dve.wait_ge(mixhi_done, 3 * (KT // KC) + g + 1)
                V.tensor_tensor(alo[:, g * KC:(g + 1) * KC], ps[:, 4 + g % 4, :].rearrange("p (k t) -> p k t", k=KC),
                                ahi[:, g * KC:(g + 1) * KC].bitcast(F32), ALU.subtract).then_inc(z_tr_done, 1)

            def residual(c0, kt, n, last=False):
                per = kt // KC
                for b in range(NJ):
                    left = per if not (last and b == NJ - 1) else per - RING
                    first = c0 + b * per + RING
                    for ch in range(left):
                        s = (first + ch) % RING
                        dve.wait_ge(hi_done, first + ch + 1)
                        V.tensor_tensor(wlo[:, s], raw[:, s], whi[:, s].bitcast(F32), ALU.subtract).then_inc(split_done, 1)
                    dve.wait_ge(chunk_used, c0 + (b + 1) * per)
                    if b == 0 and n == 0:
                        dve.wait_ge(h0_in, 16)
                    cs = slice(b * NB, (b + 1) * NB)
                    V.scalar_tensor_tensor(out=Zn[:, :, cs], in0=H[:, :, cs], scalar=ALPHA, in1=ps[:, 2 * (b % 2):2 * (b % 2) + 2, :],
                                           op0=ALU.mult, op1=ALU.add).then_inc(bank_free[b % 2], 1)
                    dve.wait_ge(bank_free[b % 2], (c_jobs[n] + b) // 2 + 2)
                    for t in range(TT):
                        ins = V.bn_stats(stats[:, t, b, :], Zn[:, t, cs])
                then(ins)
                for t in range(TT):
                    then(V.bn_aggr(mv[:, t, :], stats[:, t]))
                then(V.tensor_scalar(var[:], mv[:, :, 1], LN_EPS, None, ALU.add))
                rsqrt(rstd[:], var[:], small[:, 8:8 + TT])
                for t in range(TT):
                    V.tensor_scalar(Zn[:, t], Zn[:, t], mv[:, t, 0:1], rstd[:, t:t + 1], ALU.subtract, ALU.mult).then_inc(xhat_done, 1)

            c_jobs = [PH["wo"][1], PH["down0"][1], PH["ao"][1], PH["down1"][1]]

            def norm_split(n):
                for g in range(KT // KC):
                    dve.wait_ge(ln_aff, n * (KT // KC) + g + 1)
                    k = slice(g * KC, (g + 1) * KC)
                    then(V.tensor_copy(ahi[:, k], ltmp[:, g % 2]))
                    V.tensor_tensor(alo[:, k], ltmp[:, g % 2], ahi[:, k].bitcast(F32), ALU.subtract).then_inc(ln_hi, 1)

            def natural(n):
                dve.wait_ge(wb_in, (n + 1) * 16)
                dve.wait_ge(xhat_done, (n + 1) * TT)
                for t in range(TT):
                    then(V.tensor_tensor(H[:, t], Zn[:, t], wb[:, 0], ALU.mult))
                    V.tensor_tensor(H[:, t], H[:, t], wb[:, 1], ALU.add).then_inc(h_done, 1)

            def ffn(layer):
                c0, j0 = PH[f"up{layer}"]
                u0 = layer * FB

                def multiply(c_end, up_seen):
                    dve.wait_ge(bank_free[0], up_seen)
                    dve.wait_ge(chunk_used, c_end)
                    V.tensor_tensor(gtmp, gtmp, ps[:, 2:4, :], ALU.mult).then_inc(bank_free[1], 1)

                def hidden_lo(i, f0):
                    dve.wait_ge(hhi_done, i + 1)
                    V.tensor_tensor(hTlo[:, f0, :], ps[:, 4:6, :].rearrange("p a (k t) -> p (a k) t", k=2),
                                    hThi[:, f0, :].bitcast(F32), ALU.subtract).then_inc(hlo_done, 1)

                natural(0 if layer == 0 else 2)
                split_lo(c0 + RING, 2 * CJ)
                with dve.Fori(0, FB - 1) as i:
                    c = i * (2 * CJ) + (c0 + 2 * CJ)
                    multiply(c, i + (j0 // 2 + 2))
                    split_lo(c + RING, CJ)
                    hidden_lo(i + u0, bass.ds(i * 4, 4))
                    split_lo(c + (RING + CJ), CJ)
                multiply(c0 + FB * 2 * CJ, j0 // 2 + FB + 1)
                hidden_lo(u0 + FB - 1, slice((FB - 1) * 4, FB * 4))

            residual(PH["wo"][0], KT, 0)
            norm_split(0)
            ffn(0)
            residual(PH["down0"][0], FT, 1)
            norm_split(1)
            natural(1)
            quiet(PH["kvq"][0], 12)
            dve.wait_ge(bank_free[0], PH["ao"][1] // 2 + 1)
            dve.wait_ge(bank_free[1], PH["ao"][1] // 2 + 1)
            dve.wait_ge(cap_in, 16)
            with dve.Fori(0, HEADS) as h:
                step.enter(h, 3)
                one = h + 1
                V.tensor_copy(Va, Vn[:, :, bass.ds(h * P, P)]).then_inc(t_["v_staged"], 1)
                dve.wait_ge(t_["s_made"], one)
                then(V.tensor_tensor(Sm, ps[:, 5, 0:3 * P].rearrange("p (a b) -> p a b", a=3), cap, ALU.min))
                V.tensor_reduce(small[:, 0:1], Sm[:, 0, :], AX.X, ALU.max)
                then(V.tensor_reduce(small[:, 1:2], Sm[:, 1:3, :], AX.XY, ALU.max))
                V.tensor_scalar(small[:, 2:4], small[:, 0:2], NEG / SCALE, -SCALE, ALU.max, ALU.mult).then_inc(t_["nm_set"], 1)
                dve.wait_ge(t_["p_set"], one)
                then(V.reciprocal(small[:, 6:8], small[:, 4:6]))
                V.tensor_scalar(Pr[:, 0, :], Pr[:, 0, :], small[:, 6:7], None, ALU.mult)
                V.tensor_scalar(Pr[:, 1:3, :], Pr[:, 1:3, :], small[:, 7:8], None, ALU.mult).then_inc(t_["p_normed"], 1)
                dve.wait_ge(t_["ohi_set"], one)
                V.tensor_tensor(alo[:, bass.ds(h, 1), :], ps[:, 7, 0:T].unsqueeze(1), ahi[:, bass.ds(h, 1), :].bitcast(F32),
                                ALU.subtract).then_inc(t_["olo_set"], 1)
                step.leave(HEADS)
            residual(PH["ao"][0], KT, 2)
            norm_split(2)
            ffn(1)
            residual(PH["down1"][0], FT, 3, last=True)
            natural(3)


_OUT = ((1, T, D), "float32")


def kernel(**inputs):
    import concourse.bacc as bacc
    from concourse.bass_utils import run_bass_kernel_spmd as run

    nc = bacc.Bacc("TRN2", target_bir_lowering=False, num_devices=1)
    arrays = {}

    def give(name, a):
        a = np.ascontiguousarray(a)
        arrays[name] = a
        return nc.dram_tensor(name, a.shape, mybir.dt.from_np(a.dtype), kind="ExternalInput").ap()

    i = {k: np.asarray(v) for k, v in inputs.items()}
    x = give("x", i["x"])
    rows = give("mix_rows", i["a_mix"][0].reshape(6 * KT, P))
    rwkv_rows = give("rwkv_rows", np.stack([i["a_k_k"][0], i["a_k_a"][0], i["a_r_k"][0].reshape(D), i["a_lnx_w"][0], i["a_lnx_b"][0]]))
    lora = {m: give("lora_" + m, i["a_" + m][0]) for m in ("w1", "w2", "a1", "a2", "g1", "g2")}
    lora.update({m: give("lora_" + m, i["a_" + m]) for m in ("w0", "a0")})
    w = {"r": give("w_r", i["a_w_r"][0]), "k": give("w_k", i["a_w_k"][0]), "v": give("w_v", i["a_w_v"][0]), "o": give("w_o", i["a_w_o"][0]),
         "kv_k": give("kv_k", i["kv_w_k"]), "kv_v": give("kv_v", i["kv_w_v"]), "q": give("w_q", i["b_w_q"][0]), "ao": give("w_ao", i["b_w_o"][0]),
         "gate": give("w_gate", i["ffn_w_gate"]), "up": give("w_up", i["ffn_w_up"]), "down": give("w_down", i["ffn_w_down"])}
    ln = give("ln_rows", np.stack([np.stack([np.stack([i[f"ln{n}_w"][l], i[f"ln{n}_b"][l]]) for n in (1, 2)]) for l in range(DEPTH)]))
    c = give("consts", constants())
    y = nc.dram_tensor("y", _OUT[0], F32, kind="ExternalOutput").ap()
    trunk(nc, x, rows, rwkv_rows, lora, w, c, ln, y)
    return run(nc, [arrays], core_ids=[0]).results[0]["y"]
```

```python
from contextlib import ExitStack

import numpy as np

import concourse.bass as bass
from concourse import mybir

F32 = mybir.dt.float32
F32R = mybir.dt.float32r
ALU = mybir.AluOpType
ACT = mybir.ActivationFunctionType
AX = mybir.AxisListType

P = 128
D = 2048
T = 256
TT = T // P
KT = D // P
NB = 512
NJ = D // NB
FF = 5632
FT = FF // P
FB = FF // NB
KC = 2
RING = 4
CJ = KT // KC
CF = FT // KC
LR = 96
LG = 256
HD = 64
CHUNK = 64
PAIRS = D // P
LEVELS = 6
HEADS = 16
DEPTH = 2
ALPHA = float((2 * DEPTH) ** 0.25)
LN_EPS = 1e-5
GN_EPS = 64e-5
NEG = -1e30
SCALE = float(P) ** -0.5
DECAY = float(np.exp(-0.5))

C_ID, C_TI, C_TE, C_IND, C_AR, C_LM, C_BD, C_CAP = np.cumsum(
    [0, P, P, P, 2, 2 * P, LEVELS * P, P]).tolist()
C_END = C_CAP + 3 * P


def constants():
    i = np.arange(P)
    s, t = i[:, None], i[None, :]
    same = s // CHUNK == t // CHUNK
    c = np.zeros((P, C_END), np.float32)
    c[:, C_ID:C_ID + P] = s == t
    c[:, C_TI:C_TI + P] = np.where(same & (s <= t), -DECAY, 0)
    c[:, C_TE:C_TE + P] = np.where(same & (s < t), -DECAY, 0)
    c[:, C_IND:C_IND + 2] = np.where(s // CHUNK == np.arange(2)[None, :], -DECAY, 0)
    c[:, C_AR:C_AR + P] = same & (s < t)
    c[:, C_AR + P:C_AR + 2 * P] = same & (s <= t)
    for l in range(LEVELS):
        m = 2 ** l
        a, b = (s, t) if l else (t, s)
        c[:, C_LM + l * P:C_LM + (l + 1) * P] = (s == t) | ((a // (2 * m) == b // (2 * m)) & (a // m % 2 == 1) & (b // m % 2 == 0))
    c[:, C_BD:C_BD + P] = s // HD == t // HD
    cap = np.where(t <= s, 3e38, NEG / SCALE)
    c[:, C_CAP:C_CAP + P] = cap
    c[:, C_CAP + P:C_CAP + 2 * P] = 3e38
    c[:, C_CAP + 2 * P:C_CAP + 3 * P] = cap
    return c


PH = {}
_c = _j = 0
for _name, _jobs, _per in (("proj", 12, CJ), ("wo", NJ, CJ), ("up0", 2 * FB, CJ), ("down0", NJ, CF), ("kvq", 12, CJ),
                           ("ao", NJ, CJ), ("up1", 2 * FB, CJ), ("down1", NJ, CF)):
    assert _c % RING == 0 and _j % 2 == 0
    PH[_name] = (_c, _j)
    _c += _jobs * _per
    _j += _jobs
CHUNKS = _c


class Count:

    def __init__(self, sem):
        self.sem, self.base, self.n = sem, 0, 0

    def up(self, ins):
        ins.then_inc(self.sem, 1)
        self.n += 1

    def now(self, back=0):
        return self.base + (self.n - back)

    def enter(self, i, per):
        self.start, self.per = self.n, per
        self.base = i * per + self.start
        self.n = 0

    def leave(self, trips):
        assert self.n == self.per, (self.n, self.per)
        self.base, self.n = 0, self.start + trips * self.per


def trunk(nc, x, rows, rwkv_rows, lora, w, consts, ln_rows, y):
    with ExitStack() as ctx:
        def sem(name):
            return ctx.enter_context(nc.semaphore(name))

        def sb(name, shape, dt=F32, stack=ctx):
            return stack.enter_context(nc.sbuf_tensor(name, shape, dt))

        raw = sb("raw", [P, RING, KC, NB])
        whi = sb("whi", [P, RING, KC, NB], F32R)
        wlo = sb("wlo", [P, RING, KC, NB], F32R)
        ident = sb("ident", [P, P])
        mixT = sb("mixT", [P, 6 * KT])
        lnT = sb("lnT", [P, 2 * 2 * 2 * KT])
        stats = sb("stats", [P, TT, NJ, 6])
        mv = sb("mv", [P, TT, 2])
        var = sb("var", [P, TT])
        rstd = sb("rstd", [P, TT])
        small = sb("small", [P, 32])
        gsm = sb("gsm", [P, 5, 8])
        nsmall = sb("nsmall", [P, 48])
        with ExitStack() as early:
            a2t = sb("a2t", [P, 8192], stack=early)
        ahi = sb("ahi", [P, KT, T], F32R)
        alo = sb("alo", [P, KT, T], F32R)
        with ExitStack() as early:
            big = sb("big", [P, 124 * 256], stack=early)
        common = sb("common", [P, 36 * 256])
        hThi = sb("hThi", [P, FT, T], F32R)
        hTlo = sb("hTlo", [P, FT, T], F32R)
        ps = ctx.enter_context(nc.psum_tensor("ps", [P, 8, NB], F32))

        def carve(base, at, *shape):
            n = int(np.prod(shape))
            v = base[:, at:at + n]
            if len(shape) == 1:
                return v
            names = "abcd"[:len(shape)]
            return v.rearrange(f"p ({' '.join(names)}) -> p {' '.join(names)}", **{q: n for q, n in zip(names[:-1], shape[:-1])})

        KB = 256
        K_ = carve(big, 0, TT, D)
        L_ = carve(big, 16 * KB, TT, D)
        hw = carve(big, 32 * KB, T)
        ha = carve(big, 33 * KB, T)
        hg = carve(big, 34 * KB, 2, T)
        mtmp = carve(big, 36 * KB, 2, KC, T)
        R_ = carve(big, 40 * KB, TT, D)
        V_ = carve(big, 56 * KB, TT, D)
        A_ = carve(big, 72 * KB, TT, D)
        xT = carve(big, 88 * KB, KT, T + 1)
        xxT = carve(big, 88 * KB + KT * (T + 1), KT, T)
        rowsn = carve(big, 121 * KB, P)
        rowsl = carve(big, 122 * KB, P)
        xn = K_
        w1 = carve(big, 56 * KB, KT, LR)
        a1 = carve(big, 62 * KB, KT, LR)
        g1 = carve(big, 40 * KB, KT, LG)
        w2 = carve(big, 0, D)
        a2 = carve(big, 8 * KB, D)
        g2 = carve(big, 56 * KB, 2, D)
        places = [[a2t, 0, 8192], [big, 104 * KB, 124 * KB], [big, 36 * KB, 40 * KB], [big, 32 * KB, 34 * KB]]

        def tmp(*shape):
            n = int(np.prod(shape))
            place = next(p for p in places if p[1] + n <= p[2])
            place[1] += n
            return carve(place[0], place[1] - n, *shape)

        tri_i, tri_e, ind = tmp(P), tmp(P), tmp(2)
        mask_ar, mask_lv, mask_bd = tmp(2 * P), tmp(LEVELS, P), tmp(P)

        class Lane:

            def __init__(self, n):
                self.bank = 4 * n
                self.G = tmp(2, 2, 4, P)
                self.Z, self.XT = tmp(4, P), tmp(4, P)
                self.Ls, self.Vs = tmp(TT, P), tmp(TT, P)
                self.bh, self.kh = tmp(TT, P), tmp(TT, P)
                self.arT = tmp(TT, 2, P)
                self.bkT = tmp(2, 2, TT, P)
                PP = tmp(3, TT, P)
                self.Pi, self.Pn, self.Pe = (PP[:, n] for n in range(3))
                self.at, self.rt = self.Pe, self.Pi
                self.X = PP[:, 0:2].rearrange("p n t c -> p (n t) c")
                self.AV = self.Ls.rearrange("p t (b c) -> p (t b) c", c=CHUNK)
                self.U = self.Pi
                self.WT = self.Pn
                self.S = self.Z

        lanes = [Lane(0), Lane(1)]
        for ln in lanes:
            ln.PC = tmp(4)
        idle = tmp(5)
        par = tmp(2, 2 * P)
        y_sq = lanes[0].G[:, 0, 0].rearrange("p j c -> p (j c)").rearrange("p (t c) -> p t c", t=TT)
        KN_ = carve(big, 88 * KB, TT, D)
        bsum = sb("bsum", [P, TT, 2 * PAIRS])
        npar = [carve(big, (104 + 6 * n) * KB, 3, NB) for n in range(2)]
        ntmp = carve(big, 36 * KB, TT, NB)
        H = carve(common, 0, TT, D)
        Zn = carve(common, 16 * KB, TT, D)
        ltmp = carve(common, 32 * KB, 2, KC, T)
        gtmp = carve(common, 32 * KB, TT, NB)
        wb = carve(big, 40 * KB, 2, D)
        Kn = carve(big, 40 * KB, TT, D)
        Vn = carve(big, 56 * KB, TT, D)
        Qn = carve(big, 72 * KB, TT, D)
        Qs = carve(big, 88 * KB, TT, P)
        Ks = carve(big, 89 * KB, TT, P)
        Va = carve(big, 90 * KB, TT, P)
        QKT = carve(big, 91 * KB, 4, P)
        Sm = carve(big, 93 * KB, 3, P)
        Pr = carve(big, 95 * KB, 3, P)
        PT = carve(big, 97 * KB, 3, P)
        cap = carve(big, 99 * KB, 3, P)

        raw_landed = [sem(f"raw_landed{s}") for s in range(RING)]
        hi_done, split_done, chunk_used = sem("hi_done"), sem("split_done"), sem("chunk_used")
        bank_free = [sem("bank_free0"), sem("bank_free1")]
        x_in, rows_in, g1_in, wa1_in, wa2_in, id_in = (sem(n) for n in ("x_in", "rows_in", "g1_in", "wa1_in", "wa2_in", "id_in"))
        xt_made, xt_copied, xx_done, rows_made = (
            sem(n) for n in ("xt_made", "xt_copied", "xx_done", "rows_made"))
        lmix_done, lora1_made, lora1_copied, ones_set, lora2_made, lora2_copied = (
            sem(n) for n in ("lmix_done", "lora1_made", "lora1_copied", "ones_set", "lora2_made", "lora2_copied"))
        mix_done, mixhi_done, act_ready = sem("mix_done"), sem("mixhi_done"), sem("act_ready")
        dve_step, act_step = sem("dve_step"), sem("act_step")
        masks_in, g2_in, h0_in, wb_in, cap_in = (sem(n) for n in ("masks_in", "g2_in", "h0_in", "wb_in", "cap_in"))
        names = ("ls_set cum_made decay_done rt_done tr_made arT_set bkT_set g_made g_raw g_set z_made z_set x_made x_set "
                 "xt_made xt_set av_made av_set uh_made u_set wt_made wt_set pu_made ps_made s_set y_made y_set")
        lq = [{n: sem(f"lane{s}_{n}") for n in names.split()} for s in range(2)]
        par_in, zz_done, zeros_set, y_normed, pool_step = (sem(n) for n in ("par_in", "zz_done", "zeros_set", "y_normed", "pool_step"))
        npar_in, sq_asked, sq_done = [sem("npar_in0"), sem("npar_in1")], sem("sq_asked"), sem("sq_done")
        nk_done = sem("nk_done")
        gate_made, gated = sem("gate_made"), sem("gated")
        z_tr, z_tr_done = sem("z_tr"), sem("z_tr_done")
        xhat_done, ln_tr, ln_aff, ln_hi, h_done = (sem(n) for n in ("xhat_done", "ln_tr", "ln_aff", "ln_hi", "h_done"))
        h_tr, hhi_done, hlo_done = (sem(n) for n in ("h_tr", "hhi_done", "hlo_done"))
        anames = "qk_staged v_staged qk_tr qkt_set s_made s_capped nm_set p_set p_normed pt_made pt_set o_made ohi_set olo_set"
        t_ = {n: sem("t_" + n) for n in anames.split()}
        y_out = sem("y_out")

        block = ctx.enter_context(nc.Block())

        @block.sync
        def _(sp):
            def chunk(c, s, src):
                if not isinstance(c, int) or c >= RING:
                    sp.wait_ge(split_done, c - (RING - 1))
                sp.dma_start(raw[:, s], src.rearrange("(k p) n -> p k n", p=P)).then_inc(raw_landed[s], 16)

            def stream(c0, mats, kt, col):
                for n, m in enumerate(mats):
                    for j in range(kt // KC):
                        c = n * (kt // KC) + j
                        chunk(c0 + c, c % RING, m[j * KC * P:(j + 1) * KC * P, col])

            def blocks(c0, mats, kt, n):
                per = len(mats) * kt // KC
                if per % RING:
                    with sp.Fori(0, n // 2) as i:
                        for b in range(2):
                            for j in range(kt // KC):
                                c = b * (kt // KC) + j
                                chunk(i * (2 * per) + (c0 + c), c % RING,
                                      mats[0][j * KC * P:(j + 1) * KC * P, bass.ds(i * (2 * NB) + b * NB, NB)])
                else:
                    with sp.Fori(0, n) as i:
                        stream(i * per + c0, mats, kt, bass.ds(i * NB, NB))

            stream(0, [w["k"]], KT, slice(0, NB))
            for b in range(1, NJ):
                stream(b * CJ, [w["k"]], KT, slice(b * NB, (b + 1) * NB))
            blocks(PH["proj"][0] + NJ * CJ, [w["r"]], KT, NJ)
            blocks(PH["proj"][0] + 2 * NJ * CJ, [w["v"]], KT, NJ)
            blocks(PH["wo"][0], [w["o"]], KT, NJ)
            blocks(PH["up0"][0], [w["gate"][0], w["up"][0]], KT, FB)
            blocks(PH["down0"][0], [w["down"][0]], FT, NJ)
            for n, m in enumerate(("kv_k", "kv_v", "q")):
                blocks(PH["kvq"][0] + n * NJ * CJ, [w[m]], KT, NJ)
            blocks(PH["ao"][0], [w["ao"]], KT, NJ)
            blocks(PH["up1"][0], [w["gate"][1], w["up"][1]], KT, FB)
            blocks(PH["down1"][0], [w["down"][1]], FT, NJ)
            yv = y[0].rearrange("(t p) d -> p t d", p=P)
            for t in range(TT):
                sp.wait_ge(h_done, 3 * TT + t + 1)
                sp.dma_start(yv[:, t], H[:, t]).then_inc(y_out, 16)
            sp.wait_ge(y_out, 16 * TT)

        @block.gpsimd
        def _(pool):
            xv = x[0].rearrange("(t p) d -> p t d", p=P)
            nc.gpsimd.dma_start(ident[:], consts[:, C_ID:C_ID + P]).then_inc(id_in, 16)
            nc.gpsimd.dma_start(xn, xv).then_inc(x_in, 16)
            nc.gpsimd.dma_start(rowsn[0:6 * KT], rows).then_inc(rows_in, 16)
            nc.gpsimd.dma_start(rowsl, ln_rows.rearrange("a b n (k p) -> (a b n k) p", p=P)).then_inc(rows_in, 16)
            nc.gpsimd.dma_start(w1, lora["w1"].rearrange("(k p) n -> p k n", p=P)).then_inc(wa1_in, 16)
            nc.gpsimd.dma_start(a1, lora["a1"].rearrange("(k p) n -> p k n", p=P)).then_inc(wa1_in, 16)
            nc.gpsimd.dma_start(g1, lora["g1"].rearrange("(k p) n -> p k n", p=P)).then_inc(g1_in, 16)
            pool.wait_ge(xt_made, KT // KC)
            for dst, m, bias in ((w2, "w2", "w0"), (a2, "a2", "a0")):
                nc.gpsimd.dma_start(dst[0:LR], lora[m]).then_inc(wa2_in, 16)
                nc.gpsimd.dma_start(dst[LR:LR + 1], lora[bias]).then_inc(wa2_in, 16)
            pool.wait_ge(mix_done, 3 * (KT // KC))
            for n in range(NJ):
                if n >= 2:
                    pool.wait_ge(nk_done, n - 1)
                nc.gpsimd.dma_start(npar[n % 2], rwkv_rows[0:3, n * NB:(n + 1) * NB].partition_broadcast(P)).then_inc(npar_in[n % 2], 16)
            pool.wait_ge(chunk_used, 12 * CJ)
            nc.gpsimd.dma_start(a2t[:, 0:C_CAP - C_TI], consts[:, C_TI:C_CAP]).then_inc(masks_in, 16)

            def load_par(cs):
                nc.gpsimd.dma_start(par, rwkv_rows[3:5, cs].partition_broadcast(P)).then_inc(par_in, 16)

            pool.wait_ge(nk_done, NJ)
            load_par(slice(0, 2 * P))
            for s in range(2):
                nc.gpsimd.memset(lanes[s].bkT, 0.0).then_inc(zeros_set, 1)
            pstep = Count(pool_step)

            def finish(i):
                def wait_aside(k, ready, value):
                    pool.wait_ge(ready, value)
                    nc.gpsimd.tensor_tensor(idle[:, k:k + 1], idle[:, 0:1], idle[:, 0:1], ALU.mult)

                def then(k, ins):
                    pstep.up(ins)
                    wait_aside(k, pool_step, pstep.now())

                cs = bass.ds(i * (2 * P), 2 * P)
                yv, vv = R_[:, :, cs], V_[:, :, cs].rearrange("p t (h i) -> p t h i", i=HD)
                pool.wait_ge(lq[0]["y_set"], i + 1)
                wait_aside(1, lq[1]["y_set"], i + 1)
                nc.gpsimd.tensor_tensor(vv, vv, bsum[:, :, bass.ds(i * 4, 4)].unsqueeze(3).broadcast_to([P, TT, 4, HD]), ALU.mult)
                pool.wait_ge(par_in, i * 16 + 16)
                wait_aside(2, y_normed, i + 1)
                then(3, nc.gpsimd.tensor_tensor(yv, yv, par[:, 0].unsqueeze(1).broadcast_to([P, TT, 2 * P]), ALU.mult))
                then(4, nc.gpsimd.tensor_tensor(yv, yv, par[:, 1].unsqueeze(1).broadcast_to([P, TT, 2 * P]), ALU.add))
                nc.gpsimd.tensor_tensor(yv, yv, V_[:, :, cs], ALU.add).then_inc(zz_done, 1)

            def mask_products(i):
                for ln, q in zip(lanes, lq):
                    pool.wait_ge(q["g_raw"], i + 1)
                    for n, x in ((1, 0), (1, 1), (0, 1)):
                        m = ln.G[:, n, x]
                        last = nc.gpsimd.tensor_tensor(m, m, mask_ar[:, x * P:(x + 1) * P].unsqueeze(1).broadcast_to([P, 4, P]), ALU.mult)
                    last.then_inc(q["g_set"], 1)

            nc.gpsimd.memset(idle, 0.0).then_inc(zeros_set, 1)
            pool.wait_ge(zeros_set, 3)
            pool.wait_ge(masks_in, 16)
            mask_products(0)
            with pool.Fori(0, PAIRS // 2 - 1) as i:
                pstep.enter(i, 2)
                mask_products(i + 1)
                finish(i)
                pool.wait_ge(zz_done, i + 1)
                load_par(bass.ds(i * (2 * P) + 2 * P, 2 * P))
                pstep.leave(PAIRS // 2 - 1)
            finish(PAIRS // 2 - 1)
            pool.wait_ge(zz_done, PAIRS // 2)
            nc.gpsimd.dma_start(g2, lora["g2"].rearrange("(k p) n -> p k n", p=P)).then_inc(g2_in, 16)
            nc.gpsimd.dma_start(H, xv).then_inc(h0_in, 16)
            lnw = lambda n: ln_rows[n // 2, n % 2].partition_broadcast(P)

            def load_wb(n, ready, value):
                pool.wait_ge(ready, value)
                nc.gpsimd.dma_start(wb, lnw(n)).then_inc(wb_in, 16)
            load_wb(0, z_tr, KT // KC)
            load_wb(1, chunk_used, PH["kvq"][0])
            nc.gpsimd.dma_start(cap, consts[:, C_CAP:C_END].rearrange("p (a b) -> p a b", a=3)).then_inc(cap_in, 16)
            load_wb(2, t_["qk_staged"], HEADS)
            load_wb(3, chunk_used, CHUNKS)

        @block.tensor
        def _(pe):
            mm, tr = nc.tensor.matmul, nc.tensor.transpose

            def job(c, u, parity, kt, hi, lo):
                pe.wait_ge(bank_free[parity], u + 1)
                for ch in range(kt // KC):
                    s = (ch + (CF * parity if kt == FT else 0)) % RING
                    pe.wait_ge(split_done, c + (ch + 1))
                    for k2 in range(KC):
                        k = ch * KC + k2
                        for t in range(TT):
                            o, tok = ps[:, 2 * parity + t, :], slice(t * P, (t + 1) * P)
                            mm(o, hi[:, k, tok], whi[:, s, k2, :], start=(k == 0), stop=False)
                            mm(o, hi[:, k, tok], wlo[:, s, k2, :], start=False, stop=False)
                            last = mm(o, lo[:, k, tok], whi[:, s, k2, :], start=False, stop=(k == kt - 1))
                    last.then_inc(chunk_used, 1)

            def jobs(c0, j0, n, kt, hi, lo):
                per = kt // KC
                with pe.Fori(0, n // 2) as i:
                    for b in range(2):
                        job(i * (2 * per) + (c0 + b * per), i + j0 // 2, b, kt, hi, lo)

            pe.wait_ge(id_in, 16)
            pe.wait_ge(x_in, 16)
            for g in range(KT // KC):
                if g >= 4:
                    pe.wait_ge(xt_copied, g - 3)
                for k2 in range(KC):
                    for t in range(TT):
                        k = g * KC + k2
                        last = tr(ps[:, 4 + g % 4, k2 * T + t * P:k2 * T + (t + 1) * P], xn[:, t, k * P:(k + 1) * P], ident[:])
                last.then_inc(xt_made, 1)
            pe.wait_ge(rows_in, 32)
            tr(ps[:, 0, 0:6 * KT], rowsn[0:6 * KT], ident[0:6 * KT, 0:6 * KT]).then_inc(rows_made, 1)
            tr(ps[:, 2, 0:P], rowsl, ident[:]).then_inc(rows_made, 1)
            pe.wait_ge(xt_copied, KT // KC)
            pe.wait_ge(wa1_in, 32)
            for n, (m, buf) in enumerate(((w1, L_), (a1, A_))):
                mx = buf.rearrange("p t (k n) -> p (t k) n", n=T)
                for k in range(KT):
                    pe.wait_ge(lmix_done, n * KT + k + 1)
                    last = mm(ps[0:LR, 4 + n, 0:T], m[:, k, :], mx[:, k, :], start=(k == 0), stop=(k == KT - 1))
                last.then_inc(lora1_made, 1)
            pe.wait_ge(g1_in, 16)
            mx = L_.rearrange("p t (k n) -> p (t k) n", n=T)
            for k in range(KT):
                pe.wait_ge(lmix_done, 2 * KT + k + 1)
                for m in range(2):
                    last = mm(ps[:, 6 + m, 0:T], g1[:, k, m * P:(m + 1) * P], mx[:, k, :], start=(k == 0), stop=(k == KT - 1))
            last.then_inc(lora1_made, 1)
            pe.wait_ge(wa2_in, 64)
            pe.wait_ge(ones_set, 2)
            pe.wait_ge(lora1_copied, 4)
            for n in range(2 * NJ):
                if n >= 2:
                    pe.wait_ge(lora2_copied, n - 1)
                h, m = ((hw, w2), (ha, a2))[n // NJ]
                for t in range(TT):
                    last = mm(ps[:, 4 + 2 * (n % 2) + t, :], h[0:LR + 1, t * P:(t + 1) * P],
                              m[0:LR + 1, (n % NJ) * NB:(n % NJ + 1) * NB], start=True, stop=True)
                last.then_inc(lora2_made, 1)
            for n in range(3):
                pe.wait_ge(act_ready, (n + 1) * KT // KC)
                jobs(n * NJ * CJ, n * NJ, NJ, KT, ahi, alo)
            for b in range(2):
                pe.wait_ge(bank_free[b], 7)

            def rows_of(c):
                return c // 2, slice((c % 2) * CHUNK, (c % 2 + 1) * CHUNK)

            def blocks(out, lhs, rhs, **kw):
                for j in range(4):
                    last = mm(out(j), lhs(j), rhs(j), start=True, stop=True)
                return last

            def recur(i):
                one = i + 1
                both = [(lanes[s], lq[s], lanes[s].bank) for s in range(2)]

                def v_of(m):
                    return lambda j: m[:, j % 2, (j // 2) * HD:(j // 2 + 1) * HD]

                for ln, q, b in both:
                    pe.wait_ge(q["ls_set"], one)
                    flat = ln.Ls.rearrange("p t c -> p (t c)")
                    mm(ps[:, b, 0:T], tri_i, flat, start=True, stop=True)
                    mm(ps[:, b, T:2 * T], tri_e, flat, start=True, stop=True)
                    for t in range(TT):
                        last = mm(ps[:, b + 1, 2 * t:2 * t + 2], ln.Ls[:, t, :], ind, start=True, stop=True)
                    last.then_inc(q["cum_made"], 1)
                for ln, q, b in both:
                    pe.wait_ge(q["rt_done"], one)
                    for t in range(TT):
                        for n, src in enumerate((ln.at, ln.rt)):
                            tr(ps[:, b + 2, (t * 2 + n) * P:(t * 2 + n + 1) * P], src[:, t, :], ident[:])
                    for n, src in enumerate((ln.bh, ln.kh)):
                        for t in range(TT):
                            last = tr(ps[:, b + 3, (n * TT + t) * P:(n * TT + t + 1) * P], src[:, t, :], ident[:])
                    last.then_inc(q["tr_made"], 1)
                for ln, q, b in both:
                    pe.wait_ge(q["arT_set"], one)
                    pe.wait_ge(q["bkT_set"], one)
                    for n, x in ((0, 0), (0, 1), (1, 0), (1, 1)):
                        last = blocks(lambda j: ps[:, b + 2 * n + x, j * P:(j + 1) * P], lambda j: ln.bkT[:, n, j // 2, j % 2, :],
                                      lambda j: ln.arT[:, j % 2, x, :])
                        if n == x:
                            last.then_inc(q["g_made"], 1)
                for l in range(1, LEVELS):
                    for ln, q, b in both:
                        pe.wait_ge(q["xt_set"], i * LEVELS + l)
                        if l == 1:
                            pe.wait_ge(q["g_raw"], one)
                        for j in range(4):
                            last = tr(ps[:, b + 1, j * P:(j + 1) * P], ln.XT[:, j, :], ident[:])
                        last.then_inc(q["x_made"], 1)
                    if l == 4:
                        for ln, q, b in both:
                            pe.wait_ge(q["g_set"], one)
                            blocks(lambda j: ps[:, b + 2, j * HD:(j + 1) * HD], lambda j: ln.G[:, 1, 0, j, :], v_of(ln.Vs)).then_inc(q["av_made"], 1)
                    for ln, q, b in both:
                        pe.wait_ge(q["x_set"], i * (LEVELS - 1) + l)
                        blocks(lambda j: ps[:, b, j * P:(j + 1) * P], lambda j: ln.G[:, 0, 0, j, :], lambda j: ln.X[:, j, :]).then_inc(q["z_made"], 1)
                    for ln, q, b in both:
                        pe.wait_ge(q["z_set"], i * (LEVELS - 1) + l)
                        blocks(lambda j: ps[:, b + 3, j * P:(j + 1) * P], lambda j: ln.Z[:, j, :], lambda j: ln.XT[:, j, :]).then_inc(q["xt_made"], 1)
                for ln, q, b in both:
                    pe.wait_ge(q["xt_set"], one * LEVELS)
                    for t in range(TT):
                        for h in range(2):
                            last = mm(ps[h * HD:(h + 1) * HD, b + 1, t * P:(t + 1) * P], ln.at[:, t, h * HD:(h + 1) * HD],
                                      ln.XT[:, 2 * h + t, :], start=True, stop=True)
                    last.then_inc(q["wt_made"], 1)
                    pe.wait_ge(q["av_set"], one)
                    blocks(lambda j: v_of(ps[:, b + 2, T:2 * T].rearrange("p (t c) -> p t c", t=TT))(j), lambda j: ln.XT[:, j, :],
                           lambda j: ln.AV[:, j, :]).then_inc(q["uh_made"], 1)

                def y_part(ln, b, n, rhs, j, **kw):
                    t, hh = j % 2, slice((j // 2) * HD, (j // 2 + 1) * HD)
                    return mm(ps[:, b + 3, t * P + hh.start:t * P + hh.stop], ln.G[:, n, 1, j, :], rhs[:, t, hh], skip_group_check=True, **kw)

                for ln, q, b in both:
                    for j in range(4):
                        y_part(ln, b, 1, ln.Vs, j, start=(j == 0), stop=False)
                for c in range(4):
                    t, rc = rows_of(c)
                    for ln, q, b in both:
                        if c == 0:
                            pe.wait_ge(q["wt_set"], one)
                            continue
                        pe.wait_ge(q["s_set"], i * 3 + c)
                        mm(ps[rc, b, 0:P], ln.WT[:, t, rc], ln.S[:, c - 1, :], start=True, stop=True).then_inc(q["pu_made"], 1)
                    for ln, q, b in both:
                        if c:
                            if c < 3:
                                mm(ps[:, b + 2, 0:P], ident[:], ln.S[:, c - 1, :], start=True, stop=False)
                                mm(ps[:, b + 2, 0:P], ln.kh[rc, t, :], ln.Vs[rc, t, :], start=False, stop=False)
                            mm(ps[rc, b + 3, t * P:(t + 1) * P], ln.arT[:, t, 1, rc], ln.S[:, c - 1, :],
                               start=False, stop=False, skip_group_check=True)
                    for ln, q, b in both:
                        pe.wait_ge(q["u_set"], i * 4 + (c + 1))
                        if c == 0:
                            mm(ps[:, b + 2, 0:P], ln.kh[rc, t, :], ln.Vs[rc, t, :], start=True, stop=False)
                        if c < 3:
                            mm(ps[:, b + 2, 0:P], ln.bh[rc, t, :], ln.U[rc, t, :], start=False, stop=True).then_inc(q["ps_made"], 1)
                    if c % 2:
                        for ln, q, b in both:
                            y_part(ln, b, 0, ln.U, t, start=False, stop=False)
                            last = y_part(ln, b, 0, ln.U, 2 + t, start=False, stop=(c == 3))
                            if c == 3:
                                last.then_inc(q["y_made"], 1)

            pe.wait_ge(masks_in, 16)
            with pe.Fori(0, PAIRS // 2) as i:
                recur(i)

            pe.wait_ge(g2_in, 16)
            for s in range(2):
                pe.wait_ge(lq[s]["y_set"], PAIRS // 2)
            for n in range(NJ):
                if n >= 2:
                    pe.wait_ge(gated, n - 1)
                for t in range(TT):
                    for k in range(2):
                        last = mm(ps[:, 4 + 2 * (n % 2) + t, :], hg[:, k, t * P:(t + 1) * P], g2[:, k, n * NB:(n + 1) * NB], start=(k == 0), stop=(k == 1))
                last.then_inc(gate_made, 1)

            def transpose_act(src, made, made0, done, done0, first_wait):
                first_wait()
                for g in range(KT // KC):
                    if g >= 4:
                        pe.wait_ge(done, done0 + g - 3)
                    for k2 in range(KC):
                        for t in range(TT):
                            k = g * KC + k2
                            last = tr(ps[:, 4 + g % 4, k2 * T + t * P:k2 * T + (t + 1) * P], src[:, t, k * P:(k + 1) * P], ident[:])
                    last.then_inc(made, 1)

            transpose_act(R_, z_tr, 0, z_tr_done, 0, lambda: pe.wait_ge(gated, NJ))
            pe.wait_ge(z_tr_done, KT // KC)
            jobs(*PH["wo"], NJ, KT, ahi, alo)

            def norm_transposes(n):
                transpose_act(Zn, ln_tr, 0, ln_hi, n * KT // KC, lambda: pe.wait_ge(xhat_done, (n + 1) * TT))
                pe.wait_ge(ln_hi, (n + 1) * KT // KC)

            def ffn(layer):
                c0, j0 = PH[f"up{layer}"]
                u0 = layer * FB

                def h_transposes(i):
                    pe.wait_ge(bank_free[1], i + (j0 // 2 + 2 - u0))
                    for f in range(4):
                        for t in range(TT):
                            last = tr(ps[:, 4 + f // 2, (f % 2) * T + t * P:(f % 2) * T + (t + 1) * P], gtmp[:, t, f * P:(f + 1) * P], ident[:])
                    last.then_inc(h_tr, 1)

                job(c0, j0 // 2, 0, KT, ahi, alo)
                job(c0 + CJ, j0 // 2, 1, KT, ahi, alo)
                with pe.Fori(0, FB - 1) as i:
                    job(i * (2 * CJ) + (c0 + 2 * CJ), i + (j0 // 2 + 1), 0, KT, ahi, alo)
                    h_transposes(i + u0)
                    job(i * (2 * CJ) + (c0 + 3 * CJ), i + (j0 // 2 + 1), 1, KT, ahi, alo)
                    pe.wait_ge(hlo_done, i + (u0 + 1))
                h_transposes(u0 + FB - 1)
                pe.wait_ge(hlo_done, u0 + FB)
                jobs(*PH[f"down{layer}"], NJ, FT, hThi, hTlo)

            norm_transposes(0)
            ffn(0)
            norm_transposes(1)
            jobs(*PH["kvq"], 12, KT, ahi, alo)
            for b in range(2):
                pe.wait_ge(bank_free[b], PH["ao"][1] // 2 + 1)
            pe.wait_ge(cap_in, 16)
            with pe.Fori(0, HEADS) as h:
                one = h + 1
                pe.wait_ge(t_["qk_staged"], one)
                for i in range(4):
                    src = (Qs, Ks)[i // 2]
                    last = tr(ps[:, 4, i * P:(i + 1) * P], src[:, i % 2, :], ident[:])
                last.then_inc(t_["qk_tr"], 1)
                pe.wait_ge(t_["qkt_set"], one)
                mm(ps[:, 5, 0:P], QKT[:, 0, :], QKT[:, 2, :], start=True, stop=True)
                mm(ps[:, 5, P:3 * P], QKT[:, 1, :], QKT[:, 2:4, :].rearrange("p a b -> p (a b)"), start=True, stop=True).then_inc(t_["s_made"], 1)
                pe.wait_ge(t_["p_normed"], one)
                for i in range(3):
                    last = tr(ps[:, 6, i * P:(i + 1) * P], Pr[:, i, :], ident[:])
                last.then_inc(t_["pt_made"], 1)
                pe.wait_ge(t_["pt_set"], one)
                pe.wait_ge(t_["v_staged"], one)
                mm(ps[:, 7, 0:T], Va[:, 0, :], PT[:, 0:2, :].rearrange("p a b -> p (a b)"), start=True, stop=False, skip_group_check=True)
                mm(ps[:, 7, P:T], Va[:, 1, :], PT[:, 2, :], start=False, stop=True, skip_group_check=True).then_inc(t_["o_made"], 1)
            pe.wait_ge(t_["olo_set"], HEADS)
            jobs(*PH["ao"], NJ, KT, ahi, alo)
            norm_transposes(2)
            ffn(1)

        @block.scalar
        def _(act):
            A = nc.scalar.activation

            def split_hi(c, u, n):
                for ch in range(n):
                    s = ch % RING
                    act.wait_ge(raw_landed[s], (u + ch // RING + 1) * 16)
                    if not isinstance(c, int) or c + ch >= RING:
                        act.wait_ge(chunk_used, c + (ch - RING + 1))
                    nc.scalar.copy(whi[:, s], raw[:, s]).then_inc(hi_done, 1)

            for g in range(KT // KC):
                act.wait_ge(xt_made, g + 1)
                nc.scalar.copy(xT[:, g * KC:(g + 1) * KC, 1:T + 1], ps[:, 4 + g % 4, :].rearrange("p (k t) -> p k t", k=KC)).then_inc(xt_copied, 1)
            act.wait_ge(rows_made, 2)
            nc.scalar.copy(mixT[:], ps[:, 0, 0:6 * KT]).then_inc(bank_free[0], 1)
            nc.scalar.copy(lnT[:], ps[:, 2, 0:P]).then_inc(bank_free[1], 1)
            split_hi(0, 0, RING)
            act.wait_ge(lora1_made, 1)
            A(hw[0:LR], ps[0:LR, 4, 0:T], ACT.Tanh).then_inc(lora1_copied, 1)
            act.wait_ge(lora1_made, 2)
            nc.scalar.copy(ha[0:LR], ps[0:LR, 5, 0:T]).then_inc(lora1_copied, 1)
            act.wait_ge(lora1_made, 3)
            for m in range(2):
                A(hg[:, m], ps[:, 6 + m, 0:T], ACT.Sigmoid).then_inc(lora1_copied, 1)
            for n in range(2 * NJ):
                act.wait_ge(lora2_made, n + 1)
                dst = (L_, A_)[n // NJ][:, :, (n % NJ) * NB:(n % NJ + 1) * NB]
                A(dst, ps[:, 4 + 2 * (n % 2):6 + 2 * (n % 2), :], ACT.Sigmoid).then_inc(lora2_copied, 1)

            def project(c0, n, dst):
                with act.Fori(0, n // 2) as i:
                    for b in range(2):
                        split_hi(i * (2 * CJ) + (c0 + b * CJ + RING), i * (2 * CJ // RING) + (c0 + b * CJ + RING) // RING, CJ)
                        act.wait_ge(chunk_used, i * (2 * CJ) + (c0 + (b + 1) * CJ))
                        nc.scalar.copy(dst[:, :, bass.ds(i * (2 * NB) + b * NB, NB)], ps[:, 2 * b:2 * b + 2, :]).then_inc(bank_free[b], 1)

            def project_v(c0):
                for b in range(NJ):
                    c = c0 + b * CJ + RING
                    split_hi(c, c // RING, RING)
                    act.wait_ge(sq_asked, b + 1)
                    A(ntmp, KN_[:, :, b * NB:(b + 1) * NB], ACT.Square).then_inc(sq_done, 1)
                    split_hi(c + RING, c // RING + 1, RING)
                    act.wait_ge(chunk_used, c0 + (b + 1) * CJ)
                    nc.scalar.copy(V_[:, :, b * NB:(b + 1) * NB], ps[:, 2 * (b % 2):2 * (b % 2) + 2, :]).then_inc(bank_free[b % 2], 1)

            for n, dst in enumerate((K_, R_, V_)):
                for g in range(KT // KC):
                    act.wait_ge(mix_done, n * (KT // KC) + g + 1)
                    nc.scalar.copy(ahi[:, g * KC:(g + 1) * KC], mtmp[:, g % 2]).then_inc(mixhi_done, 1)
                if n < 2:
                    project(n * NJ * CJ, NJ, dst)
                else:
                    project_v(n * NJ * CJ)
            act.wait_ge(bank_free[0], 7)
            act.wait_ge(bank_free[1], 7)
            act.wait_ge(nk_done, NJ)

            def recur(i):
                one = i + 1
                both = [(lanes[s], lq[s], lanes[s].bank) for s in range(2)]
                for s, (ln, q, b) in enumerate(both):
                    cs = bass.ds(i * (2 * P) + s * P, P)
                    nc.scalar.copy(ln.Ls, L_[:, :, cs]).then_inc(q["ls_set"], 1)
                for s, (ln, q, b) in enumerate(both):
                    nc.scalar.copy(ln.Vs, V_[:, :, bass.ds(i * (2 * P) + s * P, P)])
                for ln, q, b in both:
                    act.wait_ge(q["cum_made"], one)
                    ci = ps[:, b, 0:T].rearrange("p (t c) -> p t c", t=TT)
                    A(ln.Pi, ci, ACT.Exp)
                    A(ln.Pn, ci, ACT.Exp, scale=-1.0)
                    A(ln.Pe, ps[:, b, T:2 * T].rearrange("p (t c) -> p t c", t=TT), ACT.Exp)
                    A(ln.PC, ps[:, b + 1, 0:4], ACT.Exp).then_inc(q["decay_done"], 1)
                for ln, q, b in both:
                    act.wait_ge(q["tr_made"], one)
                    nc.scalar.copy(ln.arT, ps[:, b + 2, :].rearrange("p (t a b) -> p t a b", t=TT, a=2)).then_inc(q["arT_set"], 1)
                    for h in range(2):
                        hh = slice(h * HD, (h + 1) * HD)
                        last = nc.scalar.copy(ln.bkT[hh, :, h], ps[hh, b + 3, :].rearrange("p (a t b) -> p a t b", a=2, t=TT))
                    last.then_inc(q["bkT_set"], 1)
                for ln, q, b in both:
                    act.wait_ge(q["g_made"], one * 2)
                    for n, x in ((0, 1), (1, 0), (1, 1)):
                        last = nc.scalar.copy(ln.G[:, n, x], ps[:, b + 2 * n + x, :].rearrange("p (j c) -> p j c", j=4))
                    last.then_inc(q["g_raw"], 1)
                for l in range(1, LEVELS):
                    if l == 4:
                        for ln, q, b in both:
                            act.wait_ge(q["av_made"], one)
                            nc.scalar.copy(ln.AV, ps[:, b + 2, 0:T].rearrange("p (a b) -> p a b", a=4)).then_inc(q["av_set"], 1)
                    for ln, q, b in both:
                        act.wait_ge(q["xt_made"], i * (LEVELS - 1) + l)
                        nc.scalar.copy(ln.XT, ps[:, b + 3, :].rearrange("p (a b) -> p a b", a=4)).then_inc(q["xt_set"], 1)
                for ln, q, b in both:
                    act.wait_ge(q["wt_made"], one)
                    nc.scalar.copy(ln.WT, ps[:, b + 1, 0:T].rearrange("p (t b) -> p t b", t=TT)).then_inc(q["wt_set"], 1)
                for s, (ln, q, b) in enumerate(both):
                    act.wait_ge(q["y_made"], one)
                    nc.scalar.copy(R_[:, :, bass.ds(i * (2 * P) + s * P, P)],
                                   ps[:, b + 3, 0:T].rearrange("p (t b) -> p t b", t=TT)).then_inc(q["y_set"], 1)

            act.wait_ge(zeros_set, 2)
            with act.Fori(0, PAIRS // 2) as i:
                recur(i)

            for g in range(KT // KC):
                act.wait_ge(z_tr, g + 1)
                nc.scalar.copy(ahi[:, g * KC:(g + 1) * KC], ps[:, 4 + g % 4, :].rearrange("p (k t) -> p k t", k=KC)).then_inc(mixhi_done, 1)

            def quiet_jobs(c0, n, kt, last=False):
                per = kt // KC
                rounds = n // 2 - (1 if last else 0)
                if rounds:
                    with act.Fori(0, rounds) as i:
                        split_hi(i * (2 * per) + (c0 + RING), i * (2 * per // RING) + (c0 + RING) // RING, 2 * per)
                if last:
                    c = c0 + rounds * 2 * per + RING
                    split_hi(c, c // RING, 2 * per - RING)

            def norm_affine(n):
                for g in range(KT // KC):
                    act.wait_ge(ln_tr, n * (KT // KC) + g + 1)
                    if g >= 2 or n:
                        act.wait_ge(ln_hi, n * (KT // KC) + g - 1)
                    for k2 in range(KC):
                        k = g * KC + k2
                        ins = A(ltmp[:, g % 2, k2], ps[:, 4 + g % 4, k2 * T:(k2 + 1) * T], ACT.Identity,
                                scale=lnT[:, (n * 2) * KT + k:(n * 2) * KT + k + 1],
                                bias=lnT[:, (n * 2 + 1) * KT + k:(n * 2 + 1) * KT + k + 1])
                    ins.then_inc(ln_aff, 1)

            def ffn(layer):
                c0, _ = PH[f"up{layer}"]
                u0 = layer * FB

                def hidden_hi(i, f0):
                    act.wait_ge(h_tr, i + 1)
                    A(hThi[:, f0, :], ps[:, 4:6, :].rearrange("p a (k t) -> p (a k) t", k=2), ACT.Copy).then_inc(hhi_done, 1)

                split_hi(c0 + RING, c0 // RING + 1, CJ)
                act.wait_ge(chunk_used, c0 + CJ)
                A(gtmp, ps[:, 0:2, :], ACT.Silu).then_inc(bank_free[0], 1)
                split_hi(c0 + RING + CJ, c0 // RING + 1 + CJ // RING, CJ)
                act.wait_ge(h_done, (1 if layer == 0 else 3) * TT)
                with act.Fori(0, FB - 1) as i:
                    c = i * (2 * CJ) + (c0 + 2 * CJ)
                    u = i * (2 * CJ // RING) + (c0 + 2 * CJ) // RING
                    split_hi(c + RING, u + 1, CJ)
                    act.wait_ge(h_tr, i + (u0 + 1))
                    act.wait_ge(chunk_used, c + CJ)
                    A(gtmp, ps[:, 0:2, :], ACT.Silu).then_inc(bank_free[0], 1)
                    hidden_hi(i + u0, bass.ds(i * 4, 4))
                    split_hi(c + (RING + CJ), u + (1 + CJ // RING), CJ)
                hidden_hi(u0 + FB - 1, slice((FB - 1) * 4, FB * 4))
                quiet_jobs(PH[f"down{layer}"][0], NJ, FT, last=(layer == 1))

            quiet_jobs(PH["wo"][0], NJ, KT)
            norm_affine(0)
            ffn(0)
            norm_affine(1)
            act.wait_ge(h_done, 2 * TT)
            for n, dst in enumerate((Kn, Vn, Qn)):
                project(PH["kvq"][0] + n * NJ * CJ, NJ, dst)
            act.wait_ge(bank_free[0], PH["ao"][1] // 2 + 1)
            act.wait_ge(bank_free[1], PH["ao"][1] // 2 + 1)
            with act.Fori(0, HEADS) as h:
                one = h + 1
                nc.scalar.copy(Qs, Qn[:, :, bass.ds(h * P, P)])
                nc.scalar.copy(Ks, Kn[:, :, bass.ds(h * P, P)]).then_inc(t_["qk_staged"], 1)
                act.wait_ge(t_["qk_tr"], one)
                nc.scalar.copy(QKT, ps[:, 4, :].rearrange("p (a b) -> p a b", a=4)).then_inc(t_["qkt_set"], 1)
                act.wait_ge(t_["nm_set"], one)
                A(Pr[:, 0, :], Sm[:, 0, :], ACT.Exp, bias=small[:, 2:3], scale=SCALE, accum_out=small[:, 4:5])
                A(Pr[:, 1:3, :], Sm[:, 1:3, :], ACT.Exp, bias=small[:, 3:4], scale=SCALE, accum_out=small[:, 5:6]).then_inc(t_["p_set"], 1)
                act.wait_ge(t_["pt_made"], one)
                nc.scalar.copy(PT, ps[:, 6, 0:3 * P].rearrange("p (a b) -> p a b", a=3)).then_inc(t_["pt_set"], 1)
                act.wait_ge(t_["o_made"], one)
                A(ahi[:, bass.ds(h, 1), :], ps[:, 7, 0:T].unsqueeze(1), ACT.Copy).then_inc(t_["ohi_set"], 1)
            quiet_jobs(PH["ao"][0], NJ, KT)
            norm_affine(2)
            ffn(1)

        @block.vector
        def _(dve):
            V = nc.vector
            step = Count(dve_step)

            def then(ins):
                step.up(ins)
                dve.wait_ge(dve_step, step.now())

            def rsqrt_seed(dst, src, t):
                I32 = mybir.dt.int32
                then(V.tensor_scalar(t.bitcast(I32), src.bitcast(I32), 1, None, ALU.logical_shift_right))
                then(V.tensor_scalar(dst.bitcast(I32), t.bitcast(I32), -1.0, float(0x5F3759DF), ALU.mult, ALU.add))

            def newton(dst, src, t):
                then(V.tensor_tensor(t, dst, dst, ALU.mult))
                then(V.scalar_tensor_tensor(out=t, in0=t, scalar=-0.5, in1=src, op0=ALU.mult, op1=ALU.mult))
                then(V.scalar_tensor_tensor(out=dst, in0=t, scalar=1.5, in1=dst, op0=ALU.add, op1=ALU.mult))

            def rsqrt(dst, src, t):
                rsqrt_seed(dst, src, t)
                for _ in range(3):
                    newton(dst, src, t)

            def split_lo(c, n, s0=0):
                for ch in range(n):
                    s = (s0 + ch) % RING
                    dve.wait_ge(hi_done, c + (ch + 1))
                    V.tensor_tensor(wlo[:, s], raw[:, s], whi[:, s].bitcast(F32), ALU.subtract).then_inc(split_done, 1)

            then(V.memset(xT[:, :, 0:1], 0.0))
            V.memset(hw[LR:LR + 1], 1.0).then_inc(ones_set, 1)
            V.memset(ha[LR:LR + 1], 1.0).then_inc(ones_set, 1)
            for g in range(KT // KC):
                dve.wait_ge(xt_copied, g + 1)
                k = slice(g * KC, (g + 1) * KC)
                V.tensor_tensor(xxT[:, k], xT[:, k, 0:T], xT[:, k, 1:T + 1], ALU.subtract).then_inc(xx_done, 1)
            dve.wait_ge(xx_done, KT // KC)
            dve.wait_ge(bank_free[0], 1)

            def mixed(out, m, k):
                return V.scalar_tensor_tensor(out=out, in0=xxT[:, k], scalar=mixT[:, m * KT + k:m * KT + k + 1], in1=xT[:, k, 1:T + 1],
                                              op0=ALU.mult, op1=ALU.add)

            for n, (m, buf) in enumerate(((1, L_), (4, A_), (5, L_))):
                mx = buf.rearrange("p t (k n) -> p (t k) n", n=T)
                if n == 2:
                    dve.wait_ge(lora1_made, 1)
                for k in range(KT):
                    mixed(mx[:, k], m, k).then_inc(lmix_done, 1)
            split_lo(0, RING)

            def mix_split(n, m):
                for g in range(KT // KC):
                    if g >= 2 or n:
                        dve.wait_ge(act_ready, n * (KT // KC) + g - 1)
                    if g == 0 and n:
                        dve.wait_ge(chunk_used, n * NJ * CJ)
                    for k2 in range(KC):
                        ins = mixed(mtmp[:, g % 2, k2], m, g * KC + k2)
                    ins.then_inc(mix_done, 1)
                    if g:
                        tail(n, g - 1)
                tail(n, KT // KC - 1)

            def tail(n, g):
                dve.wait_ge(mixhi_done, n * (KT // KC) + g + 1)
                V.tensor_tensor(alo[:, g * KC:(g + 1) * KC], mtmp[:, g % 2], ahi[:, g * KC:(g + 1) * KC].bitcast(F32),
                                ALU.subtract).then_inc(act_ready, 1)

            def quiet(c0, n, kt=KT, last=False):
                per = kt // KC
                with dve.Fori(0, n // 2) as i:
                    split_lo(i * (2 * per) + (c0 + RING), 2 * per)

            for n, m in enumerate((2, 0)):
                mix_split(n, m)
                quiet(n * NJ * CJ, NJ)
            mix_split(2, 3)

            def normalise(n, part):
                cs = slice(n * NB, (n + 1) * NB)
                hs = slice(n * 8, (n + 1) * 8)
                kn, b_, k_, r_ = (m[:, :, cs] for m in (KN_, A_, K_, R_))
                k_k, k_a, r_k = (bcast_row(npar[n % 2][:, j, :]) for j in range(3))
                nr = [nsmall[:, 16 * j:16 * (j + 1)] for j in range(3)]

                def by_head(m, v, op):
                    for t in range(TT):
                        last = V.tensor_tensor(m[:, t].rearrange("p (h i) -> p h i", i=HD), m[:, t].rearrange("p (h i) -> p h i", i=HD),
                                               v[:, 8 * t:8 * (t + 1)].unsqueeze(2).broadcast_to([P, 8, HD]), op)
                    return last

                if part == 0:
                    dve.wait_ge(npar_in[n % 2], 16 * (n // 2 + 1))
                    V.tensor_tensor(kn, k_, k_k, ALU.mult).then_inc(sq_asked, 1)
                elif part == 1:
                    dve.wait_ge(sq_done, n + 1)
                    for t in range(TT):
                        last = V.tensor_reduce(nr[0][:, 8 * t:8 * (t + 1)], ntmp[:, t].rearrange("p (h i) -> p h i", i=HD), AX.X, ALU.add)
                    then(last)
                    then(V.tensor_scalar(nr[0], nr[0], 1e-24, None, ALU.max))
                    rsqrt(nr[1], nr[0], nr[2])
                    then(V.scalar_tensor_tensor(out=ntmp, in0=b_, scalar=1.0, in1=k_a, op0=ALU.subtract, op1=ALU.mult))
                    then(V.scalar_tensor_tensor(out=k_, in0=ntmp, scalar=1.0, in1=k_, op0=ALU.add, op1=ALU.mult))
                elif part == 2:
                    then(by_head(kn, nr[1], ALU.mult))
                    V.tensor_tensor(b_, kn, b_, ALU.mult)
                    then(V.tensor_tensor(ntmp, k_, r_k, ALU.mult))
                else:
                    then(V.tensor_tensor(ntmp, ntmp, r_, ALU.mult))
                    for t in range(TT):
                        last = V.tensor_reduce(bsum[:, t, hs], ntmp[:, t].rearrange("p (h i) -> p h i", i=HD), AX.X, ALU.add)
                    last.then_inc(nk_done, 1)
                    dve.wait_ge(nk_done, n + 1)

            def bcast_row(v):
                return v.unsqueeze(1).broadcast_to([P, TT, v.shape[-1]])

            for b in range(2):
                dve.wait_ge(bank_free[b], 5)
            for n in range(NJ):
                for part in range(4):
                    split_lo(2 * NJ * CJ + n * CJ + RING + 2 * part, 2, 2 * part % RING)
                    normalise(n, part)

            dve.wait_ge(masks_in, 16)

            def recur(i):
                one = i + 1
                both = [(lanes[s], lq[s], lanes[s].bank) for s in range(2)]
                if not isinstance(i, int):
                    group_norm(i - 1)
                for s, (ln, q, b) in enumerate(both):
                    cs = bass.ds(i * (2 * P) + s * P, P)
                    dve.wait_ge(q["decay_done"], one)
                    V.scalar_tensor_tensor(out=ln.at, in0=KN_[:, :, cs], scalar=-1.0, in1=ln.Pe, op0=ALU.mult, op1=ALU.mult)
                    V.tensor_tensor(ln.bh, A_[:, :, cs], ln.Pn, ALU.mult)
                    V.tensor_tensor(ln.kh, K_[:, :, cs], ln.Pn, ALU.mult)
                    V.tensor_tensor(ln.rt, R_[:, :, cs], ln.Pi, ALU.mult).then_inc(q["rt_done"], 1)

                def level_mask(l):
                    return mask_lv[:, l].unsqueeze(1).broadcast_to([P, 4, P])

                for ln, q, b in both:
                    dve.wait_ge(q["g_made"], i * 2 + 1)
                    A = ln.G[:, 0, 0]
                    then(V.tensor_tensor(A, ps[:, b, :].rearrange("p (j c) -> p j c", j=4), mask_ar[:, 0:P].unsqueeze(1).broadcast_to([P, 4, P]), ALU.mult))
                    then(V.tensor_tensor(A, A, ident[:].unsqueeze(1).broadcast_to([P, 4, P]), ALU.add))
                    V.tensor_tensor(ln.XT, A, level_mask(0), ALU.mult).then_inc(q["xt_set"], 1)

                def take_x(l):
                    for ln, q, b in both:
                        dve.wait_ge(q["x_made"], i * (LEVELS - 1) + l)
                        V.tensor_copy(ln.X, ps[:, b + 1, :].rearrange("p (a b) -> p a b", a=4)).then_inc(q["x_set"], 1)

                take_x(1)
                for l in range(1, LEVELS):
                    for ln, q, b in both:
                        dve.wait_ge(q["z_made"], i * (LEVELS - 1) + l)
                        V.tensor_tensor(ln.Z, ps[:, b, :].rearrange("p (a b) -> p a b", a=4), level_mask(l), ALU.mult).then_inc(q["z_set"], 1)
                    if l < LEVELS - 1:
                        take_x(l + 1)
                for ln, q, b in both:
                    dve.wait_ge(q["uh_made"], one)
                    V.tensor_copy(ln.U, ps[:, b + 2, T:2 * T].rearrange("p (t b) -> p t b", t=TT)).then_inc(q["u_set"], 1)
                for c in range(4):
                    t, rc = c // 2, slice((c % 2) * CHUNK, (c % 2 + 1) * CHUNK)
                    if c:
                        for ln, q, b in both:
                            dve.wait_ge(q["pu_made"], i * 3 + c)
                            V.tensor_tensor(ln.U[rc, t], ps[rc, b, 0:P], ln.U[rc, t], ALU.add).then_inc(q["u_set"], 1)
                    if c < 3:
                        for ln, q, b in both:
                            dve.wait_ge(q["ps_made"], i * 3 + (c + 1))
                            V.scalar_tensor_tensor(out=ln.S[:, c], in0=ps[:, b + 2, 0:P], scalar=ln.PC[:, c:c + 1], in1=mask_bd, op0=ALU.mult,
                                                   op1=ALU.mult).then_inc(q["s_set"], 1)

            def group_norm(i):
                cs = bass.ds(i * (2 * P), 2 * P)
                yv = R_[:, :, cs]

                def heads(v):
                    return v.rearrange("p t (h i) -> p t h i", i=HD)

                def per_head(v):
                    return v.rearrange("p (t h) -> p t h", t=TT).unsqueeze(3).broadcast_to([P, TT, 4, HD])

                for q in lq:
                    dve.wait_ge(q["y_set"], i + 1)
                then(V.tensor_reduce(gsm[:, 0].rearrange("p (t h) -> p t h", t=TT), heads(yv), AX.X, ALU.add))
                then(V.tensor_scalar(gsm[:, 1], gsm[:, 0], 1.0 / HD, None, ALU.mult))
                then(V.tensor_tensor(heads(yv), heads(yv), per_head(gsm[:, 1]), ALU.subtract))
                then(V.tensor_tensor(y_sq, yv, yv, ALU.mult))
                then(V.tensor_reduce(gsm[:, 0].rearrange("p (t h) -> p t h", t=TT), heads(y_sq), AX.X, ALU.add))
                then(V.tensor_scalar(gsm[:, 2], gsm[:, 0], 1.0 / HD, GN_EPS, ALU.mult, ALU.add))
                rsqrt(gsm[:, 3], gsm[:, 2], gsm[:, 4])
                V.tensor_tensor(heads(yv), heads(yv), per_head(gsm[:, 3]), ALU.mult).then_inc(y_normed, 1)

            dve.wait_ge(bank_free[0], 7)
            dve.wait_ge(bank_free[1], 7)
            recur(0)
            with dve.Fori(0, PAIRS // 2 - 1) as i:
                step.enter(i, 2 * 2 + 6 + 11)
                recur(i + 1)
                step.leave(PAIRS // 2 - 1)
            group_norm(PAIRS // 2 - 1)

            dve.wait_ge(zz_done, PAIRS // 2)
            for n in range(NJ):
                dve.wait_ge(gate_made, n + 1)
                c = slice(n * NB, (n + 1) * NB)
                V.tensor_tensor(R_[:, :, c], R_[:, :, c], ps[:, 4 + 2 * (n % 2):6 + 2 * (n % 2), :], ALU.mult).then_inc(gated, 1)
            for g in range(KT // KC):
                dve.wait_ge(mixhi_done, 3 * (KT // KC) + g + 1)
                V.tensor_tensor(alo[:, g * KC:(g + 1) * KC], ps[:, 4 + g % 4, :].rearrange("p (k t) -> p k t", k=KC),
                                ahi[:, g * KC:(g + 1) * KC].bitcast(F32), ALU.subtract).then_inc(z_tr_done, 1)

            def residual(c0, kt, n, last=False):
                per = kt // KC
                for b in range(NJ):
                    left = per if not (last and b == NJ - 1) else per - RING
                    first = c0 + b * per + RING
                    for ch in range(left):
                        s = (first + ch) % RING
                        dve.wait_ge(hi_done, first + ch + 1)
                        V.tensor_tensor(wlo[:, s], raw[:, s], whi[:, s].bitcast(F32), ALU.subtract).then_inc(split_done, 1)
                    dve.wait_ge(chunk_used, c0 + (b + 1) * per)
                    if b == 0 and n == 0:
                        dve.wait_ge(h0_in, 16)
                    cs = slice(b * NB, (b + 1) * NB)
                    V.scalar_tensor_tensor(out=Zn[:, :, cs], in0=H[:, :, cs], scalar=ALPHA, in1=ps[:, 2 * (b % 2):2 * (b % 2) + 2, :],
                                           op0=ALU.mult, op1=ALU.add).then_inc(bank_free[b % 2], 1)
                    dve.wait_ge(bank_free[b % 2], (c_jobs[n] + b) // 2 + 2)
                    for t in range(TT):
                        ins = V.bn_stats(stats[:, t, b, :], Zn[:, t, cs])
                then(ins)
                for t in range(TT):
                    then(V.bn_aggr(mv[:, t, :], stats[:, t]))
                then(V.tensor_scalar(var[:], mv[:, :, 1], LN_EPS, None, ALU.add))
                rsqrt(rstd[:], var[:], small[:, 8:8 + TT])
                for t in range(TT):
                    V.tensor_scalar(Zn[:, t], Zn[:, t], mv[:, t, 0:1], rstd[:, t:t + 1], ALU.subtract, ALU.mult).then_inc(xhat_done, 1)

            c_jobs = [PH["wo"][1], PH["down0"][1], PH["ao"][1], PH["down1"][1]]

            def norm_split(n):
                for g in range(KT // KC):
                    dve.wait_ge(ln_aff, n * (KT // KC) + g + 1)
                    k = slice(g * KC, (g + 1) * KC)
                    then(V.tensor_copy(ahi[:, k], ltmp[:, g % 2]))
                    V.tensor_tensor(alo[:, k], ltmp[:, g % 2], ahi[:, k].bitcast(F32), ALU.subtract).then_inc(ln_hi, 1)

            def natural(n):
                dve.wait_ge(wb_in, (n + 1) * 16)
                dve.wait_ge(xhat_done, (n + 1) * TT)
                for t in range(TT):
                    then(V.tensor_tensor(H[:, t], Zn[:, t], wb[:, 0], ALU.mult))
                    V.tensor_tensor(H[:, t], H[:, t], wb[:, 1], ALU.add).then_inc(h_done, 1)

            def ffn(layer):
                c0, j0 = PH[f"up{layer}"]
                u0 = layer * FB

                def multiply(c_end, up_seen):
                    dve.wait_ge(bank_free[0], up_seen)
                    dve.wait_ge(chunk_used, c_end)
                    V.tensor_tensor(gtmp, gtmp, ps[:, 2:4, :], ALU.mult).then_inc(bank_free[1], 1)

                def hidden_lo(i, f0):
                    dve.wait_ge(hhi_done, i + 1)
                    V.tensor_tensor(hTlo[:, f0, :], ps[:, 4:6, :].rearrange("p a (k t) -> p (a k) t", k=2),
                                    hThi[:, f0, :].bitcast(F32), ALU.subtract).then_inc(hlo_done, 1)

                natural(0 if layer == 0 else 2)
                split_lo(c0 + RING, 2 * CJ)
                with dve.Fori(0, FB - 1) as i:
                    c = i * (2 * CJ) + (c0 + 2 * CJ)
                    multiply(c, i + (j0 // 2 + 2))
                    split_lo(c + RING, CJ)
                    hidden_lo(i + u0, bass.ds(i * 4, 4))
                    split_lo(c + (RING + CJ), CJ)
                multiply(c0 + FB * 2 * CJ, j0 // 2 + FB + 1)
                hidden_lo(u0 + FB - 1, slice((FB - 1) * 4, FB * 4))

            residual(PH["wo"][0], KT, 0)
            norm_split(0)
            ffn(0)
            residual(PH["down0"][0], FT, 1)
            norm_split(1)
            natural(1)
            quiet(PH["kvq"][0], 12)
            dve.wait_ge(bank_free[0], PH["ao"][1] // 2 + 1)
            dve.wait_ge(bank_free[1], PH["ao"][1] // 2 + 1)
            dve.wait_ge(cap_in, 16)
            with dve.Fori(0, HEADS) as h:
                step.enter(h, 3)
                one = h + 1
                V.tensor_copy(Va, Vn[:, :, bass.ds(h * P, P)]).then_inc(t_["v_staged"], 1)
                dve.wait_ge(t_["s_made"], one)
                then(V.tensor_tensor(Sm, ps[:, 5, 0:3 * P].rearrange("p (a b) -> p a b", a=3), cap, ALU.min))
                V.tensor_reduce(small[:, 0:1], Sm[:, 0, :], AX.X, ALU.max)
                then(V.tensor_reduce(small[:, 1:2], Sm[:, 1:3, :], AX.XY, ALU.max))
                V.tensor_scalar(small[:, 2:4], small[:, 0:2], NEG / SCALE, -SCALE, ALU.max, ALU.mult).then_inc(t_["nm_set"], 1)
                dve.wait_ge(t_["p_set"], one)
                then(V.reciprocal(small[:, 6:8], small[:, 4:6]))
                V.tensor_scalar(Pr[:, 0, :], Pr[:, 0, :], small[:, 6:7], None, ALU.mult)
                V.tensor_scalar(Pr[:, 1:3, :], Pr[:, 1:3, :], small[:, 7:8], None, ALU.mult).then_inc(t_["p_normed"], 1)
                dve.wait_ge(t_["ohi_set"], one)
                V.tensor_tensor(alo[:, bass.ds(h, 1), :], ps[:, 7, 0:T].unsqueeze(1), ahi[:, bass.ds(h, 1), :].bitcast(F32),
                                ALU.subtract).then_inc(t_["olo_set"], 1)
                step.leave(HEADS)
            residual(PH["ao"][0], KT, 2)
            norm_split(2)
            ffn(1)
            residual(PH["down1"][0], FT, 3, last=True)
            natural(3)


_OUT = ((1, T, D), "float32")


def kernel(**inputs):
    import concourse.bacc as bacc
    from concourse.bass_utils import run_bass_kernel_spmd as run

    nc = bacc.Bacc("TRN2", target_bir_lowering=False, num_devices=1)
    arrays = {}

    def give(name, a):
        a = np.ascontiguousarray(a)
        arrays[name] = a
        return nc.dram_tensor(name, a.shape, mybir.dt.from_np(a.dtype), kind="ExternalInput").ap()

    i = {k: np.asarray(v) for k, v in inputs.items()}
    x = give("x", i["x"])
    rows = give("mix_rows", i["a_mix"][0].reshape(6 * KT, P))
    rwkv_rows = give("rwkv_rows", np.stack([i["a_k_k"][0], i["a_k_a"][0], i["a_r_k"][0].reshape(D), i["a_lnx_w"][0], i["a_lnx_b"][0]]))
    lora = {m: give("lora_" + m, i["a_" + m][0]) for m in ("w1", "w2", "a1", "a2", "g1", "g2")}
    lora.update({m: give("lora_" + m, i["a_" + m]) for m in ("w0", "a0")})
    w = {"r": give("w_r", i["a_w_r"][0]), "k": give("w_k", i["a_w_k"][0]), "v": give("w_v", i["a_w_v"][0]), "o": give("w_o", i["a_w_o"][0]),
         "kv_k": give("kv_k", i["kv_w_k"]), "kv_v": give("kv_v", i["kv_w_v"]), "q": give("w_q", i["b_w_q"][0]), "ao": give("w_ao", i["b_w_o"][0]),
         "gate": give("w_gate", i["ffn_w_gate"]), "up": give("w_up", i["ffn_w_up"]), "down": give("w_down", i["ffn_w_down"])}
    ln = give("ln_rows", np.stack([np.stack([np.stack([i[f"ln{n}_w"][l], i[f"ln{n}_b"][l]]) for n in (1, 2)]) for l in range(DEPTH)]))
    c = give("consts", constants())
    y = nc.dram_tensor("y", _OUT[0], F32, kind="ExternalOutput").ap()
    trunk(nc, x, rows, rwkv_rows, lora, w, c, ln, y)
    return run(nc, [arrays], core_ids=[0]).results[0]["y"]
```

```python
from contextlib import ExitStack

import numpy as np

import concourse.bass as bass
from concourse import mybir

F32 = mybir.dt.float32
F32R = mybir.dt.float32r
ALU = mybir.AluOpType
ACT = mybir.ActivationFunctionType
AX = mybir.AxisListType

P = 128
D = 2048
T = 256
TT = T // P
KT = D // P
NB = 512
NJ = D // NB
FF = 5632
FT = FF // P
FB = FF // NB
KC = 2
RING = 4
CJ = KT // KC
CF = FT // KC
LR = 96
LG = 256
HD = 64
CHUNK = 64
PAIRS = D // P
LEVELS = 6
HEADS = 16
DEPTH = 2
ALPHA = float((2 * DEPTH) ** 0.25)
LN_EPS = 1e-5
GN_EPS = 64e-5
NEG = -1e30
SCALE = float(P) ** -0.5
DECAY = float(np.exp(-0.5))

C_ID, C_TI, C_IND, C_AR, C_LM, C_BD, C_CAP = np.cumsum(
    [0, P, P, 2, 2 * P, LEVELS * P, P]).tolist()
C_END = C_CAP + 3 * P


def constants():
    i = np.arange(P)
    s, t = i[:, None], i[None, :]
    same = s // CHUNK == t // CHUNK
    c = np.zeros((P, C_END), np.float32)
    c[:, C_ID:C_ID + P] = s == t
    c[:, C_TI:C_TI + P] = np.where(same & (s <= t), -DECAY, 0)
    c[:, C_IND:C_IND + 2] = np.where(s // CHUNK == np.arange(2)[None, :], -DECAY, 0)
    c[:, C_AR:C_AR + P] = same & (s < t)
    c[:, C_AR + P:C_AR + 2 * P] = same & (s <= t)
    for l in range(LEVELS):
        m = 2 ** l
        a, b = (s, t) if l else (t, s)
        c[:, C_LM + l * P:C_LM + (l + 1) * P] = (s == t) | ((a // (2 * m) == b // (2 * m)) & (a // m % 2 == 1) & (b // m % 2 == 0))
    c[:, C_BD:C_BD + P] = s // HD == t // HD
    cap = np.where(t <= s, 3e38, NEG / SCALE)
    c[:, C_CAP:C_CAP + P] = cap
    c[:, C_CAP + P:C_CAP + 2 * P] = 3e38
    c[:, C_CAP + 2 * P:C_CAP + 3 * P] = cap
    return c


PH = {}
_c = _j = 0
for _name, _jobs, _per in (("proj", 12, CJ), ("wo", NJ, CJ), ("up0", 2 * FB, CJ), ("down0", NJ, CF), ("kvq", 12, CJ),
                           ("ao", NJ, CJ), ("up1", 2 * FB, CJ), ("down1", NJ, CF)):
    assert _c % RING == 0 and _j % 2 == 0
    PH[_name] = (_c, _j)
    _c += _jobs * _per
    _j += _jobs
CHUNKS = _c


class Count:

    def __init__(self, sem):
        self.sem, self.base, self.n = sem, 0, 0

    def up(self, ins):
        ins.then_inc(self.sem, 1)
        self.n += 1

    def now(self, back=0):
        return self.base + (self.n - back)

    def enter(self, i, per):
        self.start, self.per = self.n, per
        self.base = i * per + self.start
        self.n = 0

    def leave(self, trips):
        assert self.n == self.per, (self.n, self.per)
        self.base, self.n = 0, self.start + trips * self.per


def trunk(nc, x, rows, rwkv_rows, lora, w, consts, ln_rows, y):
    with ExitStack() as ctx:
        def sem(name):
            return ctx.enter_context(nc.semaphore(name))

        def sb(name, shape, dt=F32, stack=ctx):
            return stack.enter_context(nc.sbuf_tensor(name, shape, dt))

        raw = sb("raw", [P, RING, KC, NB])
        whi = sb("whi", [P, RING, KC, NB], F32R)
        wlo = sb("wlo", [P, RING, KC, NB], F32R)
        ident = sb("ident", [P, P])
        mixT = sb("mixT", [P, 6 * KT])
        lnT = sb("lnT", [P, 2 * 2 * 2 * KT])
        stats = sb("stats", [P, TT, NJ, 6])
        mv = sb("mv", [P, TT, 2])
        var = sb("var", [P, TT])
        rstd = sb("rstd", [P, TT])
        small = sb("small", [P, 32])
        gsm = sb("gsm", [P, 5, 8])
        nsmall = sb("nsmall", [P, 48])
        idle = sb("idle", [P, 10])
        with ExitStack() as early:
            a2t = sb("a2t", [P, 8192], stack=early)
        ahi = sb("ahi", [P, KT, T], F32R)
        alo = sb("alo", [P, KT, T], F32R)
        with ExitStack() as early:
            big = sb("big", [P, 124 * 256], stack=early)
        common = sb("common", [P, 36 * 256])
        hThi = sb("hThi", [P, FT, T], F32R)
        hTlo = sb("hTlo", [P, FT, T], F32R)
        ps = ctx.enter_context(nc.psum_tensor("ps", [P, 8, NB], F32))

        def carve(base, at, *shape):
            n = int(np.prod(shape))
            v = base[:, at:at + n]
            if len(shape) == 1:
                return v
            names = "abcd"[:len(shape)]
            return v.rearrange(f"p ({' '.join(names)}) -> p {' '.join(names)}", **{q: n for q, n in zip(names[:-1], shape[:-1])})

        KB = 256
        K_ = carve(big, 0, TT, D)
        L_ = carve(big, 16 * KB, TT, D)
        hw = carve(big, 32 * KB, T)
        ha = carve(big, 33 * KB, T)
        hg = carve(big, 34 * KB, 2, T)
        mtmp = carve(big, 36 * KB, 2, KC, T)
        R_ = carve(big, 40 * KB, TT, D)
        V_ = carve(big, 56 * KB, TT, D)
        A_ = carve(big, 72 * KB, TT, D)
        xT = carve(big, 88 * KB, KT, T + 1)
        xxT = carve(big, 88 * KB + KT * (T + 1), KT, T)
        rowsn = carve(big, 121 * KB, P)
        rowsl = carve(big, 122 * KB, P)
        xn = K_
        w1 = carve(big, 56 * KB, KT, LR)
        a1 = carve(big, 62 * KB, KT, LR)
        g1 = carve(big, 40 * KB, KT, LG)
        w2 = carve(big, 0, D)
        a2 = carve(big, 8 * KB, D)
        g2 = carve(big, 88 * KB, 2, D)
        places = [[a2t, 0, 8192], [big, 104 * KB, 124 * KB], [big, 36 * KB, 40 * KB], [big, 32 * KB, 34 * KB]]

        def tmp(*shape):
            n = int(np.prod(shape))
            place = next(p for p in places if p[1] + n <= p[2])
            place[1] += n
            return carve(place[0], place[1] - n, *shape)

        tri_i, ind = tmp(P), tmp(2)
        mask_ar, mask_lv, mask_bd = tmp(2 * P), tmp(LEVELS, P), tmp(P)

        class Lane:

            def __init__(self, n):
                self.bank = 4 * n
                self.G = tmp(2, 2, 4, P)
                self.Z, self.XT = tmp(4, P), tmp(4, P)
                self.Ls, self.Vs = tmp(TT, P), tmp(TT, P)
                self.bh, self.kh = tmp(TT, P), tmp(TT, P)
                self.arT = tmp(TT, 2, P)
                self.bkT = tmp(2, 2, TT, P)
                PP = tmp(3, TT, P)
                self.Pi, self.Pn, self.Pe = (PP[:, n] for n in range(3))
                self.at, self.rt = self.Pe, self.Pi
                self.X = PP[:, 0:2].rearrange("p n t c -> p (n t) c")
                over = [self.G[:, 1, 0, 2 * k:2 * k + 2, :] for k in range(2)]
                self.AV = over[0].rearrange("p t (b c) -> p (t b) c", c=CHUNK)
                self.U = over[1]
                self.WT = self.G[:, 0, 0, 0:2, :]
                self.S = self.Z

        lanes = [Lane(0), Lane(1)]
        for ln in lanes:
            ln.PC, ln.PCn = tmp(4), tmp(4)
        par = tmp(2, 2 * P)
        y_sq = lanes[0].G[:, 0, 0].rearrange("p j c -> p (j c)").rearrange("p (t c) -> p t c", t=TT)
        KN_ = carve(big, 88 * KB, TT, D)
        bsum = sb("bsum", [P, TT, 2 * PAIRS])
        npar = [carve(big, (104 + 6 * n) * KB, 3, NB) for n in range(2)]
        ntmp = carve(big, 36 * KB, TT, NB)
        H = carve(common, 0, TT, D)
        Zn = carve(common, 16 * KB, TT, D)
        ltmp = carve(common, 32 * KB, 2, KC, T)
        gtmp = carve(common, 32 * KB, TT, NB)
        wb = carve(big, 40 * KB, 2, D)
        Kn = carve(big, 40 * KB, TT, D)
        Vn = carve(big, 56 * KB, TT, D)
        Qn = carve(big, 72 * KB, TT, D)
        stg = [carve(big, (88 + 6 * n) * KB, 3, TT, 2 * P) for n in range(2)]
        QKT = [carve(big, (100 + 4 * n) * KB, 2, 4 * P) for n in range(2)]
        Sm = [carve(big, (108 + 3 * n) * KB, 2, 3 * P) for n in range(2)]
        PT = [carve(big, (114 + 3 * n) * KB, 2, 3 * P) for n in range(2)]
        asm = [sb(f"asm{n}", [P, 3, 2, 2]) for n in range(2)]
        cap = carve(big, 120 * KB, 3 * P)

        raw_landed = [sem(f"raw_landed{s}") for s in range(RING)]
        hi_done, split_done, chunk_used = sem("hi_done"), sem("split_done"), sem("chunk_used")
        bank_free = [sem("bank_free0"), sem("bank_free1")]
        x_in = [sem(f"x_in{b}") for b in range(NJ)]
        rows_in, g1_in, wa1_in, wa2_in, id_in = (sem(n) for n in ("rows_in", "g1_in", "wa1_in", "wa2_in", "id_in"))
        xt_made, xt_copied, xx_done, rows_made = (
            sem(n) for n in ("xt_made", "xt_copied", "xx_done", "rows_made"))
        lmix_done, lora1_made, lora1_copied, ones_set, lora2_made, lora2_copied = (
            sem(n) for n in ("lmix_done", "lora1_made", "lora1_copied", "ones_set", "lora2_made", "lora2_copied"))
        mix_done, mixhi_done, act_ready = sem("mix_done"), sem("mixhi_done"), sem("act_ready")
        dve_step = sem("dve_step")
        masks_in, g2_in, h0_in, wb_in, cap_in = (sem(n) for n in ("masks_in", "g2_in", "h0_in", "wb_in", "cap_in"))
        names = ("ls_set cum_made decay_done rt_done tr_made arT_set bkT_set g_made g_raw g_set z_made z_set x_made x_set "
                 "xt_made xt_set av_made av_set uh_made u_set wt_made wt_set pu_made ps_made s_set y_made y_set")
        lq = [{n: sem(f"lane{s}_{n}") for n in names.split()} for s in range(2)]
        par_in, zz_done, zeros_set, idle_set, y_normed, pool_step = (sem(n) for n in ("par_in", "zz_done", "zeros_set", "idle_set", "y_normed", "pool_step"))
        npar_in, sq_asked, sq_done = [sem("npar_in0"), sem("npar_in1")], sem("sq_asked"), sem("sq_done")
        nk_done = sem("nk_done")
        gate_made, gated = sem("gate_made"), sem("gated")
        z_tr, z_tr_done = sem("z_tr"), sem("z_tr_done")
        xhat_done, ln_tr, ln_aff, ln_hi, h_done = (sem(n) for n in ("xhat_done", "ln_tr", "ln_aff", "ln_hi", "h_done"))
        h_tr, hhi_done, hlo_done = (sem(n) for n in ("h_tr", "hhi_done", "hlo_done"))
        anames = "qk_staged v_staged qk_tr qkt_set s_made nm_set p_set p_normed pt_made pt_set o_made ohi_set olo_set"
        al = [{n: sem(f"heads{s}_{n}") for n in anames.split()} for s in range(2)]
        y_out = sem("y_out")

        block = ctx.enter_context(nc.Block())

        @block.sync
        def _(sp):
            def chunk(c, s, src):
                if not isinstance(c, int) or c >= RING:
                    sp.wait_ge(split_done, c - (RING - 1))
                sp.dma_start(raw[:, s], src.rearrange("(k p) n -> p k n", p=P)).then_inc(raw_landed[s], 16)

            def stream(c0, mats, kt, col):
                for n, m in enumerate(mats):
                    for j in range(kt // KC):
                        c = n * (kt // KC) + j
                        chunk(c0 + c, c % RING, m[j * KC * P:(j + 1) * KC * P, col])

            def blocks(c0, mats, kt, n):
                per = len(mats) * kt // KC
                if per % RING:
                    with sp.Fori(0, n // 2) as i:
                        for b in range(2):
                            for j in range(kt // KC):
                                c = b * (kt // KC) + j
                                chunk(i * (2 * per) + (c0 + c), c % RING,
                                      mats[0][j * KC * P:(j + 1) * KC * P, bass.ds(i * (2 * NB) + b * NB, NB)])
                else:
                    with sp.Fori(0, n) as i:
                        stream(i * per + c0, mats, kt, bass.ds(i * NB, NB))

            stream(0, [w["k"]], KT, slice(0, NB))
            for b in range(1, NJ):
                stream(b * CJ, [w["k"]], KT, slice(b * NB, (b + 1) * NB))
            blocks(PH["proj"][0] + NJ * CJ, [w["r"]], KT, NJ)
            blocks(PH["proj"][0] + 2 * NJ * CJ, [w["v"]], KT, NJ)
            blocks(PH["wo"][0], [w["o"]], KT, NJ)
            blocks(PH["up0"][0], [w["gate"][0], w["up"][0]], KT, FB)
            blocks(PH["down0"][0], [w["down"][0]], FT, NJ)
            for n, m in enumerate(("kv_k", "kv_v", "q")):
                blocks(PH["kvq"][0] + n * NJ * CJ, [w[m]], KT, NJ)
            blocks(PH["ao"][0], [w["ao"]], KT, NJ)
            blocks(PH["up1"][0], [w["gate"][1], w["up"][1]], KT, FB)
            blocks(PH["down1"][0], [w["down"][1]], FT, NJ)
            yv = y[0].rearrange("(t p) d -> p t d", p=P)
            for b in range(NJ):
                cs = slice(b * NB, (b + 1) * NB)
                sp.wait_ge(h_done, 3 * TT + b + 1)
                sp.dma_start(yv[:, :, cs], H[:, :, cs]).then_inc(y_out, 16)
            sp.wait_ge(y_out, 16 * NJ)

        @block.gpsimd
        def _(pool):
            xv = x[0].rearrange("(t p) d -> p t d", p=P)
            nc.gpsimd.memset(idle[:], 0.0).then_inc(idle_set, 1)
            pool.wait_ge(idle_set, 1)

            def wait_aside(k, ready, value):
                pool.wait_ge(ready, value)
                nc.gpsimd.tensor_tensor(idle[:, k:k + 1], idle[:, 0:1], idle[:, 0:1], ALU.mult)

            nc.gpsimd.dma_start(ident[:], consts[:, C_ID:C_ID + P]).then_inc(id_in, 16)
            for b in range(NJ):
                cs = slice(b * NB, (b + 1) * NB)
                nc.gpsimd.dma_start(xn[:, :, cs], xv[:, :, cs]).then_inc(x_in[b], 16)
            nc.gpsimd.dma_start(rowsn[0:6 * KT], rows).then_inc(rows_in, 16)
            nc.gpsimd.dma_start(rowsl, ln_rows.rearrange("a b n (k p) -> (a b n k) p", p=P)).then_inc(rows_in, 16)
            nc.gpsimd.dma_start(w1, lora["w1"].rearrange("(k p) n -> p k n", p=P)).then_inc(wa1_in, 16)
            nc.gpsimd.dma_start(a1, lora["a1"].rearrange("(k p) n -> p k n", p=P)).then_inc(wa1_in, 16)
            nc.gpsimd.dma_start(g1, lora["g1"].rearrange("(k p) n -> p k n", p=P)).then_inc(g1_in, 16)
            pool.wait_ge(xt_made, KT // KC)
            for dst, m, bias in ((w2, "w2", "w0"), (a2, "a2", "a0")):
                nc.gpsimd.dma_start(dst[0:LR], lora[m]).then_inc(wa2_in, 16)
                nc.gpsimd.dma_start(dst[LR:LR + 1], lora[bias]).then_inc(wa2_in, 16)
            pool.wait_ge(mix_done, 3 * (KT // KC))
            for n in range(NJ):
                if n >= 2:
                    pool.wait_ge(nk_done, n - 1)
                nc.gpsimd.dma_start(npar[n % 2], rwkv_rows[0:3, n * NB:(n + 1) * NB].partition_broadcast(P)).then_inc(npar_in[n % 2], 16)
            pool.wait_ge(chunk_used, 12 * CJ)
            nc.gpsimd.dma_start(a2t[:, 0:C_CAP - C_TI], consts[:, C_TI:C_CAP]).then_inc(masks_in, 16)

            def load_par(cs):
                nc.gpsimd.dma_start(par, rwkv_rows[3:5, cs].partition_broadcast(P)).then_inc(par_in, 16)

            pool.wait_ge(nk_done, NJ)
            for s in range(2):
                nc.gpsimd.memset(lanes[s].bkT, 0.0).then_inc(zeros_set, 1)
            load_par(slice(0, 2 * P))
            pstep = Count(pool_step)

            def finish(i):
                def then(k, ins):
                    pstep.up(ins)
                    wait_aside(k, pool_step, pstep.now())

                cs = bass.ds(i * (2 * P), 2 * P)
                yv, vv = R_[:, :, cs], V_[:, :, cs].rearrange("p t (h i) -> p t h i", i=HD)
                pool.wait_ge(lq[0]["y_set"], i + 1)
                wait_aside(1, lq[1]["y_set"], i + 1)
                nc.gpsimd.tensor_tensor(vv, vv, bsum[:, :, bass.ds(i * 4, 4)].unsqueeze(3).broadcast_to([P, TT, 4, HD]), ALU.mult)
                pool.wait_ge(par_in, i * 16 + 16)
                wait_aside(2, y_normed, i + 1)
                then(3, nc.gpsimd.tensor_tensor(yv, yv, par[:, 0].unsqueeze(1).broadcast_to([P, TT, 2 * P]), ALU.mult))
                then(4, nc.gpsimd.tensor_tensor(yv, yv, par[:, 1].unsqueeze(1).broadcast_to([P, TT, 2 * P]), ALU.add))
                nc.gpsimd.tensor_tensor(yv, yv, V_[:, :, cs], ALU.add).then_inc(zz_done, 1)

            def mask_products(i):
                for ln, q in zip(lanes, lq):
                    pool.wait_ge(q["g_raw"], i + 1)
                    for n, x in ((1, 0), (1, 1), (0, 1)):
                        m = ln.G[:, n, x]
                        last = nc.gpsimd.tensor_tensor(m, m, mask_ar[:, x * P:(x + 1) * P].unsqueeze(1).broadcast_to([P, 4, P]), ALU.mult)
                    last.then_inc(q["g_set"], 1)

            pool.wait_ge(masks_in, 16)
            mask_products(0)
            with pool.Fori(0, PAIRS // 2 - 1) as i:
                pstep.enter(i, 2)
                mask_products(i + 1)
                finish(i)
                pool.wait_ge(zz_done, i + 1)
                load_par(bass.ds(i * (2 * P) + 2 * P, 2 * P))
                pstep.leave(PAIRS // 2 - 1)
            for q in lq:
                pool.wait_ge(q["rt_done"], PAIRS // 2)
            nc.gpsimd.dma_start(g2, lora["g2"].rearrange("(k p) n -> p k n", p=P)).then_inc(g2_in, 16)
            nc.gpsimd.dma_start(H, xv).then_inc(h0_in, 16)
            finish(PAIRS // 2 - 1)
            lnw = lambda n: ln_rows[n // 2, n % 2].partition_broadcast(P)

            def load_wb(n, ready, value):
                pool.wait_ge(ready, value)
                nc.gpsimd.dma_start(wb, lnw(n)).then_inc(wb_in, 16)
            load_wb(0, z_tr, KT // KC)
            load_wb(1, chunk_used, PH["kvq"][0])
            nc.gpsimd.dma_start(cap, consts[:, C_CAP:C_END]).then_inc(cap_in, 16)

            def stage(i, s, which):
                cs = bass.ds(i * (4 * P) + 2 * s * P, 2 * P)
                if which == "qk":
                    nc.gpsimd.tensor_copy(stg[s][:, 0], Qn[:, :, cs])
                    nc.gpsimd.tensor_copy(stg[s][:, 1], Kn[:, :, cs]).then_inc(al[s]["qk_staged"], 1)
                else:
                    nc.gpsimd.tensor_copy(stg[s][:, 2], Vn[:, :, cs]).then_inc(al[s]["v_staged"], 1)

            q0 = PH["kvq"][1] + 2 * NJ
            pool.wait_ge(bank_free[0], q0 // 2 + 2)
            pool.wait_ge(bank_free[1], q0 // 2 + 1)
            for which in ("qk", "v"):
                for s in range(2):
                    stage(0, s, which)
            with pool.Fori(0, HEADS // 4 - 1) as i:
                for n, (which, used) in enumerate((("qk", "qk_tr"), ("v", "o_made"))):
                    for s in range(2):
                        wait_aside(5 + 2 * n + s, al[s][used], i + 1)
                        stage(i + 1, s, which)
            load_wb(2, al[1]["v_staged"], HEADS // 4)
            load_wb(3, chunk_used, CHUNKS)

        @block.tensor
        def _(pe):
            mm, tr = nc.tensor.matmul, nc.tensor.transpose

            def chunk(c, ch, parity, kt, hi, lo):
                s = (ch + (CF * parity if kt == FT else 0)) % RING
                pe.wait_ge(split_done, c + (ch + 1))
                for k2 in range(KC):
                    k = ch * KC + k2
                    for t in range(TT):
                        o, tok = ps[:, 2 * parity + t, :], slice(t * P, (t + 1) * P)
                        mm(o, hi[:, k, tok], whi[:, s, k2, :], start=(k == 0), stop=False)
                        mm(o, hi[:, k, tok], wlo[:, s, k2, :], start=False, stop=False)
                        last = mm(o, lo[:, k, tok], whi[:, s, k2, :], start=False, stop=(k == kt - 1))
                last.then_inc(chunk_used, 1)

            def job(c, u, parity, kt, hi, lo):
                pe.wait_ge(bank_free[parity], u + 1)
                for ch in range(kt // KC):
                    chunk(c, ch, parity, kt, hi, lo)

            def first_job(c, u, ready, ready0, src=None, made=None, src_ready=None):
                def transposes(g):
                    src_ready(g)
                    for k2 in range(KC):
                        for t in range(TT):
                            k = g * KC + k2
                            last = tr(ps[:, 4 + g % 4, k2 * T + t * P:k2 * T + (t + 1) * P], src[:, t, k * P:(k + 1) * P], ident[:])
                    last.then_inc(made, 1)

                if src is not None:
                    for g in range(4):
                        transposes(g)
                pe.wait_ge(bank_free[0], u + 1)
                for ch in range(CJ):
                    pe.wait_ge(ready, ready0 + ch + 1)
                    chunk(c, ch, 0, KT, ahi, alo)
                    if src is not None and ch + 4 < CJ:
                        transposes(ch + 4)

            def jobs(c0, j0, n, kt, hi, lo):
                per = kt // KC
                with pe.Fori(0, n // 2) as i:
                    for b in range(2):
                        job(i * (2 * per) + (c0 + b * per), i + j0 // 2, b, kt, hi, lo)

            pe.wait_ge(id_in, 16)
            for g in range(KT // KC):
                pe.wait_ge(x_in[g * KC * P // NB], 16)
                if g >= 4:
                    pe.wait_ge(xt_copied, g - 3)
                for k2 in range(KC):
                    for t in range(TT):
                        k = g * KC + k2
                        last = tr(ps[:, 4 + g % 4, k2 * T + t * P:k2 * T + (t + 1) * P], xn[:, t, k * P:(k + 1) * P], ident[:])
                last.then_inc(xt_made, 1)
            pe.wait_ge(rows_in, 32)
            tr(ps[:, 0, 0:6 * KT], rowsn[0:6 * KT], ident[0:6 * KT, 0:6 * KT]).then_inc(rows_made, 1)
            tr(ps[:, 2, 0:P], rowsl, ident[:]).then_inc(rows_made, 1)
            pe.wait_ge(xt_copied, KT // KC)
            pe.wait_ge(wa1_in, 32)
            for n, (m, buf) in enumerate(((w1, L_), (a1, A_))):
                mx = buf.rearrange("p t (k n) -> p (t k) n", n=T)
                for k in range(KT):
                    pe.wait_ge(lmix_done, n * KT + k + 1)
                    last = mm(ps[0:LR, 4 + n, 0:T], m[:, k, :], mx[:, k, :], start=(k == 0), stop=(k == KT - 1))
                last.then_inc(lora1_made, 1)
            pe.wait_ge(g1_in, 16)
            mx = L_.rearrange("p t (k n) -> p (t k) n", n=T)
            for k in range(KT):
                pe.wait_ge(lmix_done, 2 * KT + k + 1)
                for m in range(2):
                    last = mm(ps[:, 6 + m, 0:T], g1[:, k, m * P:(m + 1) * P], mx[:, k, :], start=(k == 0), stop=(k == KT - 1))
            last.then_inc(lora1_made, 1)
            pe.wait_ge(wa2_in, 64)
            pe.wait_ge(ones_set, 2)
            pe.wait_ge(lora1_copied, 4)
            for n in range(2 * NJ):
                if n >= 2:
                    pe.wait_ge(lora2_copied, n - 1)
                h, m = ((hw, w2), (ha, a2))[n // NJ]
                for t in range(TT):
                    last = mm(ps[:, 4 + 2 * (n % 2) + t, :], h[0:LR + 1, t * P:(t + 1) * P],
                              m[0:LR + 1, (n % NJ) * NB:(n % NJ + 1) * NB], start=True, stop=True)
                last.then_inc(lora2_made, 1)
            for n in range(3):
                c, j = n * NJ * CJ, n * NJ
                first_job(c, j // 2, act_ready, n * (KT // KC))
                job(c + CJ, j // 2, 1, KT, ahi, alo)
                jobs(c + 2 * CJ, j + 2, NJ - 2, KT, ahi, alo)
            for b in range(2):
                pe.wait_ge(bank_free[b], 7)

            def rows_of(c):
                return c // 2, slice((c % 2) * CHUNK, (c % 2 + 1) * CHUNK)

            def blocks(out, lhs, rhs):
                for j in range(4):
                    last = mm(out(j), lhs(j), rhs(j), start=True, stop=True)
                return last

            def decays(i):
                for ln, q in zip(lanes, lq):
                    pe.wait_ge(q["ls_set"], i + 1)
                    mm(ps[:, ln.bank + 1, 0:T], tri_i, ln.Ls.rearrange("p t c -> p (t c)"), start=True, stop=True)
                    for t in range(TT):
                        last = mm(ps[:, ln.bank + 1, T + 2 * t:T + 2 * t + 2], ln.Ls[:, t, :], ind, start=True, stop=True)
                    last.then_inc(q["cum_made"], 1)

            def recur(i, more):
                one = i + 1
                both = [(lanes[s], lq[s], lanes[s].bank) for s in range(2)]

                def v_of(m):
                    return lambda j: m[:, j % 2, (j // 2) * HD:(j // 2 + 1) * HD]

                for ln, q, b in both:
                    pe.wait_ge(q["rt_done"], one)
                    for t in range(TT):
                        for n, src in enumerate((ln.at, ln.rt)):
                            tr(ps[:, b + 2, (t * 2 + n) * P:(t * 2 + n + 1) * P], src[:, t, :], ident[:])
                    for n, src in enumerate((ln.bh, ln.kh)):
                        for t in range(TT):
                            last = tr(ps[:, b + 3, (n * TT + t) * P:(n * TT + t + 1) * P], src[:, t, :], ident[:])
                    last.then_inc(q["tr_made"], 1)
                def products(ln, b, n, x):
                    return blocks(lambda j: ps[:, b + 2 * n + x, j * P:(j + 1) * P], lambda j: ln.bkT[:, n, j // 2, j % 2, :],
                                  lambda j: ln.arT[:, j % 2, x, :])

                for ln, q, b in both:
                    pe.wait_ge(q["arT_set"], one)
                    pe.wait_ge(q["bkT_set"], one)
                    products(ln, b, 0, 0).then_inc(q["g_made"], 1)
                for ln, q, b in both:
                    for n, x in ((0, 1), (1, 0), (1, 1)):
                        last = products(ln, b, n, x)
                    last.then_inc(q["g_made"], 1)
                for l in range(1, LEVELS):
                    for ln, q, b in both:
                        pe.wait_ge(q["xt_set"], i * LEVELS + l)
                        if l == 1:
                            pe.wait_ge(q["g_raw"], one)
                        for j in range(4):
                            last = tr(ps[:, b + 1, j * P:(j + 1) * P], ln.XT[:, j, :], ident[:])
                        last.then_inc(q["x_made"], 1)
                    if l == 4:
                        for ln, q, b in both:
                            pe.wait_ge(q["g_set"], one)
                            blocks(lambda j: ps[:, b + 2, j * HD:(j + 1) * HD], lambda j: ln.G[:, 1, 0, j, :], v_of(ln.Vs)).then_inc(q["av_made"], 1)
                    for ln, q, b in both:
                        pe.wait_ge(q["x_set"], i * (LEVELS - 1) + l)
                        blocks(lambda j: ps[:, b, j * P:(j + 1) * P], lambda j: ln.G[:, 0, 0, j, :], lambda j: ln.X[:, j, :]).then_inc(q["z_made"], 1)
                    for ln, q, b in both:
                        pe.wait_ge(q["z_set"], i * (LEVELS - 1) + l)
                        blocks(lambda j: ps[:, b + 3, j * P:(j + 1) * P], lambda j: ln.Z[:, j, :], lambda j: ln.XT[:, j, :]).then_inc(q["xt_made"], 1)
                for ln, q, b in both:
                    pe.wait_ge(q["xt_set"], one * LEVELS)
                    for t in range(TT):
                        for h in range(2):
                            last = mm(ps[h * HD:(h + 1) * HD, b + 1, t * P:(t + 1) * P], ln.at[:, t, h * HD:(h + 1) * HD],
                                      ln.XT[:, 2 * h + t, :], start=True, stop=True)
                    last.then_inc(q["wt_made"], 1)
                    pe.wait_ge(q["av_set"], one)
                    blocks(lambda j: v_of(ps[:, b + 2, T:2 * T].rearrange("p (t c) -> p t c", t=TT))(j), lambda j: ln.XT[:, j, :],
                           lambda j: ln.AV[:, j, :]).then_inc(q["uh_made"], 1)

                def y_part(ln, b, n, rhs, j, **kw):
                    t, hh = j % 2, slice((j // 2) * HD, (j // 2 + 1) * HD)
                    return mm(ps[:, b + 3, t * P + hh.start:t * P + hh.stop], ln.G[:, n, 1, j, :], rhs[:, t, hh], skip_group_check=True, **kw)

                def y_state(ln, b, c):
                    t, rc = rows_of(c)
                    return mm(ps[rc, b + 3, t * P:(t + 1) * P], ln.arT[:, t, 1, rc], ln.S[:, c - 1, :],
                              start=False, stop=False, skip_group_check=True)

                for c in range(4):
                    t, rc = rows_of(c)
                    for ln, q, b in both:
                        if c == 0:
                            continue
                        pe.wait_ge(q["s_set"], i * 3 + c)
                        mm(ps[rc, b, 0:P], ln.WT[:, t, rc], ln.S[:, c - 1, :], start=True, stop=True).then_inc(q["pu_made"], 1)
                    if 0 < c < 3:
                        for ln, q, b in both:
                            mm(ps[:, b + 2, 0:P], ident[:], ln.S[:, c - 1, :], start=True, stop=False)
                            mm(ps[:, b + 2, 0:P], ln.kh[rc, t, :], ln.Vs[rc, t, :], start=False, stop=False)
                    elif c == 3:
                        for ln, q, b in both:
                            y_state(ln, b, 3)
                    for ln, q, b in both:
                        pe.wait_ge(q["u_set"], i * 4 + (c + 1))
                        if c == 0:
                            mm(ps[:, b + 2, 0:P], ln.kh[rc, t, :], ln.Vs[rc, t, :], start=True, stop=False)
                        if c < 3:
                            mm(ps[:, b + 2, 0:P], ln.bh[rc, t, :], ln.U[rc, t, :], start=False, stop=True).then_inc(q["ps_made"], 1)
                    if c == 0:
                        for q in lq:
                            pe.wait_ge(q["wt_set"], one)
                        if more:
                            decays(i + 1)
                    for ln, q, b in both:
                        if c == 0:
                            for j in range(4):
                                y_part(ln, b, 1, ln.Vs, j, start=(j == 0), stop=False)
                        elif c == 1:
                            y_state(ln, b, 1)
                            y_part(ln, b, 0, ln.U, 0, start=False, stop=False)
                        elif c == 2:
                            y_state(ln, b, 2)
                            y_part(ln, b, 0, ln.U, 2, start=False, stop=False)
                        elif c == 3:
                            y_part(ln, b, 0, ln.U, 1, start=False, stop=False)
                            y_part(ln, b, 0, ln.U, 3, start=False, stop=True).then_inc(q["y_made"], 1)
                for q in lq:
                    pe.wait_ge(q["y_set"], one)

            pe.wait_ge(masks_in, 16)
            decays(0)
            with pe.Fori(0, PAIRS // 2 - 1) as i:
                recur(i, True)
            recur(PAIRS // 2 - 1, False)

            pe.wait_ge(g2_in, 16)
            for s in range(2):
                pe.wait_ge(lq[s]["y_set"], PAIRS // 2)
            for n in range(NJ):
                for t in range(TT):
                    for k in range(2):
                        last = mm(ps[:, 2 * n + t, :], hg[:, k, t * P:(t + 1) * P], g2[:, k, n * NB:(n + 1) * NB], start=(k == 0), stop=(k == 1))
                last.then_inc(gate_made, 1)

            c, j = PH["wo"]
            first_job(c, j // 2, z_tr_done, 0, R_, z_tr, lambda g: pe.wait_ge(gated, NJ if g > 1 else NJ - 1))
            job(c + CJ, j // 2, 1, KT, ahi, alo)
            jobs(c + 2 * CJ, j + 2, NJ - 2, KT, ahi, alo)

            def normed_job(n, name):
                c, j = PH[name]
                first_job(c, j // 2, ln_hi, n * (KT // KC), Zn, ln_tr,
                          lambda g: pe.wait_ge(xhat_done, n * NJ + g // (NJ // 2) + 1))
                job(c + CJ, j // 2, 1, KT, ahi, alo)

            def ffn(layer):
                c0, j0 = PH[f"up{layer}"]
                u0 = layer * FB

                def h_transposes(i):
                    pe.wait_ge(bank_free[1], i + (j0 // 2 + 2 - u0))
                    for f in range(4):
                        for t in range(TT):
                            last = tr(ps[:, 4 + f // 2, (f % 2) * T + t * P:(f % 2) * T + (t + 1) * P], gtmp[:, t, f * P:(f + 1) * P], ident[:])
                    last.then_inc(h_tr, 1)

                normed_job(2 * layer, f"up{layer}")
                with pe.Fori(0, FB - 1) as i:
                    job(i * (2 * CJ) + (c0 + 2 * CJ), i + (j0 // 2 + 1), 0, KT, ahi, alo)
                    h_transposes(i + u0)
                    job(i * (2 * CJ) + (c0 + 3 * CJ), i + (j0 // 2 + 1), 1, KT, ahi, alo)
                    pe.wait_ge(hlo_done, i + (u0 + 1))
                h_transposes(u0 + FB - 1)
                pe.wait_ge(hlo_done, u0 + FB)
                jobs(*PH[f"down{layer}"], NJ, FT, hThi, hTlo)

            ffn(0)
            normed_job(1, "kvq")
            jobs(PH["kvq"][0] + 2 * CJ, PH["kvq"][1] + 2, 10, KT, ahi, alo)
            for b in range(2):
                pe.wait_ge(bank_free[b], PH["ao"][1] // 2 + 1)
            pe.wait_ge(cap_in, 16)
            with pe.Fori(0, HEADS // 4) as i:
                one = i + 1
                lane = [(al[s], 4 * s, stg[s], QKT[s], Sm[s], PT[s]) for s in range(2)]
                for q, b, st, qkt, sm, pt in lane:
                    pe.wait_ge(q["qk_staged"], one)
                    for h in range(2):
                        for n in range(4):
                            last = tr(ps[:, b + h, n * P:(n + 1) * P], st[:, n // 2, n % 2, h * P:(h + 1) * P], ident[:])
                    last.then_inc(q["qk_tr"], 1)
                for q, b, st, qkt, sm, pt in lane:
                    pe.wait_ge(q["qkt_set"], one)
                    for h in range(2):
                        mm(ps[:, b + 2 + h, 0:P], qkt[:, h, 0:P], qkt[:, h, 2 * P:3 * P], start=True, stop=True)
                        last = mm(ps[:, b + 2 + h, P:3 * P], qkt[:, h, P:2 * P], qkt[:, h, 2 * P:4 * P], start=True, stop=True)
                    last.then_inc(q["s_made"], 1)
                for q, b, st, qkt, sm, pt in lane:
                    pe.wait_ge(q["p_normed"], one)
                    for h in range(2):
                        for n in range(3):
                            last = tr(ps[:, b + h, n * P:(n + 1) * P], sm[:, h, n * P:(n + 1) * P], ident[:])
                    last.then_inc(q["pt_made"], 1)
                for q, b, st, qkt, sm, pt in lane:
                    pe.wait_ge(q["pt_set"], one)
                    pe.wait_ge(q["v_staged"], one)
                    for h in range(2):
                        v = st[:, 2, :, h * P:(h + 1) * P]
                        mm(ps[:, b + 2 + h, 0:T], v[:, 0], pt[:, h, 0:2 * P], start=True, stop=False, skip_group_check=True)
                        last = mm(ps[:, b + 2 + h, P:T], v[:, 1], pt[:, h, 2 * P:3 * P], start=False, stop=True, skip_group_check=True)
                    last.then_inc(q["o_made"], 1)
            for q in al:
                pe.wait_ge(q["olo_set"], HEADS // 4)
            jobs(*PH["ao"], NJ, KT, ahi, alo)
            ffn(1)

        @block.scalar
        def _(act):
            A = nc.scalar.activation

            def split_hi(c, u, n):
                for ch in range(n):
                    s = ch % RING
                    act.wait_ge(raw_landed[s], (u + ch // RING + 1) * 16)
                    if not isinstance(c, int) or c + ch >= RING:
                        act.wait_ge(chunk_used, c + (ch - RING + 1))
                    nc.scalar.copy(whi[:, s], raw[:, s]).then_inc(hi_done, 1)

            for g in range(KT // KC):
                act.wait_ge(xt_made, g + 1)
                nc.scalar.copy(xT[:, g * KC:(g + 1) * KC, 1:T + 1], ps[:, 4 + g % 4, :].rearrange("p (k t) -> p k t", k=KC)).then_inc(xt_copied, 1)
            act.wait_ge(rows_made, 2)
            nc.scalar.copy(mixT[:], ps[:, 0, 0:6 * KT]).then_inc(bank_free[0], 1)
            nc.scalar.copy(lnT[:], ps[:, 2, 0:P]).then_inc(bank_free[1], 1)
            split_hi(0, 0, RING)
            act.wait_ge(lora1_made, 1)
            A(hw[0:LR], ps[0:LR, 4, 0:T], ACT.Tanh).then_inc(lora1_copied, 1)
            act.wait_ge(lora1_made, 2)
            nc.scalar.copy(ha[0:LR], ps[0:LR, 5, 0:T]).then_inc(lora1_copied, 1)
            act.wait_ge(lora1_made, 3)
            for m in range(2):
                A(hg[:, m], ps[:, 6 + m, 0:T], ACT.Sigmoid).then_inc(lora1_copied, 1)
            for n in range(2 * NJ):
                act.wait_ge(lora2_made, n + 1)
                dst = (L_, A_)[n // NJ][:, :, (n % NJ) * NB:(n % NJ + 1) * NB]
                A(dst, ps[:, 4 + 2 * (n % 2):6 + 2 * (n % 2), :], ACT.Sigmoid).then_inc(lora2_copied, 1)

            def project(c0, n, dst, col=0):
                with act.Fori(0, n // 2) as i:
                    for b in range(2):
                        split_hi(i * (2 * CJ) + (c0 + b * CJ + RING), i * (2 * CJ // RING) + (c0 + b * CJ + RING) // RING, CJ)
                        act.wait_ge(chunk_used, i * (2 * CJ) + (c0 + (b + 1) * CJ))
                        nc.scalar.copy(dst[:, :, bass.ds(i * (2 * NB) + (col + b * NB), NB)], ps[:, 2 * b:2 * b + 2, :]).then_inc(bank_free[b], 1)

            def project_v(c0):
                for b in range(NJ):
                    c = c0 + b * CJ + RING
                    split_hi(c, c // RING, RING)
                    act.wait_ge(sq_asked, b + 1)
                    A(ntmp, KN_[:, :, b * NB:(b + 1) * NB], ACT.Square).then_inc(sq_done, 1)
                    split_hi(c + RING, c // RING + 1, RING)
                    act.wait_ge(chunk_used, c0 + (b + 1) * CJ)
                    nc.scalar.copy(V_[:, :, b * NB:(b + 1) * NB], ps[:, 2 * (b % 2):2 * (b % 2) + 2, :]).then_inc(bank_free[b % 2], 1)

            for n, dst in enumerate((K_, R_, V_)):
                for g in range(KT // KC):
                    act.wait_ge(mix_done, n * (KT // KC) + g + 1)
                    nc.scalar.copy(ahi[:, g * KC:(g + 1) * KC], mtmp[:, g % 2]).then_inc(mixhi_done, 1)
                if n < 2:
                    project(n * NJ * CJ, NJ, dst)
                else:
                    project_v(n * NJ * CJ)
            act.wait_ge(bank_free[0], 7)
            act.wait_ge(bank_free[1], 7)
            act.wait_ge(nk_done, NJ)

            def take_logs(i):
                for s, (ln, q) in enumerate(zip(lanes, lq)):
                    nc.scalar.copy(ln.Ls, L_[:, :, bass.ds(i * (2 * P) + s * P, P)]).then_inc(q["ls_set"], 1)

            def decays(i):
                for ln, q in zip(lanes, lq):
                    act.wait_ge(q["cum_made"], i + 1)
                    ci = ps[:, ln.bank + 1, 0:T].rearrange("p (t c) -> p t c", t=TT)
                    A(ln.Pi, ci, ACT.Exp)
                    A(ln.Pn, ci, ACT.Exp, scale=-1.0)
                    A(ln.Pe, ln.Ls, ACT.Exp, scale=DECAY)
                    A(ln.PCn, ps[:, ln.bank + 1, T:T + 4], ACT.Exp).then_inc(q["decay_done"], 1)

            def recur(i, more):
                one = i + 1
                both = [(lanes[s], lq[s], lanes[s].bank) for s in range(2)]
                for s, (ln, q, b) in enumerate(both):
                    nc.scalar.copy(ln.Vs, V_[:, :, bass.ds(i * (2 * P) + s * P, P)])
                for ln, q, b in both:
                    act.wait_ge(q["tr_made"], one)
                    for h in range(2):
                        hh = slice(h * HD, (h + 1) * HD)
                        last = nc.scalar.copy(ln.bkT[hh, :, h], ps[hh, b + 3, :].rearrange("p (a t b) -> p a t b", a=2, t=TT))
                    last.then_inc(q["bkT_set"], 1)
                for ln, q, b in both:
                    act.wait_ge(q["g_made"], one * 2)
                    for n, x in ((0, 1), (1, 0), (1, 1)):
                        last = nc.scalar.copy(ln.G[:, n, x], ps[:, b + 2 * n + x, :].rearrange("p (j c) -> p j c", j=4))
                    last.then_inc(q["g_raw"], 1)
                for l in range(1, LEVELS):
                    for ln, q, b in both:
                        act.wait_ge(q["x_made"], i * (LEVELS - 1) + l)
                        nc.scalar.copy(ln.X, ps[:, b + 1, :].rearrange("p (a b) -> p a b", a=4)).then_inc(q["x_set"], 1)
                    if l == 4:
                        for ln, q, b in both:
                            act.wait_ge(q["av_made"], one)
                            nc.scalar.copy(ln.AV, ps[:, b + 2, 0:T].rearrange("p (a b) -> p a b", a=4)).then_inc(q["av_set"], 1)
                if more:
                    take_logs(i + 1)
                for ln, q, b in both:
                    act.wait_ge(q["wt_made"], one)
                    nc.scalar.copy(ln.WT, ps[:, b + 1, 0:T].rearrange("p (t b) -> p t b", t=TT)).then_inc(q["wt_set"], 1)
                if more:
                    decays(i + 1)
                for s, (ln, q, b) in enumerate(both):
                    act.wait_ge(q["y_made"], one)
                    nc.scalar.copy(R_[:, :, bass.ds(i * (2 * P) + s * P, P)],
                                   ps[:, b + 3, 0:T].rearrange("p (t b) -> p t b", t=TT)).then_inc(q["y_set"], 1)

            act.wait_ge(zeros_set, 2)
            take_logs(0)
            decays(0)
            with act.Fori(0, PAIRS // 2 - 1) as i:
                recur(i, True)
            recur(PAIRS // 2 - 1, False)

            for g in range(KT // KC):
                act.wait_ge(z_tr, g + 1)
                nc.scalar.copy(ahi[:, g * KC:(g + 1) * KC], ps[:, 4 + g % 4, :].rearrange("p (k t) -> p k t", k=KC)).then_inc(mixhi_done, 1)

            def quiet_jobs(c0, n, kt, last=False):
                per = kt // KC
                rounds = n // 2 - (1 if last else 0)
                if rounds:
                    with act.Fori(0, rounds) as i:
                        split_hi(i * (2 * per) + (c0 + RING), i * (2 * per // RING) + (c0 + RING) // RING, 2 * per)
                if last:
                    c = c0 + rounds * 2 * per + RING
                    split_hi(c, c // RING, 2 * per - RING)

            def norm_affine(n):
                for g in range(KT // KC):
                    act.wait_ge(ln_tr, n * (KT // KC) + g + 1)
                    if g >= 2 or n:
                        act.wait_ge(ln_hi, n * (KT // KC) + g - 1)
                    for k2 in range(KC):
                        k = g * KC + k2
                        ins = A(ltmp[:, g % 2, k2], ps[:, 4 + g % 4, k2 * T:(k2 + 1) * T], ACT.Identity,
                                scale=lnT[:, (n * 2) * KT + k:(n * 2) * KT + k + 1],
                                bias=lnT[:, (n * 2 + 1) * KT + k:(n * 2 + 1) * KT + k + 1])
                    ins.then_inc(ln_aff, 1)

            def ffn(layer):
                c0, _ = PH[f"up{layer}"]
                u0 = layer * FB

                def hidden_hi(i, f0):
                    act.wait_ge(h_tr, i + 1)
                    A(hThi[:, f0, :], ps[:, 4:6, :].rearrange("p a (k t) -> p (a k) t", k=2), ACT.Copy).then_inc(hhi_done, 1)

                split_hi(c0 + RING, c0 // RING + 1, CJ)
                act.wait_ge(chunk_used, c0 + CJ)
                A(gtmp, ps[:, 0:2, :], ACT.Silu).then_inc(bank_free[0], 1)
                split_hi(c0 + RING + CJ, c0 // RING + 1 + CJ // RING, CJ)
                act.wait_ge(h_done, (1 if layer == 0 else 3) * TT)
                with act.Fori(0, FB - 1) as i:
                    c = i * (2 * CJ) + (c0 + 2 * CJ)
                    u = i * (2 * CJ // RING) + (c0 + 2 * CJ) // RING
                    split_hi(c + RING, u + 1, CJ)
                    act.wait_ge(h_tr, i + (u0 + 1))
                    act.wait_ge(chunk_used, c + CJ)
                    A(gtmp, ps[:, 0:2, :], ACT.Silu).then_inc(bank_free[0], 1)
                    hidden_hi(i + u0, bass.ds(i * 4, 4))
                    split_hi(c + (RING + CJ), u + (1 + CJ // RING), CJ)
                hidden_hi(u0 + FB - 1, slice((FB - 1) * 4, FB * 4))
                quiet_jobs(PH[f"down{layer}"][0], NJ, FT, last=(layer == 1))

            quiet_jobs(PH["wo"][0], NJ, KT)
            norm_affine(0)
            ffn(0)
            norm_affine(1)
            c = PH["kvq"][0]
            for b in range(2):
                split_hi(c + RING + b * CJ, (c + RING + b * CJ) // RING, CJ)
                if b == 0:
                    act.wait_ge(h_done, 2 * TT)
                act.wait_ge(chunk_used, c + (b + 1) * CJ)
                nc.scalar.copy(Kn[:, :, b * NB:(b + 1) * NB], ps[:, 2 * b:2 * b + 2, :]).then_inc(bank_free[b], 1)
            project(c + 2 * CJ, 2, Kn, 2 * NB)
            project(c + NJ * CJ, NJ, Vn)
            project(c + 2 * NJ * CJ, NJ, Qn)
            act.wait_ge(bank_free[0], PH["ao"][1] // 2 + 1)
            act.wait_ge(bank_free[1], PH["ao"][1] // 2 + 1)
            with act.Fori(0, HEADS // 4) as i:
                one = i + 1
                for s, q in enumerate(al):
                    act.wait_ge(q["nm_set"], one)
                    for h in range(2):
                        A(Sm[s][:, h, 0:P], Sm[s][:, h, 0:P], ACT.Exp, bias=asm[s][:, 0, 0, h:h + 1], scale=SCALE,
                          accum_out=asm[s][:, 1, 0, h:h + 1])
                        last = A(Sm[s][:, h, P:3 * P], Sm[s][:, h, P:3 * P], ACT.Exp, bias=asm[s][:, 0, 1, h:h + 1], scale=SCALE,
                                 accum_out=asm[s][:, 1, 1, h:h + 1])
                    last.then_inc(q["p_set"], 1)
                for s, q in enumerate(al):
                    act.wait_ge(q["pt_made"], one)
                    nc.scalar.copy(PT[s], ps[:, 4 * s:4 * s + 2, 0:3 * P]).then_inc(q["pt_set"], 1)
                for s, q in enumerate(al):
                    act.wait_ge(q["o_made"], one)
                    A(ahi[:, bass.ds(i * 4 + 2 * s, 2), :], ps[:, 4 * s + 2:4 * s + 4, 0:T], ACT.Copy).then_inc(q["ohi_set"], 1)
            quiet_jobs(PH["ao"][0], NJ, KT)
            norm_affine(2)
            ffn(1)

        @block.vector
        def _(dve):
            V = nc.vector
            step = Count(dve_step)

            def then(ins):
                step.up(ins)
                dve.wait_ge(dve_step, step.now())

            def rsqrt_seed(dst, src, t):
                I32 = mybir.dt.int32
                then(V.tensor_scalar(t.bitcast(I32), src.bitcast(I32), 1, None, ALU.logical_shift_right))
                then(V.tensor_scalar(dst.bitcast(I32), t.bitcast(I32), -1.0, float(0x5F3759DF), ALU.mult, ALU.add))

            def newton(dst, src, t):
                then(V.tensor_tensor(t, dst, dst, ALU.mult))
                then(V.scalar_tensor_tensor(out=t, in0=t, scalar=-0.5, in1=src, op0=ALU.mult, op1=ALU.mult))
                then(V.scalar_tensor_tensor(out=dst, in0=t, scalar=1.5, in1=dst, op0=ALU.add, op1=ALU.mult))

            def rsqrt(dst, src, t):
                rsqrt_seed(dst, src, t)
                for _ in range(3):
                    newton(dst, src, t)

            def split_lo(c, n, s0=0):
                for ch in range(n):
                    s = (s0 + ch) % RING
                    dve.wait_ge(hi_done, c + (ch + 1))
                    V.tensor_tensor(wlo[:, s], raw[:, s], whi[:, s].bitcast(F32), ALU.subtract).then_inc(split_done, 1)

            then(V.memset(xT[:, :, 0:1], 0.0))
            V.memset(hw[LR:LR + 1], 1.0).then_inc(ones_set, 1)
            V.memset(ha[LR:LR + 1], 1.0).then_inc(ones_set, 1)
            for g in range(KT // KC):
                dve.wait_ge(xt_copied, g + 1)
                k = slice(g * KC, (g + 1) * KC)
                V.tensor_tensor(xxT[:, k], xT[:, k, 0:T], xT[:, k, 1:T + 1], ALU.subtract).then_inc(xx_done, 1)
            dve.wait_ge(xx_done, KT // KC)
            dve.wait_ge(bank_free[0], 1)

            def mixed(out, m, k):
                return V.scalar_tensor_tensor(out=out, in0=xxT[:, k], scalar=mixT[:, m * KT + k:m * KT + k + 1], in1=xT[:, k, 1:T + 1],
                                              op0=ALU.mult, op1=ALU.add)

            for n, (m, buf) in enumerate(((1, L_), (4, A_), (5, L_))):
                mx = buf.rearrange("p t (k n) -> p (t k) n", n=T)
                if n == 2:
                    dve.wait_ge(lora1_made, 1)
                for k in range(KT):
                    mixed(mx[:, k], m, k).then_inc(lmix_done, 1)
            split_lo(0, RING)

            def mix_split(n, m):
                for g in range(KT // KC):
                    if g >= 2 or n:
                        dve.wait_ge(act_ready, n * (KT // KC) + g - 1)
                    if g == 0 and n:
                        dve.wait_ge(chunk_used, n * NJ * CJ)
                    for k2 in range(KC):
                        ins = mixed(mtmp[:, g % 2, k2], m, g * KC + k2)
                    ins.then_inc(mix_done, 1)
                    if g:
                        tail(n, g - 1)
                tail(n, KT // KC - 1)

            def tail(n, g):
                dve.wait_ge(mixhi_done, n * (KT // KC) + g + 1)
                V.tensor_tensor(alo[:, g * KC:(g + 1) * KC], mtmp[:, g % 2], ahi[:, g * KC:(g + 1) * KC].bitcast(F32),
                                ALU.subtract).then_inc(act_ready, 1)

            def quiet(c0, n, kt=KT, last=False):
                per = kt // KC
                with dve.Fori(0, n // 2) as i:
                    split_lo(i * (2 * per) + (c0 + RING), 2 * per)

            for n, m in enumerate((2, 0)):
                mix_split(n, m)
                quiet(n * NJ * CJ, NJ)
            mix_split(2, 3)

            def normalise(n, part):
                cs = slice(n * NB, (n + 1) * NB)
                hs = slice(n * 8, (n + 1) * 8)
                kn, b_, k_, r_ = (m[:, :, cs] for m in (KN_, A_, K_, R_))
                k_k, k_a, r_k = (bcast_row(npar[n % 2][:, j, :]) for j in range(3))
                nr = [nsmall[:, 16 * j:16 * (j + 1)] for j in range(3)]

                def by_head(m, v, op):
                    for t in range(TT):
                        last = V.tensor_tensor(m[:, t].rearrange("p (h i) -> p h i", i=HD), m[:, t].rearrange("p (h i) -> p h i", i=HD),
                                               v[:, 8 * t:8 * (t + 1)].unsqueeze(2).broadcast_to([P, 8, HD]), op)
                    return last

                if part == 0:
                    dve.wait_ge(npar_in[n % 2], 16 * (n // 2 + 1))
                    V.tensor_tensor(kn, k_, k_k, ALU.mult).then_inc(sq_asked, 1)
                elif part == 1:
                    dve.wait_ge(sq_done, n + 1)
                    for t in range(TT):
                        last = V.tensor_reduce(nr[0][:, 8 * t:8 * (t + 1)], ntmp[:, t].rearrange("p (h i) -> p h i", i=HD), AX.X, ALU.add)
                    then(last)
                    then(V.tensor_scalar(nr[0], nr[0], 1e-24, None, ALU.max))
                    rsqrt(nr[1], nr[0], nr[2])
                    then(V.scalar_tensor_tensor(out=ntmp, in0=b_, scalar=1.0, in1=k_a, op0=ALU.subtract, op1=ALU.mult))
                    then(V.scalar_tensor_tensor(out=k_, in0=ntmp, scalar=1.0, in1=k_, op0=ALU.add, op1=ALU.mult))
                elif part == 2:
                    then(by_head(kn, nr[1], ALU.mult))
                    V.tensor_tensor(b_, kn, b_, ALU.mult)
                    then(V.tensor_tensor(ntmp, k_, r_k, ALU.mult))
                else:
                    then(V.tensor_tensor(ntmp, ntmp, r_, ALU.mult))
                    for t in range(TT):
                        last = V.tensor_reduce(bsum[:, t, hs], ntmp[:, t].rearrange("p (h i) -> p h i", i=HD), AX.X, ALU.add)
                    last.then_inc(nk_done, 1)
                    dve.wait_ge(nk_done, n + 1)

            def bcast_row(v):
                return v.unsqueeze(1).broadcast_to([P, TT, v.shape[-1]])

            for b in range(2):
                dve.wait_ge(bank_free[b], 5)
            for n in range(NJ):
                for part in range(4):
                    split_lo(2 * NJ * CJ + n * CJ + RING + 2 * part, 2, 2 * part % RING)
                    normalise(n, part)

            dve.wait_ge(masks_in, 16)

            def recur(i):
                one = i + 1
                both = [(lanes[s], lq[s], lanes[s].bank) for s in range(2)]
                for s, (ln, q, b) in enumerate(both):
                    cs = bass.ds(i * (2 * P) + s * P, P)
                    dve.wait_ge(q["decay_done"], one)
                    V.tensor_copy(ln.PC, ln.PCn)
                    then(V.scalar_tensor_tensor(out=ln.at, in0=KN_[:, :, cs], scalar=-1.0, in1=ln.Pe, op0=ALU.mult, op1=ALU.mult))
                    V.tensor_tensor(ln.at, ln.at, ln.Pi, ALU.mult)
                    V.tensor_tensor(ln.bh, A_[:, :, cs], ln.Pn, ALU.mult)
                    V.tensor_tensor(ln.kh, K_[:, :, cs], ln.Pn, ALU.mult)
                    V.tensor_tensor(ln.rt, R_[:, :, cs], ln.Pi, ALU.mult).then_inc(q["rt_done"], 1)
                for ln, q, b in both:
                    dve.wait_ge(q["tr_made"], one)
                    V.tensor_copy(ln.arT, ps[:, b + 2, :].rearrange("p (t a b) -> p t a b", t=TT, a=2)).then_inc(q["arT_set"], 1)
                if not isinstance(i, int):
                    group_norm(i - 1, 0)

                def level_mask(l):
                    return mask_lv[:, l].unsqueeze(1).broadcast_to([P, 4, P])

                for ln, q, b in both:
                    dve.wait_ge(q["g_made"], i * 2 + 1)
                    A = ln.G[:, 0, 0]
                    then(V.tensor_tensor(A, ps[:, b, :].rearrange("p (j c) -> p j c", j=4), mask_ar[:, 0:P].unsqueeze(1).broadcast_to([P, 4, P]), ALU.mult))
                    then(V.tensor_tensor(A, A, ident[:].unsqueeze(1).broadcast_to([P, 4, P]), ALU.add))
                    V.tensor_tensor(ln.XT, A, level_mask(0), ALU.mult).then_inc(q["xt_set"], 1)
                if not isinstance(i, int):
                    group_norm(i - 1, 1)
                    group_norm(i - 1, 2)

                for l in range(1, LEVELS):
                    for ln, q, b in both:
                        dve.wait_ge(q["z_made"], i * (LEVELS - 1) + l)
                        V.tensor_tensor(ln.Z, ps[:, b, :].rearrange("p (a b) -> p a b", a=4), level_mask(l), ALU.mult).then_inc(q["z_set"], 1)
                    if l == 1 and not isinstance(i, int):
                        group_norm(i - 1, 3)
                    for ln, q, b in both:
                        dve.wait_ge(q["xt_made"], i * (LEVELS - 1) + l)
                        V.tensor_copy(ln.XT, ps[:, b + 3, :].rearrange("p (a b) -> p a b", a=4)).then_inc(q["xt_set"], 1)
                for ln, q, b in both:
                    dve.wait_ge(q["uh_made"], one)
                    V.tensor_copy(ln.U, ps[:, b + 2, T:2 * T].rearrange("p (t b) -> p t b", t=TT)).then_inc(q["u_set"], 1)
                for c in range(4):
                    t, rc = c // 2, slice((c % 2) * CHUNK, (c % 2 + 1) * CHUNK)
                    if c:
                        for ln, q, b in both:
                            dve.wait_ge(q["pu_made"], i * 3 + c)
                            V.tensor_tensor(ln.U[rc, t], ps[rc, b, 0:P], ln.U[rc, t], ALU.add).then_inc(q["u_set"], 1)
                    if c < 3:
                        for ln, q, b in both:
                            dve.wait_ge(q["ps_made"], i * 3 + (c + 1))
                            V.scalar_tensor_tensor(out=ln.S[:, c], in0=ps[:, b + 2, 0:P], scalar=ln.PC[:, c:c + 1], in1=mask_bd, op0=ALU.mult,
                                                   op1=ALU.mult).then_inc(q["s_set"], 1)

            def group_norm(i, part):
                cs = bass.ds(i * (2 * P), 2 * P)
                yv = R_[:, :, cs]

                def heads(v):
                    return v.rearrange("p t (h i) -> p t h i", i=HD)

                def per_head(v):
                    return v.rearrange("p (t h) -> p t h", t=TT).unsqueeze(3).broadcast_to([P, TT, 4, HD])

                if part == 0:
                    for q in lq:
                        dve.wait_ge(q["y_set"], i + 1)
                    then(V.tensor_reduce(gsm[:, 0].rearrange("p (t h) -> p t h", t=TT), heads(yv), AX.X, ALU.add))
                    then(V.tensor_scalar(gsm[:, 1], gsm[:, 0], 1.0 / HD, None, ALU.mult))
                    then(V.tensor_tensor(heads(yv), heads(yv), per_head(gsm[:, 1]), ALU.subtract))
                    then(V.tensor_tensor(y_sq, yv, yv, ALU.mult))
                    then(V.tensor_reduce(gsm[:, 0].rearrange("p (t h) -> p t h", t=TT), heads(y_sq), AX.X, ALU.add))
                    then(V.tensor_scalar(gsm[:, 2], gsm[:, 0], 1.0 / HD, GN_EPS, ALU.mult, ALU.add))
                elif part == 1:
                    rsqrt_seed(gsm[:, 3], gsm[:, 2], gsm[:, 4])
                    newton(gsm[:, 3], gsm[:, 2], gsm[:, 4])
                elif part == 2:
                    newton(gsm[:, 3], gsm[:, 2], gsm[:, 4])
                    newton(gsm[:, 3], gsm[:, 2], gsm[:, 4])
                else:
                    V.tensor_tensor(heads(yv), heads(yv), per_head(gsm[:, 3]), ALU.mult).then_inc(y_normed, 1)

            dve.wait_ge(bank_free[0], 7)
            dve.wait_ge(bank_free[1], 7)
            recur(0)
            with dve.Fori(0, PAIRS // 2 - 1) as i:
                step.enter(i, 2 + 2 * 2 + 6 + 11)
                recur(i + 1)
                step.leave(PAIRS // 2 - 1)
            for part in range(4):
                group_norm(PAIRS // 2 - 1, part)

            dve.wait_ge(zz_done, PAIRS // 2)
            for n in range(NJ):
                dve.wait_ge(gate_made, n + 1)
                c = slice(n * NB, (n + 1) * NB)
                V.tensor_tensor(R_[:, :, c], R_[:, :, c], ps[:, 2 * n:2 * n + 2, :], ALU.mult).then_inc(gated, 1)
            for g in range(KT // KC):
                dve.wait_ge(mixhi_done, 3 * (KT // KC) + g + 1)
                V.tensor_tensor(alo[:, g * KC:(g + 1) * KC], ps[:, 4 + g % 4, :].rearrange("p (k t) -> p k t", k=KC),
                                ahi[:, g * KC:(g + 1) * KC].bitcast(F32), ALU.subtract).then_inc(z_tr_done, 1)

            def residual(c0, kt, n, last=False):
                per = kt // KC
                for b in range(NJ):
                    left = per if not (last and b == NJ - 1) else per - RING
                    first = c0 + b * per + RING
                    for ch in range(left):
                        s = (first + ch) % RING
                        dve.wait_ge(hi_done, first + ch + 1)
                        V.tensor_tensor(wlo[:, s], raw[:, s], whi[:, s].bitcast(F32), ALU.subtract).then_inc(split_done, 1)
                    dve.wait_ge(chunk_used, c0 + (b + 1) * per)
                    if b == 0 and n == 0:
                        dve.wait_ge(h0_in, 16)
                    cs = slice(b * NB, (b + 1) * NB)
                    V.scalar_tensor_tensor(out=Zn[:, :, cs], in0=H[:, :, cs], scalar=ALPHA, in1=ps[:, 2 * (b % 2):2 * (b % 2) + 2, :],
                                           op0=ALU.mult, op1=ALU.add).then_inc(bank_free[b % 2], 1)
                    dve.wait_ge(bank_free[b % 2], (c_jobs[n] + b) // 2 + 2)
                    for t in range(TT):
                        ins = V.bn_stats(stats[:, t, b, :], Zn[:, t, cs])
                then(ins)
                for t in range(TT):
                    then(V.bn_aggr(mv[:, t, :], stats[:, t]))
                then(V.tensor_scalar(var[:], mv[:, :, 1], LN_EPS, None, ALU.add))
                rsqrt(rstd[:], var[:], small[:, 8:8 + TT])
                for b in range(NJ):
                    cs = slice(b * NB, (b + 1) * NB)
                    for t in range(TT):
                        ins = V.tensor_scalar(Zn[:, t, cs], Zn[:, t, cs], mv[:, t, 0:1], rstd[:, t:t + 1], ALU.subtract, ALU.mult)
                    ins.then_inc(xhat_done, 1)

            c_jobs = [PH["wo"][1], PH["down0"][1], PH["ao"][1], PH["down1"][1]]

            def norm_split(n):
                for g in range(KT // KC):
                    dve.wait_ge(ln_aff, n * (KT // KC) + g + 1)
                    k = slice(g * KC, (g + 1) * KC)
                    then(V.tensor_copy(ahi[:, k], ltmp[:, g % 2]))
                    V.tensor_tensor(alo[:, k], ltmp[:, g % 2], ahi[:, k].bitcast(F32), ALU.subtract).then_inc(ln_hi, 1)

            def natural(n, t):
                dve.wait_ge(wb_in, (n + 1) * 16)
                dve.wait_ge(xhat_done, (n + 1) * NJ)
                then(V.tensor_tensor(H[:, t], Zn[:, t], wb[:, 0], ALU.mult))
                V.tensor_tensor(H[:, t], H[:, t], wb[:, 1], ALU.add).then_inc(h_done, 1)

            def natural_and_split(n, c0):
                for t in range(TT):
                    split_lo(c0 + RING + 2 * t, 2, 2 * t % RING)
                    natural(n, t)
                split_lo(c0 + RING + 2 * TT, CJ - 2 * TT, 2 * TT % RING)

            def ffn(layer):
                c0, j0 = PH[f"up{layer}"]
                u0 = layer * FB

                def multiply(c_end, up_seen):
                    dve.wait_ge(bank_free[0], up_seen)
                    dve.wait_ge(chunk_used, c_end)
                    V.tensor_tensor(gtmp, gtmp, ps[:, 2:4, :], ALU.mult).then_inc(bank_free[1], 1)

                def hidden_lo(i, f0):
                    dve.wait_ge(hhi_done, i + 1)
                    V.tensor_tensor(hTlo[:, f0, :], ps[:, 4:6, :].rearrange("p a (k t) -> p (a k) t", k=2),
                                    hThi[:, f0, :].bitcast(F32), ALU.subtract).then_inc(hlo_done, 1)

                natural_and_split(2 * layer, c0)
                split_lo(c0 + RING + CJ, CJ)
                with dve.Fori(0, FB - 1) as i:
                    c = i * (2 * CJ) + (c0 + 2 * CJ)
                    multiply(c, i + (j0 // 2 + 2))
                    split_lo(c + RING, CJ)
                    hidden_lo(i + u0, bass.ds(i * 4, 4))
                    split_lo(c + (RING + CJ), CJ)
                multiply(c0 + FB * 2 * CJ, j0 // 2 + FB + 1)
                hidden_lo(u0 + FB - 1, slice((FB - 1) * 4, FB * 4))

            residual(PH["wo"][0], KT, 0)
            norm_split(0)
            ffn(0)
            residual(PH["down0"][0], FT, 1)
            norm_split(1)
            natural_and_split(1, PH["kvq"][0])
            split_lo(PH["kvq"][0] + RING + CJ, CJ)
            quiet(PH["kvq"][0] + 2 * CJ, 10)
            dve.wait_ge(bank_free[0], PH["ao"][1] // 2 + 1)
            dve.wait_ge(bank_free[1], PH["ao"][1] // 2 + 1)
            dve.wait_ge(cap_in, 16)
            with dve.Fori(0, HEADS // 4) as i:
                step.enter(i, 2 * 3)
                one = i + 1
                for s, q in enumerate(al):
                    dve.wait_ge(q["qk_tr"], one)
                    V.tensor_copy(QKT[s], ps[:, 4 * s:4 * s + 2, :]).then_inc(q["qkt_set"], 1)
                for s, q in enumerate(al):
                    sm, mx = Sm[s], asm[s][:, 0]
                    dve.wait_ge(q["s_made"], one)
                    then(V.tensor_tensor(sm, ps[:, 4 * s + 2:4 * s + 4, 0:3 * P], cap.unsqueeze(1).broadcast_to([P, 2, 3 * P]), ALU.min))
                    V.tensor_reduce(mx[:, 0], sm[:, :, 0:P], AX.X, ALU.max)
                    then(V.tensor_reduce(mx[:, 1], sm[:, :, P:3 * P], AX.X, ALU.max))
                    V.tensor_scalar(mx, mx, NEG / SCALE, -SCALE, ALU.max, ALU.mult).then_inc(q["nm_set"], 1)
                for s, q in enumerate(al):
                    sm, rs = Sm[s], asm[s][:, 2]
                    dve.wait_ge(q["p_set"], one)
                    then(V.reciprocal(rs, asm[s][:, 1]))
                    V.tensor_tensor(sm[:, :, 0:P], sm[:, :, 0:P], rs[:, 0].unsqueeze(2).broadcast_to([P, 2, P]), ALU.mult)
                    V.tensor_tensor(sm[:, :, P:3 * P], sm[:, :, P:3 * P], rs[:, 1].unsqueeze(2).broadcast_to([P, 2, 2 * P]),
                                    ALU.mult).then_inc(q["p_normed"], 1)
                for s, q in enumerate(al):
                    dve.wait_ge(q["ohi_set"], one)
                    hs = bass.ds(i * 4 + 2 * s, 2)
                    V.tensor_tensor(alo[:, hs, :], ps[:, 4 * s + 2:4 * s + 4, 0:T], ahi[:, hs, :].bitcast(F32), ALU.subtract).then_inc(q["olo_set"], 1)
                step.leave(HEADS // 4)
            residual(PH["ao"][0], KT, 2)
            norm_split(2)
            ffn(1)
            residual(PH["down1"][0], FT, 3, last=True)
            dve.wait_ge(wb_in, 4 * 16)
            for b in range(NJ):
                cs = slice(b * NB, (b + 1) * NB)
                dve.wait_ge(xhat_done, 3 * NJ + b + 1)
                then(V.tensor_tensor(H[:, :, cs], Zn[:, :, cs], bcast_row(wb[:, 0, cs]), ALU.mult))
                V.tensor_tensor(H[:, :, cs], H[:, :, cs], bcast_row(wb[:, 1, cs]), ALU.add).then_inc(h_done, 1)


_OUT = ((1, T, D), "float32")


def kernel(**inputs):
    import concourse.bacc as bacc
    from concourse.bass_utils import run_bass_kernel_spmd as run

    nc = bacc.Bacc("TRN2", target_bir_lowering=False, num_devices=1)
    arrays = {}

    def give(name, a):
        a = np.ascontiguousarray(a)
        arrays[name] = a
        return nc.dram_tensor(name, a.shape, mybir.dt.from_np(a.dtype), kind="ExternalInput").ap()

    i = {k: np.asarray(v) for k, v in inputs.items()}
    x = give("x", i["x"])
    rows = give("mix_rows", i["a_mix"][0].reshape(6 * KT, P))
    rwkv_rows = give("rwkv_rows", np.stack([i["a_k_k"][0], i["a_k_a"][0], i["a_r_k"][0].reshape(D), i["a_lnx_w"][0], i["a_lnx_b"][0]]))
    lora = {m: give("lora_" + m, i["a_" + m][0]) for m in ("w1", "w2", "a1", "a2", "g1", "g2")}
    lora.update({m: give("lora_" + m, i["a_" + m]) for m in ("w0", "a0")})
    w = {"r": give("w_r", i["a_w_r"][0]), "k": give("w_k", i["a_w_k"][0]), "v": give("w_v", i["a_w_v"][0]), "o": give("w_o", i["a_w_o"][0]),
         "kv_k": give("kv_k", i["kv_w_k"]), "kv_v": give("kv_v", i["kv_w_v"]), "q": give("w_q", i["b_w_q"][0]), "ao": give("w_ao", i["b_w_o"][0]),
         "gate": give("w_gate", i["ffn_w_gate"]), "up": give("w_up", i["ffn_w_up"]), "down": give("w_down", i["ffn_w_down"])}
    ln = give("ln_rows", np.stack([np.stack([np.stack([i[f"ln{n}_w"][l], i[f"ln{n}_b"][l]]) for n in (1, 2)]) for l in range(DEPTH)]))
    c = give("consts", constants())
    y = nc.dram_tensor("y", _OUT[0], F32, kind="ExternalOutput").ap()
    trunk(nc, x, rows, rwkv_rows, lora, w, c, ln, y)
    return run(nc, [arrays], core_ids=[0]).results[0]["y"]
```
